# Optimizing a Trainium2 kernel written in Bass

```python
import math, functools
import jax, jax.numpy as jnp
from jax import lax
import numpy as np

D_MODEL = 1024
BATCH = 1
SEQ = 1024
DEPTH = 1
DEC_BATCH = 1
DEC_SEQ = 64
PAST_LEN = 2048

CHUNK = 64
QBLOCK = 128
N_HEADS = 8
HEAD_DIM = 64
ATTN_W = N_HEADS * HEAD_DIM
CONV_CH = 512
CONV_W = 31
D_FF = 2816
FFN_CONV_W = 3
N_IN = 3 * ATTN_W + 2 * CONV_CH + 2 * D_MODEL
SPLITS = (ATTN_W, 2 * ATTN_W, 3 * ATTN_W, 3 * ATTN_W + CONV_CH,
          3 * ATTN_W + 2 * CONV_CH, 3 * ATTN_W + 2 * CONV_CH + D_MODEL)
EPS = 1e-6

kernel_name = "hybrid_stickbreak_conformer_convffn_stream_step"

def rmsnorm(x, g):
    xf = x.astype(jnp.float32)
    y = xf * lax.rsqrt(jnp.mean(xf * xf, axis=-1, keepdims=True) + EPS)
    return (y * g.astype(jnp.float32)).astype(x.dtype)

def layernorm(x, g, b):
    xf = x.astype(jnp.float32)
    mu = jnp.mean(xf, axis=-1, keepdims=True)
    xc = xf - mu
    y = xc * lax.rsqrt(jnp.mean(xc * xc, axis=-1, keepdims=True) + EPS)
    return (y * g.astype(jnp.float32) + b.astype(jnp.float32)).astype(x.dtype)

def causal_dwconv(x, buf, w, b):
    width, ch = w.shape
    xp = jnp.concatenate([buf.astype(x.dtype), x], axis=1)
    y = lax.conv_general_dilated(xp, w[:, None, :].astype(x.dtype), window_strides=(1,),
                                 padding='VALID', dimension_numbers=('NWC', 'WIO', 'NWC'),
                                 feature_group_count=ch)
    return y + b, xp[:, -(width - 1):]

def sb_attend(q, k, v, q_pos, k_pos):
    z = jnp.einsum('bqhd,bkhd->bhqk', q.astype(jnp.float32), k.astype(jnp.float32)) * (HEAD_DIM ** -0.5)
    mask = k_pos[None, :] < q_pos[:, None]
    log_one_minus = jnp.where(mask, jax.nn.log_sigmoid(-z), 0.0)
    between = lax.cumsum(log_one_minus, axis=3, reverse=True) - log_one_minus
    weights = jnp.where(mask, jnp.exp(jax.nn.log_sigmoid(z) + between), 0.0)
    return jnp.einsum('bhqk,bkhd->bqhd', weights, v.astype(jnp.float32))

def sb_prompt(q, k, v):
    b, s, h, d = q.shape
    nb = s // QBLOCK
    qb = q.reshape(b, nb, QBLOCK, h, d).transpose(1, 0, 2, 3, 4)
    qpos = jnp.arange(s).reshape(nb, QBLOCK)
    kpos = jnp.arange(s)
    out = lax.map(lambda a: sb_attend(a[0], k, v, a[1], kpos), (qb, qpos))
    return out.transpose(1, 0, 2, 3, 4).reshape(b, s, h, d)

def sb_sample(q, k, v, k_past, v_past):
    p = k_past.shape[1]
    t = q.shape[1]
    k_all = jnp.concatenate([k_past.astype(k.dtype), k], axis=1)
    v_all = jnp.concatenate([v_past.astype(v.dtype), v], axis=1)
    return sb_attend(q, k_all, v_all, p + jnp.arange(t), jnp.arange(p + t))

def layer(x, conv_buf, ffn_buf, attend, norm1_g, w_in, b_in, q_norm_g, k_norm_g, w_attn_out,
          dw_w, dw_b, cn_g, cn_b, w_conv_out, b_conv_out, w_out, norm2_g, w_up,
          ffn_dw_w, ffn_dw_b, w_down):
    b, t, _ = x.shape
    h = rmsnorm(x, norm1_g)
    proj = h @ w_in + b_in
    q, k, v, glu_a, glu_b, g_attn, g_conv = jnp.split(proj, SPLITS, axis=-1)
    q = rmsnorm(q.reshape(b, t, N_HEADS, HEAD_DIM), q_norm_g)
    k = rmsnorm(k.reshape(b, t, N_HEADS, HEAD_DIM), k_norm_g)
    v = v.reshape(b, t, N_HEADS, HEAD_DIM)
    a = attend(q, k, v).astype(x.dtype).reshape(b, t, ATTN_W) @ w_attn_out
    u = glu_a * jax.nn.sigmoid(glu_b)
    c, new_conv = causal_dwconv(u, conv_buf, dw_w, dw_b)
    c = jax.nn.silu(layernorm(c, cn_g, cn_b)) @ w_conv_out + b_conv_out
    x = x + (jax.nn.sigmoid(g_attn) * a + jax.nn.sigmoid(g_conv) * c) @ w_out
    up, new_ffn = causal_dwconv(rmsnorm(x, norm2_g) @ w_up, ffn_buf, ffn_dw_w, ffn_dw_b)
    gate, val = jnp.split(up, 2, axis=-1)
    x = x + (jax.nn.silu(gate) * val) @ w_down
    return x, k, v, new_conv, new_ffn

def setup_inputs(seed: int = 0) -> dict:
    key = jax.random.key(seed)
    ks = jax.random.split(key, 32)
    f32 = jnp.float32
    nrm = lambda k, shape, s: jax.random.normal(k, shape, f32) * s
    gain = lambda k, shape: 1.0 + 0.02 * jax.random.normal(k, shape, f32)
    return {
        "x_prompt": nrm(ks[0], (BATCH, SEQ, D_MODEL), 1.0),
        "x_sample": nrm(ks[1], (DEC_BATCH, DEC_SEQ, D_MODEL), 1.0),
        "cache_sb_k": nrm(ks[2], (DEPTH, DEC_BATCH, PAST_LEN, N_HEADS, HEAD_DIM), 1.0),
        "cache_sb_v": nrm(ks[3], (DEPTH, DEC_BATCH, PAST_LEN, N_HEADS, HEAD_DIM), 1.0),
        "state_conv": nrm(ks[4], (DEPTH, DEC_BATCH, CONV_W - 1, CONV_CH), 0.5),
        "state_ffn_conv": nrm(ks[5], (DEPTH, DEC_BATCH, FFN_CONV_W - 1, 2 * D_FF), 1.0),
        "norm1_g": gain(ks[6], (DEPTH, D_MODEL)),
        "w_in": nrm(ks[7], (DEPTH, D_MODEL, N_IN), D_MODEL ** -0.5),
        "b_in": nrm(ks[8], (DEPTH, N_IN), 0.02),
        "q_norm_g": gain(ks[9], (DEPTH, HEAD_DIM)),
        "k_norm_g": gain(ks[10], (DEPTH, HEAD_DIM)),
        "w_attn_out": nrm(ks[11], (DEPTH, ATTN_W, D_MODEL), ATTN_W ** -0.5),
        "dw_w": nrm(ks[12], (DEPTH, CONV_W, CONV_CH), CONV_W ** -0.5),
        "dw_b": nrm(ks[13], (DEPTH, CONV_CH), 0.02),
        "cn_g": gain(ks[14], (DEPTH, CONV_CH)),
        "cn_b": nrm(ks[15], (DEPTH, CONV_CH), 0.02),
        "w_conv_out": nrm(ks[16], (DEPTH, CONV_CH, D_MODEL), CONV_CH ** -0.5),
        "b_conv_out": nrm(ks[17], (DEPTH, D_MODEL), 0.02),
        "w_out": nrm(ks[18], (DEPTH, D_MODEL, D_MODEL), D_MODEL ** -0.5),
        "norm2_g": gain(ks[19], (DEPTH, D_MODEL)),
        "w_up": nrm(ks[20], (DEPTH, D_MODEL, 2 * D_FF), D_MODEL ** -0.5),
        "ffn_dw_w": nrm(ks[21], (DEPTH, FFN_CONV_W, 2 * D_FF), FFN_CONV_W ** -0.5),
        "ffn_dw_b": nrm(ks[22], (DEPTH, 2 * D_FF), 0.02),
        "w_down": nrm(ks[23], (DEPTH, D_FF, D_MODEL), D_FF ** -0.5),
        "final_g": gain(ks[24], (D_MODEL,)),
    }

def reference(x_prompt, x_sample, cache_sb_k, cache_sb_v, state_conv, state_ffn_conv,
              norm1_g, w_in, b_in, q_norm_g, k_norm_g, w_attn_out, dw_w, dw_b, cn_g, cn_b,
              w_conv_out, b_conv_out, w_out, norm2_g, w_up, ffn_dw_w, ffn_dw_b, w_down, final_g):
    bp = x_prompt.shape[0]
    conv_zero = jnp.zeros((bp, CONV_W - 1, CONV_CH), x_prompt.dtype)
    ffn_zero = jnp.zeros((bp, FFN_CONV_W - 1, 2 * D_FF), x_prompt.dtype)
    xp, xs = x_prompt, x_sample
    kp, vp, ks_, vs_, cp, cs, fp, fs = [], [], [], [], [], [], [], []
    for l in range(DEPTH):
        w = (norm1_g[l], w_in[l], b_in[l], q_norm_g[l], k_norm_g[l], w_attn_out[l],
             dw_w[l], dw_b[l], cn_g[l], cn_b[l], w_conv_out[l], b_conv_out[l], w_out[l],
             norm2_g[l], w_up[l], ffn_dw_w[l], ffn_dw_b[l], w_down[l])
        xp, k1, v1, c1, f1 = layer(xp, conv_zero, ffn_zero, sb_prompt, *w)
        attend_s = functools.partial(sb_sample, k_past=cache_sb_k[l], v_past=cache_sb_v[l])
        xs, k2, v2, c2, f2 = layer(xs, state_conv[l], state_ffn_conv[l], attend_s, *w)
        kp.append(k1); vp.append(v1); cp.append(c1); fp.append(f1)
        ks_.append(k2); vs_.append(v2); cs.append(c2); fs.append(f2)
    y_prompt = rmsnorm(xp, final_g)
    y_sample = rmsnorm(xs, final_g)
    return (y_prompt, y_sample, jnp.stack(kp), jnp.stack(vp), jnp.stack(ks_), jnp.stack(vs_),
            jnp.stack(cp), jnp.stack(cs), jnp.stack(fp), jnp.stack(fs))


_drawn_inputs = setup_inputs


def setup_inputs(seed=0):
    import zlib

    import numpy as np

    out = dict(_drawn_inputs(seed))
    spreads = {}
    factors = {'q_norm_g': 53.983,
     'dw_b': 4.344,
     'cn_g': 7.491,
     'cn_b': 8.0,
     'b_conv_out': 5.238,
     'norm2_g': 2.804,
     'ffn_dw_b': 4.219,
     'final_g': 8.13}
    for name, (base, spread) in spreads.items():
        noise = np.random.default_rng([zlib.crc32(name.encode()), seed]).standard_normal(out[name].shape)
        drawn = base * np.exp(spread * noise) if base else spread * noise
        out[name] = __import__('jax').numpy.asarray(drawn.astype(out[name].dtype))
    for name, factor in factors.items():
        out[name] = (out[name] * factor).astype(out[name].dtype)
    return out
```

```python
from contextlib import ExitStack

import concourse.bass as bass
from concourse import mybir
from concourse.bass import ds

F32 = mybir.dt.float32
F32R = mybir.dt.float32r
BF16 = mybir.dt.bfloat16
ALU = mybir.AluOpType
ACT = mybir.ActivationFunctionType
AX_X = mybir.AxisListType.X

P = 128
D = 1024
SEQ, DEC, PAST = 1024, 64, 2048
T = SEQ + DEC
H, DH = 8, 64
AW = H * DH
CC, CW = 512, 31
FF, FW = 2816, 3
KT = D // P
NT = (T + P - 1) // P
PAIRS = H // 2
TOK = [P * t for t in range(NT - 1)] + [T - P]
CHUNKS = [(0, 364), (364, 728), (728, T)]
EPS = 1e-6
QB = 64
NB = T // QB
UCOLS = CW - 1 + T + CW - 1
U_SAMPLE = CW - 1 + SEQ
COUT = SEQ + CW - 1 + DEC
NSLOT = 5


def attention_units():
    units = []
    for i in range(NB - 1):
        keys = P * (i // 2 + 1)
        cuts = list(range(0, keys, 512)) + [keys]
        spans = list(zip(cuts[:-1], cuts[1:]))[::-1]
        for n, (a, b) in enumerate(spans):
            units.append((i, a, b - a, n == 0, n == len(spans) - 1, None, i % 2 if n == 0 else None))
    units.append((NB - 1, T - P, P, True, False, None, 2))
    for c in range(PAST // 512)[::-1]:
        units.append((NB - 1, 512 * c, 512, False, c == 0, c, None))
    return units


UNITS = attention_units()
NU = len(UNITS)
NS = NU + 4
PASTS = [u for u, x in enumerate(UNITS) if x[5] is not None]
ACT_EVACS = ["k0", "k1", "k2"]
WT_JOBS = ["k0", "k1", "k2", "q0", "q1", "q2"]
for _s in range(NS):
    if _s + 1 in PASTS:
        ACT_EVACS.append(f"past{PASTS.index(_s + 1)}")
        WT_JOBS.append(f"past{PASTS.index(_s + 1)}")
    if 0 <= _s - 2 < NU:
        ACT_EVACS.append(f"w{_s - 2}")
        WT_JOBS.append(f"w{_s - 2}")
NEV, NWT = len(ACT_EVACS), len(WT_JOBS)


def build(nc, a, o, scr):
    ctx = ExitStack()
    with ctx:
        def sb(name, shape, dt=F32, c=ctx):
            return c.enter_context(nc.sbuf_tensor(name, shape, dt))

        def sem(name):
            return ctx.enter_context(nc.semaphore(name))

        bank = [ctx.enter_context(nc.psum_tensor(f"bank{i}", [P, 512], F32)) for i in range(8)]
        ident = sb("ident", [P, P])
        identb = sb("identb", [P, P], BF16)
        maskb = sb("maskb", [P, 3, P], BF16)
        prm = sb("prm", [P, 88])
        dww = sb("dww", [P, 4, CW])
        ffw = sb("ffw", [P, FW, 44])
        epst = sb("epst", [P, 1])
        conv_state = sb("conv_state", [P, 4, CW - 1])
        ffn_state = sb("ffn_state", [P, 2, 44])
        PRM_BIN, PRM_DWB, PRM_CNG, PRM_CNB, PRM_BCO, PRM_FDB = 0, 24, 28, 32, 36, 44
        wraw = sb("wraw", [P, 2, KT * P])
        whi = sb("whi", [P, NSLOT, KT * P], F32R)
        wlo = sb("wlo", [P, NSLOT, KT * P], F32R)
        hctx = ctx.enter_context(ExitStack())
        hhi = sb("hhi", [P, KT, T], F32R, hctx)
        hlo = sb("hlo", [P, KT, T], F32R, hctx)
        w_in = a["w_in"][0].rearrange("(k p) n -> p k n", p=P)

        def gate_col(g):
            return 3 * AW + 2 * CC + D * (g % 2) + P * (g // 2)

        def later(n, least=1):
            return not isinstance(n, int) or n >= least

        def split_passes(x_hi, x_lo, y_hi, y_lo):
            return ((x_hi, y_hi), (x_hi, y_lo), (x_lo, y_hi))

        with ExitStack() as c1:
            xt = sb("xt", [P, 3, D], c=c1)
            sq = sb("sq", [P, 2, D], c=c1)
            g1 = sb("g1", [P, D], c=c1)
            ss = sb("ss1", [P, NT], c=c1)
            sd = sb("sd1", [P, NT], c=c1)
            rs = sb("rs1", [P, NT], c=c1)
            prm_rows = sb("prm_rows", [88, P], c=c1)
            dww_rows = sb("dww_rows", [CW, CC], c=c1)
            ffw_rows = sb("ffw_rows", [44, FW, P], c=c1)
            fst_rows = sb("fst_rows", [44, 2, P], c=c1)
            cst_rows = sb("cst_rows", [CW - 1, CC], c=c1)
            x_in = [sem(f"x_in{i}") for i in range(3)]
            par_in, g_in = sem("par_in"), sem("g_in")
            const_done, maskf_done = sem("const_done"), sem("maskf_done")
            maskf = sb("maskf", [P, 3, P], c=c1)
            sq_done, sd_done, rs_done1 = sem("sq_done"), sem("sd_done"), sem("rs_done1")
            xn_done, xt_ready = sem("xn_done"), sem("xt_ready")
            h_hi_done, h_lo_done = sem("h_hi_done"), sem("h_lo_done")
            par_ready, par_done = sem("par_ready"), sem("par_done")

            block = c1.enter_context(nc.Block())

            @block.sync
            def _(sp):
                def load_x(t):
                    if t >= 3:
                        sp.wait_ge(xt_ready, t - 2)
                    if t < NT - 1:
                        sp.dma_start(xt[:, t % 3, :], a["x_prompt"][0, P * t:P * t + P, :]).then_inc(x_in[t % 3], 16)
                    else:
                        sp.dma_start(xt[0:64, t % 3, :], a["x_prompt"][0, SEQ - 64:SEQ, :]).then_inc(x_in[t % 3], 16)
                        sp.dma_start(xt[64:P, t % 3, :], a["x_sample"][0]).then_inc(x_in[t % 3], 16)

                load_x(0)
                sp.dma_start(g1[:, :], a["norm1_g"][0:1, :].to_broadcast([P, D])).then_inc(g_in, 16)
                load_x(1)
                load_x(2)
                rows = lambda ap, n: ap.rearrange("(r c) -> r c", r=n)
                sp.dma_start(prm_rows[0:24, :], rows(a["b_in"][0, 3 * AW:], 24)).then_inc(par_in, 16)
                sp.dma_start(prm_rows[24:28, :], rows(a["dw_b"][0], 4)).then_inc(par_in, 16)
                sp.dma_start(prm_rows[28:32, :], rows(a["cn_g"][0], 4)).then_inc(par_in, 16)
                sp.dma_start(prm_rows[32:36, :], rows(a["cn_b"][0], 4)).then_inc(par_in, 16)
                sp.dma_start(prm_rows[36:44, :], rows(a["b_conv_out"][0], 8)).then_inc(par_in, 16)
                sp.dma_start(prm_rows[44:88, :], rows(a["ffn_dw_b"][0], 44)).then_inc(par_in, 16)
                sp.dma_start(dww_rows[:, :], a["dw_w"][0]).then_inc(par_in, 16)
                sp.dma_start(ffw_rows[:, :, :], a["ffn_dw_w"][0].rearrange("w (r c) -> r w c", c=P)).then_inc(par_in, 16)
                sp.dma_start(fst_rows[:, :, :], a["state_ffn_conv"][0, 0].rearrange("w (r c) -> r w c", c=P)).then_inc(par_in, 16)
                sp.dma_start(cst_rows[:, :], a["state_conv"][0, 0]).then_inc(par_in, 16)
                for t in range(3, NT):
                    load_x(t)

            @block.gpsimd
            def _(pool):
                pool.memset(ident[:, :], 0.0).then_inc(maskf_done, 1)
                pool.memset(maskf[:, :, :], 0.0).then_inc(maskf_done, 1)
                pool.memset(epst[:, :], EPS).then_inc(maskf_done, 1)
                pool.wait_ge(maskf_done, 3)
                pool.affine_select(out=ident[:, :], in_=ident[:, :], compare_op=ALU.not_equal, fill=1.0, base=0,
                                   pattern=[[-1, P]], channel_multiplier=1).then_inc(maskf_done, 1)
                for half in range(2):
                    rows = slice(64 * half, 64 * half + 64)
                    for m, first in enumerate((0, 64, 64)):
                        pool.wait_ge(maskf_done, 4 + 3 * half + m)
                        pool.affine_select(out=maskf[rows, m, :], in_=maskf[rows, m, :], compare_op=ALU.is_gt,
                                           fill=-1e30, base=first, pattern=[[-1, P]],
                                           channel_multiplier=1).then_inc(maskf_done, 1)
                pool.wait_ge(maskf_done, 10)
                pool.memset(maskf[:, 2, 0:64], -1e30).then_inc(maskf_done, 1)

            def hi_parts(act, t):
                for j in range(2):
                    act.wait_ge(xt_ready, t + 1)
                    new = 64 if t == NT - 1 else 0
                    act.activation(hhi[:, 4 * j:4 * j + 4, TOK[t] + new:TOK[t] + P],
                                   bank[2 * (t % 2) + j][:, :].rearrange("p (k t) -> p k t", k=4)[:, :, new:],
                                   ACT.Copy).then_inc(h_hi_done, 1)

            @block.scalar
            def _(act):
                for t in range(NT):
                    act.wait_ge(x_in[t % 3], 16 * (t // 3 + 1 + (t == NT - 1)))
                    if t >= 2:
                        act.wait_ge(sq_done, t - 1)
                    act.activation(sq[:, t % 2, :], xt[:, t % 3, :], ACT.Square,
                                   accum_out=ss[:, t:t + 1]).then_inc(sq_done, 1)
                    act.wait_ge(sq_done, t + 1)
                    act.wait_ge(maskf_done, 3)
                    act.activation(sd[:, t:t + 1], ss[:, t:t + 1], ACT.Sqrt, bias=epst[:, 0:1],
                                   scale=1.0 / D).then_inc(sd_done, 1)
                    if t >= 1:
                        hi_parts(act, t - 1)
                hi_parts(act, NT - 1)

            @block.vector
            def _(dve):
                def lo_parts(t):
                    for j in range(2):
                        dve.wait_ge(h_hi_done, 2 * t + j + 1)
                        new = 64 if t == NT - 1 else 0
                        dve.tensor_tensor(hlo[:, 4 * j:4 * j + 4, TOK[t] + new:TOK[t] + P],
                                          bank[2 * (t % 2) + j][:, :].rearrange("p (k t) -> p k t", k=4)[:, :, new:],
                                          hhi[:, 4 * j:4 * j + 4, TOK[t] + new:TOK[t] + P].bitcast(F32),
                                          ALU.subtract).then_inc(h_lo_done, 1)

                dve.wait_ge(g_in, 16)
                for t in range(NT):
                    dve.wait_ge(sd_done, t + 1)
                    dve.reciprocal(rs[:, t:t + 1], sd[:, t:t + 1]).then_inc(rs_done1, 1)
                    dve.wait_ge(rs_done1, t + 1)
                    dve.scalar_tensor_tensor(out=xt[:, t % 3, :], in0=xt[:, t % 3, :], scalar=rs[:, t:t + 1],
                                             in1=g1[:, :], op0=ALU.mult, op1=ALU.mult).then_inc(xn_done, 1)
                    if t >= 1:
                        lo_parts(t - 1)
                lo_parts(NT - 1)
                dve.wait_ge(maskf_done, 11)
                dve.tensor_copy(identb[:, :], ident[:, :]).then_inc(const_done, 1)
                dve.tensor_copy(maskb[:, :, :], maskf[:, :, :]).then_inc(const_done, 1)
                dve.wait_ge(par_ready, 1)
                b4, b5 = bank[4], bank[5]
                dve.tensor_copy(prm[:, :], b4[:, 0:88]).then_inc(par_done, 1)
                dve.tensor_copy(ffw[:, :, :], b4[:, 88:220].rearrange("p (w r) -> p w r", w=3)).then_inc(par_done, 1)
                dve.tensor_copy(ffn_state[:, :, :], b4[:, 220:308].rearrange("p (w r) -> p w r", w=2)).then_inc(par_done, 1)
                dve.tensor_copy(dww[:, :, :], b5[:, 0:128].rearrange("p (k w) -> p k w", k=4)[:, :, 0:CW]).then_inc(par_done, 1)
                dve.tensor_copy(conv_state[:, :, :],
                                b5[:, 128:256].rearrange("p (k w) -> p k w", k=4)[:, :, 0:CW - 1]).then_inc(par_done, 1)

            @block.tensor
            def _(pe):
                pe.wait_ge(maskf_done, 4)
                for t in range(NT):
                    pe.wait_ge(xn_done, t + 1)
                    if t >= 2:
                        pe.wait_ge(h_lo_done, 2 * (t - 1))
                    for k in range(KT):
                        mm = pe.transpose(bank[2 * (t % 2) + k // 4][:, (k % 4) * P:(k % 4 + 1) * P],
                                          xt[:, t % 3, k * P:(k + 1) * P], ident[:, :])
                    mm.then_inc(xt_ready, 1)
                pe.wait_ge(par_in, 160)
                b4, b5 = bank[4], bank[5]
                pe.transpose(b4[:, 0:88], prm_rows[:, :], ident[0:88, 0:88])
                for w in range(FW):
                    pe.transpose(b4[:, 88 + 44 * w:132 + 44 * w], ffw_rows[:, w, :], ident[0:44, 0:44])
                for w in range(2):
                    pe.transpose(b4[:, 220 + 44 * w:264 + 44 * w], fst_rows[:, w, :], ident[0:44, 0:44])
                for k in range(4):
                    pe.transpose(b5[:, 32 * k:32 * k + CW], dww_rows[:, P * k:P * k + P], ident[0:CW, 0:CW])
                    mm = pe.transpose(b5[:, 128 + 32 * k:128 + 32 * k + CW - 1], cst_rows[:, P * k:P * k + P],
                                      ident[0:CW - 1, 0:CW - 1])
                mm.then_inc(par_ready, 1)

        with ExitStack() as c2:
            stage = sb("stage", [P, NT, 3 * P], c=c2)
            vnew = sb("vnew", [P, NT, P], c=c2)
            kT = sb("kT", [P, T], c=c2)
            qz = sb("qz", [P, NB, P], c=c2)
            kpast = sb("kpast", [P, 2, 4, P], c=c2)
            kTpast = sb("kTpast", [P, 2, 512], c=c2)
            vpast = sb("vpast", [P, 2, 4, P], c=c2)
            sg = sb("sg", [P, 2, 512], c=c2)
            sn = sb("sn", [P, 2, 513], c=c2)
            run = sb("run", [P, 2, 513], c=c2)
            wT = sb("wT", [P, 2, 512], c=c2)
            o_sb = sb("o_sb", [P, T], c=c2)
            u = sb("u", [P, 2, UCOLS], c=c2)
            c_sb = sb("c_sb", [P, COUT], c=c2)
            sigb = sb("sigb", [P, 364], c=c2)
            bias_b = sb("bias_b", [P, 1], c=c2)
            bqkv = sb("bqkv", [P, 3 * P], c=c2)
            gqk = sb("gqk", [P, 2 * P], c=c2)
            ssq = sb("ssq", [P, NT * 4], c=c2)
            sdq = sb("sdq", [P, NT * 4], c=c2)
            rsq = sb("rsq", [P, NT * 4], c=c2)
            junk = sb("junk", [P, 4, DH], c=c2)
            utail = sb("utail", [P, 4, 2 * (CW - 1)], c=c2)

            raw_in = [sem(f"raw_in{i}") for i in range(2)]
            hi_done, lo_done = sem("hi_done"), sem("lo_done")
            g_in2, b_in2, init_done = sem("g_in2"), sem("b_in2"), sem("init_done")
            kp_in = [sem(f"kp_in{i}") for i in range(2)]
            vp_in = [sem(f"vp_in{i}") for i in range(2)]
            pj_ready, qkv_ev, b_ev, a_ev = sem("pj_ready"), sem("qkv_ev"), sem("b_ev"), sem("a_ev")
            stat_done, sdq_done, rsq_done, m1_done, norm_done = (sem("stat_done"), sem("sdq_done"), sem("rsq_done"),
                                                               sem("m1_done"), sem("norm_done"))
            bias_b_done = sem("bias_b_done")
            kv_out, v_copy, u_state = sem("kv_out"), sem("v_copy"), sem("u_state")
            wt_ready, act_ev, q_ev = sem("wt_ready"), sem("act_ev"), sem("q_ev")
            z_ready, sig_done, scan_done, w_done = sem("z_ready"), sem("sig_done"), sem("scan_done"), sem("w_done")
            av_done, o_ev, tap_done, spill = sem("av_done"), sem("o_ev"), sem("tap_done"), sem("spill")
            tail_ready, tail_done, tail_out = sem("tail_ready"), sem("tail_done"), sem("tail_out")

            ctail = c_sb[0:CW - 1, 0:2 * CC]
            PJ, ZB, WB, OB = bank[0:2], bank[2:4], bank[4:6], bank[6:8]
            PREP_BEFORE_RAW = [0, -1, 1, 2, 3]
            RAW_USES = ((3, {0: 0, 2: 1, 4: 2}), (2, {1: 0, 3: 1}))
            block = c2.enter_context(nc.Block())

            @block.sync
            def _(sp):
                def load_slot(s, p, col):
                    need = PREP_BEFORE_RAW[s] + 5 * p
                    if later(need):
                        sp.wait_ge(lo_done, need)
                    sp.dma_start(wraw[:, s % 2, :].rearrange("p (k n) -> p k n", k=KT),
                                 w_in[:, :, ds(col, P)]).then_inc(raw_in[s % 2], 16)

                def load_qkv(p):
                    for s in range(3):
                        load_slot(s, p, AW * s + P * p)

                def load_ab(p):
                    load_slot(3, p, 3 * AW + CC + P * p)
                    load_slot(4, p, 3 * AW + P * p)

                def load_bias(p):
                    sp.dma_start(bqkv[:, :].rearrange("p (x c) -> p x c", x=3),
                                 a["b_in"][0, 0:3 * AW].rearrange("(x n) -> x n", x=3)[:, ds(P * p, P)]
                                 .partition_broadcast(P)).then_inc(b_in2, 16)

                def load_past(p, j, kv):
                    dst, cache, s_in, used, pairs_uses, done = (
                        (kpast, "cache_sb_k", kp_in, wt_ready, NWT, WT_JOBS.index(f"past{j % 2}") + 1) if kv == "k" else
                        (vpast, "cache_sb_v", vp_in, av_done, NU, PASTS[j % 2] + 1))
                    if j >= 2:
                        sp.wait_ge(used, pairs_uses * p + done)
                    elif later(p):
                        sp.wait_ge(used, pairs_uses * p)
                    src = a[cache][0, 0].rearrange("(b r) h d -> r b (h d)", r=P)
                    sp.dma_start(dst[:, j % 2, :, :], src[:, 4 * (3 - j):4 * (3 - j) + 4, ds(P * p, P)]
                                 ).then_inc(s_in[j % 2], 16)

                def store_kv(p):
                    sp.wait_ge(norm_done, p + 1)
                    for x, name in ((1, "k"), (2, "v")):
                        dst = o[f"{name}_prompt"][0, 0].rearrange("(t r) h d -> r t (h d)", r=P)
                        sp.dma_start(dst[:, :, ds(P * p, P)], stage[:, 0:NT - 1, P * x:P * x + P]).then_inc(kv_out, 16)
                        dst = o[f"{name}_sample"][0, 0].rearrange("t h d -> t (h d)")
                        sp.dma_start(dst[:, ds(P * p, P)], stage[64:P, NT - 1, P * x:P * x + P]).then_inc(kv_out, 16)

                def store_oc(p):
                    sp.wait_ge(o_ev, 5 * p + 5)
                    sp.dma_start(scr["o"][ds(p, 1)].rearrange("a p t -> (a p) t"), o_sb[:, :]).then_inc(spill, 16)
                    sp.wait_ge(tap_done, CW * p + CW)
                    dst = scr["c"][ds(p, 1)].rearrange("a p t -> (a p) t")
                    sp.dma_start(dst[:, 0:SEQ], c_sb[:, 0:SEQ]).then_inc(spill, 16)
                    sp.dma_start(dst[:, SEQ:T], c_sb[:, U_SAMPLE:COUT]).then_inc(spill, 16)

                def pair(p, loads):
                    if loads:
                        sp.wait_ge(qkv_ev, NT * p + NT)
                        load_bias(p + 1)
                    store_kv(p)
                    if loads:
                        load_ab(p + 1)
                    else:
                        for s in (3, 4):
                            load_slot(s, 4, gate_col(s))
                    for j in range(2):
                        load_past(p, j, "k")
                        load_past(p, j, "v")
                    if loads == "qkv":
                        load_qkv(p + 2)
                    elif loads:
                        for s in range(3):
                            load_slot(s, 4, gate_col(s))
                    for kv in "kv":
                        load_past(p, 2, kv)
                        load_past(p, 3, kv)
                    store_oc(p)

                for x, name in enumerate(("q_norm_g", "k_norm_g")):
                    for hd in range(2):
                        sp.dma_start(gqk[:, P * x + DH * hd:P * x + DH * hd + DH],
                                     a[name][0:1, :].to_broadcast([P, DH])).then_inc(g_in2, 16)
                load_bias(0)
                load_qkv(0)
                load_ab(0)
                load_qkv(1)
                with sp.Fori(0, 2) as p:
                    pair(p, "qkv")
                pair(2, "gates")
                pair(3, "")
                sp.wait_ge(kv_out, 64 * PAIRS)
                sp.wait_ge(spill, 48 * PAIRS)
                sp.wait_ge(tail_done, 2)
                sp.dma_start(o["conv_prompt"][0, 0], ctail[:, 0:CC]).then_inc(tail_out, 16)
                sp.dma_start(o["conv_sample"][0, 0], ctail[:, CC:2 * CC]).then_inc(tail_out, 16)
                sp.wait_ge(tail_out, 32)

            @block.gpsimd
            def _(pool):
                def lo(s, p):
                    pool.wait_ge(hi_done, 5 * p + s + 1)
                    pool.tensor_tensor(wlo[:, s, :], wraw[:, s % 2, :], whi[:, s, :].bitcast(F32),
                                       ALU.subtract).then_inc(lo_done, 1)

                pool.memset(qz[:, :, :], 0.0).then_inc(init_done, 1)
                pool.memset(sn[:, :, 512:513], 1.0).then_inc(init_done, 1)
                pool.memset(u[:, :, 0:CW - 1], 0.0).then_inc(init_done, 1)
                for s in range(5):
                    lo(s, 0)
                for s in range(3):
                    lo(s, 1)
                with pool.Fori(0, 3) as p:
                    for s in (3, 4):
                        lo(s, p + 1)
                    for s in range(3):
                        lo(s, p + 2)
                for s in (3, 4):
                    lo(s, 4)

            @block.scalar
            def _(act):
                def hi(s, p):
                    per, at = RAW_USES[s % 2]
                    act.wait_ge(raw_in[s % 2], 16 * (per * p + at[s] + 1))
                    if later(p):
                        act.wait_ge(pj_ready, 15 * p - 6 if s < 3 else 15 * p)
                    act.activation(whi[:, s, :], wraw[:, s % 2, :], ACT.Copy).then_inc(hi_done, 1)

                def stats(p, t):
                    act.wait_ge(qkv_ev, NT * p + t + 1)
                    if t > 0 or later(p):
                        act.wait_ge(stat_done, NT * p + t)
                    for g in range(4):
                        ins = act.activation(junk[:, g, :], stage[:, t, DH * g:DH * g + DH], ACT.Square,
                                             accum_out=ssq[:, 4 * t + g:4 * t + g + 1])
                    ins.then_inc(stat_done, 1)

                def b_evac(p, c):
                    c0, c1_ = CHUNKS[c]
                    act.wait_ge(pj_ready, 15 * p + 10 + 2 * c)
                    need = 3 * p + c
                    if later(need):
                        act.wait_ge(a_ev, need)
                    act.wait_ge(bias_b_done, p + 1)
                    act.activation(sigb[:, 0:c1_ - c0], PJ[(9 + 2 * c) % 2][:, 0:c1_ - c0], ACT.Sigmoid,
                                   bias=bias_b[:, :]).then_inc(b_ev, 1)

                def state(p):
                    if later(p):
                        act.wait_ge(tap_done, CW * p - CW if not isinstance(p, int) else CW * (p - 1))
                    act.activation(u[:, ds(p % 2, 1), U_SAMPLE:U_SAMPLE + CW - 1].rearrange("p a t -> p (a t)"),
                                   conv_state[:, ds(p, 1), :].rearrange("p a t -> p (a t)"), ACT.Copy).then_inc(u_state, 1)

                def tails(p):
                    act.wait_ge(a_ev, 3 * p + 3)
                    act.wait_ge(u_state, 3 * p + 1)
                    for x, first in enumerate((SEQ, UCOLS - (CW - 1))):
                        act.activation(utail[:, ds(p, 1), (CW - 1) * x:(CW - 1) * (x + 1)].rearrange("p a t -> p (a t)"),
                                       u[:, ds(p % 2, 1), first:first + CW - 1].rearrange("p a t -> p (a t)"),
                                       ACT.Copy).then_inc(u_state, 1)

                def commit(p):
                    act.wait_ge(stat_done, NT * p + NT)
                    act.activation(sdq[:, :], ssq[:, :], ACT.Sqrt, bias=epst[:, 0:1], scale=1.0 / DH).then_inc(sdq_done, 1)
                    if later(p):
                        act.wait_ge(av_done, NU * p)
                    act.activation(vnew[:, :, :], stage[:, :, 2 * P:3 * P], ACT.Copy).then_inc(v_copy, 1)
                    for j in range(3):
                        act.wait_ge(wt_ready, NWT * p + j + 1)
                        t0, b0, n = (512 * j, 0, 512) if j < 2 else (SEQ, P - DEC, DEC)
                        act.activation(kT[:, t0:t0 + n], WB[j % 2][:, b0:b0 + n], ACT.Copy).then_inc(act_ev, 1)

                def sig(p, s):
                    n = UNITS[s][2]
                    act.wait_ge(z_ready, NU * p + s + 1)
                    if s >= 2:
                        act.wait_ge(wt_ready, NWT * p + WT_JOBS.index(f"w{s - 2}") + 1)
                    z = ZB[s % 2][:, 0:n]
                    act.activation(sn[:, s % 2, 512 - n:512], z, ACT.Sigmoid, scale=-DH ** -0.5)
                    act.activation(sg[:, s % 2, 0:n], z, ACT.Sigmoid, scale=DH ** -0.5).then_inc(sig_done, 1)

                def w_evac(p, s):
                    n = UNITS[s][2]
                    act.wait_ge(wt_ready, NWT * p + WT_JOBS.index(f"w{s}") + 1)
                    need = NU * p + s - 1
                    if later(need):
                        act.wait_ge(av_done, need if s >= 1 else NU * p)
                    act.activation(wT[:, s % 2, 0:n], WB[WT_JOBS.index(f"w{s}") % 2][:, 0:n], ACT.Copy).then_inc(act_ev, 1)

                def past_evac(p, j):
                    n = WT_JOBS.index(f"past{j}")
                    act.wait_ge(wt_ready, NWT * p + n + 1)
                    if j >= 2:
                        act.wait_ge(z_ready, NU * p + PASTS[j - 2] + 1)
                    act.activation(kTpast[:, j % 2, :], WB[n % 2][:, :], ACT.Copy).then_inc(act_ev, 1)

                def o_evac(p, g):
                    last = max(x for x in range(NU) if UNITS[x][0] // 4 == g)
                    nb = 4 if g < 4 else 1
                    act.wait_ge(av_done, NU * p + last + 1)
                    if g == 0 and (later(p)):
                        act.wait_ge(spill, 48 * p)
                    for hd in range(2):
                        r = slice(DH * hd, DH * hd + DH)
                        ins = act.activation(o_sb[r, 256 * g:256 * g + QB * nb].rearrange("p (b q) -> p b q", b=nb),
                                             OB[g % 2][r, 0:P * nb].rearrange("p (b q) -> p b q", b=nb)
                                             [:, :, QB * hd:QB * hd + QB], ACT.Copy)
                    ins.then_inc(o_ev, 1)

                def pair(p, more):
                    commit(p)
                    for s in range(NS):
                        if s + 1 in PASTS:
                            past_evac(p, PASTS.index(s + 1))
                        if s < NU:
                            sig(p, s)
                        if 0 <= s - 2 < NU:
                            w_evac(p, s - 2)
                        if s >= 4 and UNITS[s - 4][4] and (UNITS[s - 4][0] % 4 == 3 or UNITS[s - 4][0] == NB - 1):
                            o_evac(p, UNITS[s - 4][0] // 4)
                        if s in (1, 3):
                            hi(3 + s // 2, p + 1)
                        if more:
                            if s >= 3 and s % 2 == 1 and (s - 3) // 2 < NT:
                                stats(p + 1, (s - 3) // 2)
                            if s in (20, 24, 28):
                                b_evac(p + 1, (s - 20) // 4)
                            if s in (21, 22, 23):
                                hi(s - 21, p + 2)
                            if s == 25:
                                state(p + 1)
                            if s == 31:
                                tails(p + 1)

                act.wait_ge(init_done, 3)
                for s in range(5):
                    hi(s, 0)
                for t in range(NT):
                    stats(0, t)
                for c in range(3):
                    b_evac(0, c)
                state(0)
                tails(0)
                for s in range(3):
                    hi(s, 1)
                with act.Fori(0, 3) as p:
                    pair(p, True)
                pair(3, False)
                for x in range(2):
                    act.wait_ge(tail_ready, 1)
                    act.wait_ge(spill, 48 * PAIRS)
                    act.activation(ctail[:, CC * x:CC * x + CC], WB[x][0:CW - 1, :], ACT.Copy).then_inc(tail_done, 1)

            @block.vector
            def _(dve):
                def qkv_evac(p, t):
                    dve.wait_ge(pj_ready, 15 * p + t + 1)
                    if t == 0:
                        if later(p):
                            dve.wait_ge(b_ev, 3 * p)
                        bias = prm[:, ds(PRM_BIN + 4 + p, 1)]
                        dve.tensor_tensor(bias_b[:, :], bias, bias, ALU.max).then_inc(bias_b_done, 1)
                        dve.wait_ge(b_in2, 16 * p + 16)
                        if later(p):
                            dve.wait_ge(kv_out, 64 * p)
                            dve.wait_ge(v_copy, p)
                            dve.wait_ge(wt_ready, NWT * (p - 1) + 6)
                    dve.tensor_tensor(stage[:, t, :], PJ[t % 2][:, 0:3 * P], bqkv[:, :], ALU.add).then_inc(qkv_ev, 1)

                def a_evac(p, c):
                    c0, c1_ = CHUNKS[c]
                    dve.wait_ge(pj_ready, 15 * p + 11 + 2 * c)
                    dve.wait_ge(b_ev, 3 * p + c + 1)
                    bias = prm[:, ds(PRM_BIN + p, 1)]
                    parts = [(c0, c1_)] if c1_ <= SEQ else [(c0, SEQ), (SEQ, c1_)]
                    for x0, x1 in parts:
                        at = x0 + (CW - 1 if x0 < SEQ else 2 * (CW - 1))
                        ins = dve.scalar_tensor_tensor(
                            out=u[:, ds(p % 2, 1), at:at + x1 - x0].rearrange("p a t -> p (a t)"),
                            in0=PJ[(10 + 2 * c) % 2][:, x0 - c0:x1 - c0], scalar=bias, in1=sigb[:, x0 - c0:x1 - c0],
                            op0=ALU.add, op1=ALU.mult)
                    ins.then_inc(a_ev, 1)

                def tap(p, k):
                    if k == 0:
                        dve.wait_ge(a_ev, 3 * p + 3)
                        dve.wait_ge(u_state, 3 * p + 3)
                        if later(p):
                            dve.wait_ge(spill, 48 * p)
                    x = u[:, ds(p % 2, 1), k:k + COUT].rearrange("p a t -> p (a t)")
                    w = dww[:, ds(p, 1), k:k + 1].rearrange("p a t -> p (a t)")
                    if k == 0:
                        dve.tensor_scalar(c_sb[:, :], x, w, prm[:, ds(PRM_DWB + p, 1)], ALU.mult, ALU.add).then_inc(tap_done, 1)
                    else:
                        dve.wait_ge(tap_done, CW * p + k)
                        dve.scalar_tensor_tensor(out=c_sb[:, :], in0=x, scalar=w, in1=c_sb[:, :], op0=ALU.mult,
                                                 op1=ALU.add).then_inc(tap_done, 1)

                def commit(p):
                    dve.wait_ge(sdq_done, p + 1)
                    dve.reciprocal(rsq[:, :], sdq[:, :]).then_inc(rsq_done, 1)
                    dve.wait_ge(rsq_done, p + 1)
                    x = stage[:, :, 0:2 * P].rearrange("p t (g d) -> p t g d", d=DH)
                    dve.tensor_tensor(x, x, rsq[:, :].rearrange("p (t g) -> p t g", g=4).unsqueeze(3)
                                      .to_broadcast([P, NT, 4, DH]), ALU.mult).then_inc(m1_done, 1)
                    dve.wait_ge(m1_done, p + 1)
                    if isinstance(p, int) and p == 0:
                        dve.wait_ge(g_in2, 64)
                    y = stage[:, :, 0:2 * P]
                    dve.tensor_tensor(y, y, gqk[:, :].unsqueeze(1).to_broadcast([P, NT, 2 * P]), ALU.mult).then_inc(norm_done, 1)
                    for j in range(3):
                        dve.wait_ge(wt_ready, NWT * p + 4 + j)
                        b = WB[(3 + j) % 2]
                        for hd in range(2):
                            r = slice(DH * hd, DH * hd + DH)
                            if j < 2:
                                out = qz[r, 8 * j:8 * j + 8, QB * hd:QB * hd + QB]
                                src = b[r, :].rearrange("p (b q) -> p b q", b=8)
                            else:
                                out, src = qz[r, NB - 1, QB * hd:QB * hd + QB], b[r, 64:P]
                            ins = dve.tensor_copy(out, src)
                        ins.then_inc(q_ev, 1)

                def weights(p, s):
                    n, first = UNITS[s][2], UNITS[s][3]
                    dve.wait_ge(sig_done, NU * p + s + 1)
                    x = sn[:, s % 2, 512 - n:513][:, ::-1]
                    if s >= 2 or later(p):
                        dve.wait_ge(w_done, NU * p + max(s - 1, 0))
                    init = 1.0 if first else run[:, (s - 1) % 2, 512 - UNITS[s - 1][2]:513 - UNITS[s - 1][2]]
                    dve.tensor_tensor_scan(run[:, s % 2, 512 - n:513][:, ::-1], x, x, init, ALU.mult,
                                           ALU.min).then_inc(scan_done, 1)
                    dve.wait_ge(scan_done, NU * p + s + 1)
                    dve.tensor_tensor(sg[:, s % 2, 0:n], sg[:, s % 2, 0:n], run[:, s % 2, 513 - n:513],
                                      ALU.mult).then_inc(w_done, 1)

                def pair(p, more):
                    commit(p)
                    for s in range(NS):
                        if s < NU:
                            weights(p, s)
                        if more and s >= 2 and s % 2 == 0 and (s - 2) // 2 < NT:
                            qkv_evac(p + 1, (s - 2) // 2)
                        if more and s in (22, 26, 30):
                            a_evac(p + 1, (s - 22) // 4)
                        if 1 <= s < 1 + CW:
                            tap(p, s - 1)

                dve.wait_ge(init_done, 3)
                for t in range(NT):
                    qkv_evac(0, t)
                for c in range(3):
                    a_evac(0, c)
                with dve.Fori(0, 3) as p:
                    pair(p, True)
                pair(3, False)

            @block.tensor
            def _(pe):
                def free(n, p):
                    if n < 2:
                        if later(p):
                            pe.wait_ge(act_ev, NEV * p)
                        return
                    job = WT_JOBS[n - 2]
                    if job[0] == "q":
                        pe.wait_ge(q_ev, 3 * p + int(job[1:]) + 1)
                    else:
                        pe.wait_ge(act_ev, NEV * p + ACT_EVACS.index(job) + 1)

                def qkv_half(p, t, half):
                    if half == 0:
                        if t == 0:
                            pe.wait_ge(lo_done, 5 * p + 3)
                        if t >= 2:
                            pe.wait_ge(qkv_ev, NT * p + t - 1)
                        elif later(p):
                            pe.wait_ge(a_ev, 3 * p)
                            pe.wait_ge(b_ev, 3 * p)
                    tok = slice(TOK[t], TOK[t] + P)
                    for k in range(4 * half, 4 * half + 4):
                        ws = slice(P * k, P * k + P)
                        for n, (x, w) in enumerate(split_passes(hhi, hlo, whi, wlo)):
                            mm = pe.matmul(PJ[t % 2][:, 0:3 * P], x[:, k, tok], w[:, 0:3, ws],
                                           start=(k == 0 and n == 0), stop=(k == KT - 1 and n == 2))
                    if half:
                        mm.then_inc(pj_ready, 1)

                def ab_half(p, n, half):
                    if half == 0:
                        if n == 0:
                            pe.wait_ge(lo_done, 5 * p + 5)
                        if n < 2:
                            pe.wait_ge(qkv_ev, NT * p + 8 + n)
                        elif n % 2 == 0:
                            pe.wait_ge(b_ev, 3 * p + n // 2)
                        else:
                            pe.wait_ge(a_ev, 3 * p + n // 2)
                    c0, c1_ = CHUNKS[n // 2]
                    slot = 3 + n % 2
                    for k in range(4 * half, 4 * half + 4):
                        ws = slice(P * k, P * k + P)
                        for i, (w, x) in enumerate(split_passes(whi, wlo, hhi, hlo)):
                            mm = pe.matmul(PJ[(9 + n) % 2][:, 0:c1_ - c0], w[:, slot, ws], x[:, k, c0:c1_],
                                           start=(k == 0 and i == 0), stop=(k == KT - 1 and i == 2))
                    if half:
                        mm.then_inc(pj_ready, 1)

                def commit(p):
                    pe.wait_ge(norm_done, p + 1)
                    for n in range(6):
                        free(n, p)
                        x, j = 1 - n // 3, n % 3
                        tiles = range(4 * j, 4 * j + 4) if j < 2 else [NT - 1]
                        for i, t in enumerate(tiles):
                            mm = pe.transpose(WB[n % 2][:, P * i:P * i + P], stage[:, t, P * x:P * x + P], ident[:, :])
                        mm.then_inc(wt_ready, 1)

                def past_transposes(p, j):
                    n = WT_JOBS.index(f"past{j}")
                    free(n, p)
                    pe.wait_ge(kp_in[j % 2], 16 * (2 * p + j // 2 + 1))
                    for b in range(4):
                        mm = pe.transpose(WB[n % 2][:, P * b:P * b + P], kpast[:, j % 2, b, :], ident[:, :])
                    mm.then_inc(wt_ready, 1)

                def scores(p, s):
                    i, k0, n, first, last, past, mask = UNITS[s]
                    if s >= 2:
                        pe.wait_ge(sig_done, NU * p + s - 1)
                    elif later(p):
                        pe.wait_ge(sig_done, NU * p)
                    if s == 0:
                        pe.wait_ge(act_ev, NEV * p + 3)
                        pe.wait_ge(q_ev, 3 * p + 3)
                    if past is None:
                        keys = kT[:, k0:k0 + n]
                    else:
                        j = PASTS.index(s)
                        pe.wait_ge(act_ev, NEV * p + ACT_EVACS.index(f"past{j}") + 1)
                        keys = kTpast[:, j % 2, :]
                    mm = pe.matmul(ZB[s % 2][:, 0:n], qz[:, i, :], keys, start=True, stop=True)
                    if mask is not None:
                        mm = pe.matmul(ZB[s % 2][:, n - P:n], identb[:, :], maskb[:, mask, :], start=False, stop=True,
                                       skip_group_check=True)
                    mm.then_inc(z_ready, 1)

                def w_transposes(p, s):
                    n = WT_JOBS.index(f"w{s}")
                    free(n, p)
                    pe.wait_ge(w_done, NU * p + s + 1)
                    for b in range(UNITS[s][2] // P):
                        mm = pe.transpose(WB[n % 2][:, P * b:P * b + P], sg[:, s % 2, P * b:P * b + P], ident[:, :])
                    mm.then_inc(wt_ready, 1)

                def outputs(p, s):
                    i, k0, n, first, last, past, mask = UNITS[s]
                    g = i // 4
                    pe.wait_ge(act_ev, NEV * p + ACT_EVACS.index(f"w{s}") + 1)
                    if s == 0:
                        pe.wait_ge(v_copy, p + 1)
                    if past is not None:
                        j = PASTS.index(s)
                        pe.wait_ge(vp_in[j % 2], 16 * (2 * p + j // 2 + 1))
                    if i % 4 == 0 and first:
                        need = 5 * p + max(g - 1, 0)
                        if later(need):
                            pe.wait_ge(o_ev, need)
                    nb = n // P
                    for b in range(nb):
                        if past is not None:
                            v = vpast[:, PASTS.index(s) % 2, b, :]
                        else:
                            v = vnew[:, k0 // P + b if k0 < T - P else NT - 1, :]
                        mm = pe.matmul(OB[g % 2][:, P * (i % 4):P * (i % 4) + P], v, wT[:, s % 2, P * b:P * b + P],
                                       start=(first and b == 0), stop=(last and b == nb - 1))
                    mm.then_inc(av_done, 1)

                def pair(p, more):
                    commit(p)
                    for s in range(NS):
                        if s + 1 in PASTS:
                            past_transposes(p, PASTS.index(s + 1))
                        if s < NU:
                            scores(p, s)
                        if 0 <= s - 2 < NU:
                            w_transposes(p, s - 2)
                        if 0 <= s - 3 < NU:
                            outputs(p, s - 3)
                        if more and s < 18:
                            qkv_half(p + 1, s // 2, s % 2)
                        elif more and s < 30:
                            ab_half(p + 1, (s - 18) // 2, s % 2)

                pe.wait_ge(init_done, 3)
                for s in range(18):
                    qkv_half(0, s // 2, s % 2)
                for s in range(12):
                    ab_half(0, s // 2, s % 2)
                with pe.Fori(0, 3) as p:
                    pair(p, True)
                pair(3, False)
                pe.wait_ge(act_ev, NEV * PAIRS)
                pe.wait_ge(u_state, 3 * PAIRS)
                for x in range(2):
                    for m in range(4):
                        mm = pe.transpose(WB[x][0:CW - 1, P * m:P * m + P],
                                          utail[:, m, (CW - 1) * x:(CW - 1) * (x + 1)], ident[:, :])
                mm.then_inc(tail_ready, 1)

        c_bytes = 4 * 4 * T
        top = nc.sbuf_usable_end

        def pinned(name, nth):
            return nc.alloc_sbuf_tensor_at(name, [P, 4, T], F32R, offset=(top - (nth + 1) * c_bytes) // 32 * 32)

        NG = 2 * KT
        FIRST_FFN = [(0, 0), (1, 1), (2, 2), (3, 3)]
        w_out = a["w_out"][0].rearrange("(k p) n -> p k n", p=P)
        w_up = a["w_up"][0].rearrange("(k p) n -> p k n", p=P)
        w_down = a["w_down"][0].rearrange("(k p) n -> p k n", p=P)
        w_ac = [a["w_attn_out"][0].rearrange("(k p) n -> p k n", p=P), a["w_conv_out"][0].rearrange("(k p) n -> p k n", p=P)]

        def send_raw(sp, sems, n, parity, halves):
            if later(n, 2):
                sp.wait_ge(sems[2], n - 1)
            for h, src in enumerate(halves):
                dst = wraw[:, parity, 512 * h:512 * h + 512]
                if len(src.shape) == 3:
                    dst = dst.rearrange("p (k n) -> p k n", n=P)
                sp.dma_start(dst, src).then_inc(sems[0][parity], 16)

        def k_halves(w, col):
            return [w[:, 0:4, ds(col, P)], w[:, 4:8, ds(col, P)]]

        def send_out_weights(sp, sems, n, parity, k, i):
            if k < 2:
                send_raw(sp, sems, n, parity, [w[:, :, ds(P * (2 * i + k), P)] for w in w_ac])
            else:
                rows = w_out[:, ds(2 * i + k - 2, 1), :].rearrange("p k n -> p (k n)")
                send_raw(sp, sems, n, parity, [rows[:, 0:512], rows[:, 512:D]])

        def send_ffn_weights(sp, sems, n, parity, what, i):
            if what < 4:
                send_raw(sp, sems, n, parity, k_halves(w_up, FF * (what % 2) + P * (2 * i + what // 2)))
            else:
                rows = w_down[:, ds(2 * i + what - 4, 1), :].rearrange("p k n -> p (k n)")
                send_raw(sp, sems, n, parity, [rows[:, 0:512], rows[:, 512:D]])

        def make_hi(act, sems, raw_count, n, parity, dst):
            act.wait_ge(sems[0][parity], 32 * raw_count)
            act.activation(dst, wraw[:, parity, :], ACT.Copy).then_inc(sems[1], 1)

        def make_lo(pool, sems, n, parity, dst, hi):
            pool.wait_ge(sems[1], n + 1)
            pool.tensor_tensor(dst, wraw[:, parity, :], hi.bitcast(F32), ALU.subtract).then_inc(sems[2], 1)

        with ExitStack() as c3:
            chi, clo = pinned("chi", 0), pinned("clo", 1)
            craw = sb("craw", [P, 4, T], c=c3)
            gst = sb("gst", [P, 2, T], c=c3)
            csq = sb("csq", [P, 4, 364], c=c3)
            csig = sb("csig", [P, 4, 364], c=c3)
            crs = sb("crs", [P, T], c=c3)
            ones = sb("ones", [P, P], c=c3)
            raw3 = ([sem("raw3_in0"), sem("raw3_in1")], sem("hi3_done"), sem("lo3_done"))
            c_in, ones_done, g_ready, g_ev = sem("c_in"), sem("ones_done"), sem("g_ready"), sem("g_ev")
            gate_out = [sem("gate_out0"), sem("gate_out1")]
            mean_ready, xc_done, csq_done, var_ready = sem("mean_ready"), sem("xc_done"), sem("csq_done"), sem("var_ready")
            csd_done, crs_done, cn_done, csig_done = sem("csd_done"), sem("crs_done"), sem("cn_done"), sem("csig_done")
            caff_done, cact_done, chi_done, clo_done = sem("caff_done"), sem("cact_done"), sem("chi_done"), sem("clo_done")
            PREP3 = [(g % 5, 3 * (g - 4)) for g in range(5, NG)] + [(1, 36), (2, 39), (3, 42), (4, 45)]
            block = c3.enter_context(nc.Block())

            @block.sync
            def _(sp):
                for m in range(4):
                    sp.dma_start(craw[:, m, :], scr["c"][m]).then_inc(c_in, 16)
                n = 0
                for g in range(NG):
                    while n < len(PREP3) and n < g + 3:
                        if n < NG - 5:
                            send_raw(sp, raw3, n, n % 2, k_halves(w_in, gate_col(5 + n)))
                        else:
                            send_out_weights(sp, raw3, n, n % 2, n - (NG - 5), 0)
                        n += 1
                    sp.wait_ge(g_ev, 3 * g + 3)
                    sp.dma_start(scr["gate"][g], gst[:, g % 2, :]).then_inc(gate_out[g % 2], 16)
                for x in range(2):
                    sp.wait_ge(gate_out[x], 16 * NG // 2)

            @block.gpsimd
            def _(pool):
                pool.memset(ones[:, :], 1.0 / CC).then_inc(ones_done, 1)

                def c_lo(c):
                    c0, c1_ = CHUNKS[c]
                    pool.wait_ge(chi_done, c + 1)
                    pool.tensor_tensor(clo[:, :, c0:c1_], craw[:, :, c0:c1_], chi[:, :, c0:c1_].bitcast(F32),
                                       ALU.subtract).then_inc(clo_done, 1)

                for n, (slot, _need) in enumerate(PREP3):
                    make_lo(pool, raw3, n, n % 2, wlo[:, slot, :], whi[:, slot, :])
                    if n in (8, 10, 12):
                        c_lo((n - 8) // 2)

            @block.scalar
            def _(act):
                def gate_evac(j):
                    g, c = j // 3, j % 3
                    c0, c1_ = CHUNKS[c]
                    act.wait_ge(g_ready, j + 1)
                    if c == 0 and g >= 2:
                        act.wait_ge(gate_out[g % 2], 16 * (g // 2))
                    act.activation(gst[:, g % 2, c0:c1_], bank[j % 4][:, 0:c1_ - c0], ACT.Sigmoid,
                                   bias=prm[:, PRM_BIN + 8 + KT * (g % 2) + g // 2:PRM_BIN + 9 + KT * (g % 2) + g // 2]
                                   ).then_inc(g_ev, 1)

                def squares(c):
                    c0, c1_ = CHUNKS[c]
                    act.wait_ge(xc_done, c + 1)
                    if c:
                        act.wait_ge(var_ready, c)
                    act.activation(csq[:, :, 0:c1_ - c0], craw[:, :, c0:c1_], ACT.Square).then_inc(csq_done, 1)

                def roots():
                    for c, (c0, c1_) in enumerate(CHUNKS):
                        act.wait_ge(var_ready, c + 1)
                        act.activation(crs[:, c0:c1_], bank[4 + c][:, 0:c1_ - c0], ACT.Sqrt,
                                       bias=epst[:, 0:1]).then_inc(csd_done, 1)

                def sigmoids(c):
                    c0, c1_ = CHUNKS[c]
                    act.wait_ge(cn_done, c + 1)
                    if c:
                        act.wait_ge(cact_done, c)
                    for m in range(4):
                        ins = act.activation(csig[:, m, 0:c1_ - c0], craw[:, m, c0:c1_], ACT.Sigmoid,
                                             scale=prm[:, PRM_CNG + m:PRM_CNG + m + 1],
                                             bias=prm[:, PRM_CNB + m:PRM_CNB + m + 1])
                    ins.then_inc(csig_done, 1)

                def c_hi(c):
                    c0, c1_ = CHUNKS[c]
                    act.wait_ge(cact_done, c + 1)
                    act.activation(chi[:, :, c0:c1_], craw[:, :, c0:c1_], ACT.Copy).then_inc(chi_done, 1)

                for j in range(3 * NG):
                    gate_evac(j)
                    if j in (4, 6, 8):
                        squares((j - 4) // 2)
                    if j == 12:
                        roots()
                    if j in (18, 22, 26):
                        sigmoids((j - 18) // 4)
                    if j in (21, 25, 29):
                        c_hi((j - 21) // 4)
                    if j % 3 == 2 and j // 3 < len(PREP3) - 4:
                        n = j // 3
                        act.wait_ge(g_ready, PREP3[n][1])
                        make_hi(act, raw3, n // 2 + 1, n, n % 2, whi[:, PREP3[n][0], :])
                    if j in (37, 40, 43, 46):
                        n = NG - 5 + (j - 37) // 3
                        act.wait_ge(g_ready, PREP3[n][1])
                        make_hi(act, raw3, n // 2 + 1, n, n % 2, whi[:, PREP3[n][0], :])

            @block.vector
            def _(dve):
                dve.wait_ge(c_in, 64)
                for c, (c0, c1_) in enumerate(CHUNKS):
                    dve.wait_ge(mean_ready, c + 1)
                    x = craw[:, :, c0:c1_]
                    dve.tensor_tensor(x, x, bank[4 + c][:, 0:c1_ - c0].unsqueeze(1).to_broadcast([P, 4, c1_ - c0]),
                                      ALU.subtract).then_inc(xc_done, 1)
                for c, (c0, c1_) in enumerate(CHUNKS):
                    dve.wait_ge(csd_done, c + 1)
                    dve.reciprocal(crs[:, c0:c1_], crs[:, c0:c1_]).then_inc(crs_done, 1)
                    dve.wait_ge(crs_done, c + 1)
                    x = craw[:, :, c0:c1_]
                    dve.tensor_tensor(x, x, crs[:, c0:c1_].unsqueeze(1).to_broadcast([P, 4, c1_ - c0]),
                                      ALU.mult).then_inc(cn_done, 1)
                for c, (c0, c1_) in enumerate(CHUNKS):
                    dve.wait_ge(csig_done, c + 1)
                    dve.wait_ge(cn_done, c + 1)
                    for m in range(4):
                        ins = dve.tensor_scalar(craw[:, m, c0:c1_], craw[:, m, c0:c1_],
                                                prm[:, PRM_CNG + m:PRM_CNG + m + 1], prm[:, PRM_CNB + m:PRM_CNB + m + 1],
                                                ALU.mult, ALU.add)
                    ins.then_inc(caff_done, 1)
                    dve.wait_ge(caff_done, c + 1)
                    dve.tensor_tensor(craw[:, :, c0:c1_], craw[:, :, c0:c1_], csig[:, :, 0:c1_ - c0],
                                      ALU.mult).then_inc(cact_done, 1)

            @block.tensor
            def _(pe):
                def gate_job(j):
                    g, c = j // 3, j % 3
                    c0, c1_ = CHUNKS[c]
                    if c == 0 and g >= 5:
                        pe.wait_ge(raw3[2], g - 4)
                    if j >= 4:
                        pe.wait_ge(g_ev, j - 3)
                    for k in range(KT):
                        ws = slice(P * k, P * k + P)
                        for i, (w, x) in enumerate(split_passes(whi, wlo, hhi, hlo)):
                            mm = pe.matmul(bank[j % 4][:, 0:c1_ - c0], w[:, g % 5, ws], x[:, k, c0:c1_],
                                           start=(k == 0 and i == 0), stop=(k == KT - 1 and i == 2))
                    mm.then_inc(g_ready, 1)

                def channel_mean(c, src, lo, done, need):
                    c0, c1_ = CHUNKS[c]
                    pe.wait_ge(done, need)
                    for m in range(4):
                        mm = pe.matmul(bank[4 + c][:, 0:c1_ - c0], ones[:, :], src[:, m, lo:lo + c1_ - c0],
                                       start=(m == 0), stop=(m == 3))
                    return mm

                pe.wait_ge(ones_done, 1)
                for j in range(3 * NG):
                    gate_job(j)
                    if j == 0:
                        for c in range(3):
                            channel_mean(c, craw, CHUNKS[c][0], c_in, 64).then_inc(mean_ready, 1)
                    if j in (5, 7, 9):
                        c = (j - 5) // 2
                        channel_mean(c, csq, 0, csq_done, c + 1).then_inc(var_ready, 1)

        hctx.close()

        x1 = sb("x1", [P, NT, D])
        CH_OF_TOK = [next(c for c in range(3) if CHUNKS[c][1] >= t0 + P) for t0 in TOK]

        def down_job(pe, d, acts, w_slots, i, down_ev, down_ready, lo_sem, lo_need, w_sem, w_need):
            t, half = d // 2, d % 2
            if d == 0:
                pe.wait_ge(w_sem, w_need)
            if half == 0:
                pe.wait_ge(lo_sem, lo_need(CH_OF_TOK[t]))
            if d >= 4:
                pe.wait_ge(down_ev, 18 * i + d - 3)
            elif later(i):
                pe.wait_ge(down_ev, 18 * i)
            x_hi, x_lo = acts
            for k in range(2):
                w_hi, w_lo = w_slots[k]
                for n, (x, w) in enumerate(split_passes(x_hi, x_lo, w_hi, w_lo)):
                    mm = pe.matmul(bank[4 + d % 4][:, :], x[:, k, TOK[t]:TOK[t] + P], w[:, 512 * half:512 * half + 512],
                                   start=(k == 0 and n == 0), stop=(k == 1 and n == 2))
            mm.then_inc(down_ready, 1)

        def down_add(dve, d, i, down_ready, down_ev):
            t, half = d // 2, d % 2
            dve.wait_ge(down_ready, 18 * i + d + 1)
            if later(i):
                dve.wait_ge(down_ev, 18 * i + d - 17)
            y = x1[:, t, 512 * half:512 * half + 512]
            dve.tensor_tensor(y, bank[4 + d % 4][:, :], y, ALU.add).then_inc(down_ev, 1)

        with ExitStack() as c4:
            ohi = sb("ohi", [P, 4, T], F32R, c4)
            olo = sb("olo", [P, 4, T], F32R, c4)
            mhi = sb("mhi", [P, 2, T], F32R, c4)
            mlo = sb("mlo", [P, 2, T], F32R, c4)
            oraw = sb("oraw", [P, 2, T], c=c4)
            gch = sb("gch", [P, 3, 2, 364], c=c4)
            mixa = sb("mixa", [P, 2, 364], c=c4)
            mixc = sb("mixc", [P, 2, 364], c=c4)
            raw4 = ([sem("raw4_in0"), sem("raw4_in1")], sem("hi4_done"), sem("lo4_done"))
            x1_in, o_hi_done, o_lo_done = sem("x1_in"), sem("o_hi_done"), sem("o_lo_done")
            o_in = [sem("o_in0"), sem("o_in1")]
            gch_in = [sem(f"gch_in{c}") for c in range(3)]
            ac_ready, ac_ev, mix_done, m_hi_done, m_lo_done = (sem("ac_ready"), sem("ac_ev"), sem("mix_done"),
                                                              sem("m_hi_done"), sem("m_lo_done"))
            dn4_ready, dn4_ev = sem("dn4_ready"), sem("dn4_ev")
            NI = KT // 2
            block = c4.enter_context(nc.Block())

            @block.sync
            def _(sp):
                def send_gates(i, j, c):
                    c0, c1_ = CHUNKS[c]
                    if j == 1:
                        sp.wait_ge(ac_ev, 12 * i + 2 * c + 2)
                    elif later(i):
                        sp.wait_ge(ac_ev, 12 * i + 2 * c - 4)
                    sp.dma_start(gch[:, c, :, 0:c1_ - c0],
                                 scr["gate"][ds(4 * i + 2 * j, 2)].rearrange("g p t -> p g t")[:, :, c0:c1_]
                                 ).then_inc(gch_in[c], 16)

                def round_(i, last):
                    for j in range(2):
                        for c in range(3):
                            send_gates(i, j, c)
                    for k in range(4):
                        n = 4 * i + k
                        if last:
                            send_ffn_weights(sp, raw4, n, k % 2, FIRST_FFN[k][1], 0)
                        else:
                            send_out_weights(sp, raw4, n, k % 2, k, i + 1)

                for m in range(4):
                    if m >= 2:
                        sp.wait_ge(o_lo_done, m - 1)
                    sp.dma_start(oraw[:, m % 2, :], scr["o"][m]).then_inc(o_in[m % 2], 16)
                sp.dma_start(x1[:, 0:NT - 1, :], a["x_prompt"][0].rearrange("(t p) n -> p t n", p=P)).then_inc(x1_in, 16)
                sp.dma_start(x1[0:64, NT - 1, :], a["x_prompt"][0, SEQ - 64:SEQ, :]).then_inc(x1_in, 16)
                sp.dma_start(x1[64:P, NT - 1, :], a["x_sample"][0]).then_inc(x1_in, 16)
                round_(0, False)
                with sp.Fori(1, NI - 1) as i:
                    round_(i, False)
                round_(NI - 1, True)

            @block.gpsimd
            def _(pool):
                for m in range(4):
                    pool.wait_ge(o_hi_done, m + 1)
                    pool.tensor_tensor(olo[:, m, :], oraw[:, m % 2, :], ohi[:, m, :].bitcast(F32),
                                       ALU.subtract).then_inc(o_lo_done, 1)

                def round_(i, slots):
                    for j in range(2):
                        for c, (c0, c1_) in enumerate(CHUNKS):
                            pool.wait_ge(m_hi_done, 6 * i + 3 * j + c + 1)
                            pool.tensor_tensor(mlo[:, j, c0:c1_], mixa[:, (3 * j + c) % 2, 0:c1_ - c0],
                                               mhi[:, j, c0:c1_].bitcast(F32), ALU.subtract).then_inc(m_lo_done, 1)
                    for k, slot in enumerate(slots):
                        make_lo(pool, raw4, 4 * i + k, k % 2, wlo[:, slot, :], whi[:, slot, :])

                with pool.Fori(0, NI - 1) as i:
                    round_(i, (1, 2, 3, 4))
                round_(NI - 1, [x[0] for x in FIRST_FFN])

            @block.scalar
            def _(act):
                for m in range(4):
                    act.wait_ge(o_in[m % 2], 16 * (m // 2 + 1))
                    act.activation(ohi[:, m, :], oraw[:, m % 2, :], ACT.Copy).then_inc(o_hi_done, 1)

                def prepare(i, k, slot):
                    if slot in (1, 2):
                        act.wait_ge(ac_ready, 12 * i + 6 * slot)
                    elif slot > 2:
                        act.wait_ge(dn4_ready, 18 * i + 18)
                    make_hi(act, raw4, 2 * i + k // 2 + 1, 4 * i + k, k % 2, whi[:, slot, :])

                def round_(i, slots):
                    for j in range(2):
                        for c, (c0, c1_) in enumerate(CHUNKS):
                            act.wait_ge(mix_done, 6 * i + 3 * j + c + 1)
                            if j == 0 and c == 0 and (later(i)):
                                act.wait_ge(dn4_ready, 18 * i)
                            act.activation(mhi[:, j, c0:c1_], mixa[:, (3 * j + c) % 2, 0:c1_ - c0],
                                           ACT.Copy).then_inc(m_hi_done, 1)
                    for k, slot in enumerate(slots):
                        prepare(i, k, slot)

                round_(0, (1, 2, 3, 4))
                with act.Fori(1, NI - 1) as i:
                    round_(i, (1, 2, 3, 4))
                round_(NI - 1, [x[0] for x in FIRST_FFN])

            @block.vector
            def _(dve):
                def mix(i, j, c):
                    c0, c1_ = CHUNKS[c]
                    n, b, x = c1_ - c0, (3 * j + c) * 2, (3 * j + c) % 2
                    dve.wait_ge(gch_in[c], 16 * (2 * i + j + 1))
                    dve.wait_ge(ac_ready, 12 * i + b + 1)
                    need = 6 * i + 3 * j + c - 1
                    if later(need):
                        dve.wait_ge(m_lo_done, need)
                        dve.wait_ge(mix_done, need + 1)
                    dve.scalar_tensor_tensor(out=mixc[:, x, 0:n], in0=bank[b % 4][:, 0:n],
                                             scalar=prm[:, ds(PRM_BCO + 2 * i + j, 1)], in1=gch[:, c, 1, 0:n],
                                             op0=ALU.add, op1=ALU.mult).then_inc(ac_ev, 1)
                    dve.wait_ge(ac_ready, 12 * i + b + 2)
                    dve.tensor_tensor(mixa[:, x, 0:n], bank[(b + 1) % 4][:, 0:n], gch[:, c, 0, 0:n],
                                      ALU.mult).then_inc(ac_ev, 1)
                    dve.wait_ge(ac_ev, 12 * i + b + 2)
                    dve.tensor_tensor(mixa[:, x, 0:n], mixa[:, x, 0:n], mixc[:, x, 0:n], ALU.add).then_inc(mix_done, 1)

                def round_(i):
                    for j in range(2):
                        for c in range(3):
                            mix(i, j, c)
                    if isinstance(i, int) and i == 0:
                        dve.wait_ge(x1_in, 48)
                    for d in range(18):
                        down_add(dve, d, i, dn4_ready, dn4_ev)

                round_(0)
                with dve.Fori(1, NI) as i:
                    round_(i)

            @block.tensor
            def _(pe):
                def branch_job(i, b):
                    j, c, attn = b // 6, b // 2 % 3, b % 2
                    c0, c1_ = CHUNKS[c]
                    if c == 0 and attn == 0 and (later(i)):
                        pe.wait_ge(raw4[2], 4 * i - 3 + j)
                    if b >= 4:
                        pe.wait_ge(ac_ev, 12 * i + b - 3)
                    elif later(i):
                        pe.wait_ge(ac_ev, 12 * i)
                    x_hi, x_lo = (ohi, olo) if attn else (chi, clo)
                    for k in range(4):
                        if attn and isinstance(i, int) and i == 0 and b == 1:
                            pe.wait_ge(o_lo_done, k + 1)
                        ws = slice(P * k + (0 if attn else 512), P * k + (0 if attn else 512) + P)
                        for n, (w, x) in enumerate(split_passes(whi, wlo, x_hi, x_lo)):
                            mm = pe.matmul(bank[b % 4][:, 0:c1_ - c0], w[:, 1 + j, ws], x[:, k, c0:c1_],
                                           start=(k == 0 and n == 0), stop=(k == 3 and n == 2))
                    mm.then_inc(ac_ready, 1)

                def round_(i):
                    for b in range(12):
                        branch_job(i, b)
                    slots = [(whi[:, 3 + k, :], wlo[:, 3 + k, :]) for k in range(2)]
                    for d in range(18):
                        down_job(pe, d, (mhi, mlo), slots, i, dn4_ev, dn4_ready, m_lo_done,
                                 lambda c: 6 * i + 4 + c, raw4[2], 4 * i)

                round_(0)
                with pe.Fori(1, NI) as i:
                    round_(i)

        FT = FF // P
        NF = FT // 2
        with ExitStack() as c5:
            h2hi = sb("h2hi", [P, KT, T], F32R, c5)
            h2lo = sb("h2lo", [P, KT, T], F32R, c5)
            w5hi = sb("w5hi", [P, D], F32R, c5)
            w5lo = sb("w5lo", [P, D], F32R, c5)
            gain = sb("gain", [P, D], c=c5)
            ftail = sb("ftail", [P, 4, 2 * FT], c=c5)
            ss5, sd5, rs5 = sb("ss5", [P, 2 * NT], c=c5), sb("sd5", [P, 2 * NT], c=c5), sb("rs5", [P, 2 * NT], c=c5)
            s5 = {n: sem(n) for n in ("gain_in", "ss_done", "sd5_done", "rs5_done", "xn5_done", "xt5_ready", "h2_hi", "h2_lo")}

            with ExitStack() as c5a:
                xn = sb("xn", [P, 2, D], c=c5a)
                sq5 = sb("sq5", [P, 2, D], c=c5a)
                block = c5a.enter_context(nc.Block())

                @block.sync
                def _(sp):
                    sp.dma_start(gain[:, :], a["norm2_g"][0:1, :].to_broadcast([P, D])).then_inc(s5["gain_in"], 16)
                    sp.wait_ge(s5["gain_in"], 16)

                def hi_parts5(act, t):
                    new = 64 if t == NT - 1 else 0
                    for j in range(2):
                        act.wait_ge(s5["xt5_ready"], t + 1)
                        act.activation(h2hi[:, 4 * j:4 * j + 4, TOK[t] + new:TOK[t] + P],
                                       bank[2 * (t % 2) + j][:, :].rearrange("p (k t) -> p k t", k=4)[:, :, new:],
                                       ACT.Copy).then_inc(s5["h2_hi"], 1)

                @block.scalar
                def _(act):
                    for t in range(NT):
                        if t >= 2:
                            act.wait_ge(s5["ss_done"], t - 1)
                        act.activation(sq5[:, t % 2, :], x1[:, t, :], ACT.Square,
                                       accum_out=ss5[:, t:t + 1]).then_inc(s5["ss_done"], 1)
                        act.wait_ge(s5["ss_done"], t + 1)
                        act.activation(sd5[:, t:t + 1], ss5[:, t:t + 1], ACT.Sqrt, bias=epst[:, 0:1],
                                       scale=1.0 / D).then_inc(s5["sd5_done"], 1)
                        if t:
                            hi_parts5(act, t - 1)
                    hi_parts5(act, NT - 1)

                @block.vector
                def _(dve):
                    def lo_parts5(t):
                        new = 64 if t == NT - 1 else 0
                        for j in range(2):
                            dve.wait_ge(s5["h2_hi"], 2 * t + j + 1)
                            at = slice(TOK[t] + new, TOK[t] + P)
                            dve.tensor_tensor(h2lo[:, 4 * j:4 * j + 4, at],
                                              bank[2 * (t % 2) + j][:, :].rearrange("p (k t) -> p k t", k=4)[:, :, new:],
                                              h2hi[:, 4 * j:4 * j + 4, at].bitcast(F32), ALU.subtract
                                              ).then_inc(s5["h2_lo"], 1)

                    dve.wait_ge(s5["gain_in"], 16)
                    for t in range(NT):
                        dve.wait_ge(s5["sd5_done"], t + 1)
                        dve.reciprocal(rs5[:, t:t + 1], sd5[:, t:t + 1]).then_inc(s5["rs5_done"], 1)
                        dve.wait_ge(s5["rs5_done"], t + 1)
                        if t >= 2:
                            dve.wait_ge(s5["xt5_ready"], t - 1)
                        dve.scalar_tensor_tensor(out=xn[:, t % 2, :], in0=x1[:, t, :], scalar=rs5[:, t:t + 1],
                                                 in1=gain[:, :], op0=ALU.mult, op1=ALU.mult).then_inc(s5["xn5_done"], 1)
                        if t:
                            lo_parts5(t - 1)
                    lo_parts5(NT - 1)

                @block.tensor
                def _(pe):
                    for t in range(NT):
                        pe.wait_ge(s5["xn5_done"], t + 1)
                        if t >= 2:
                            pe.wait_ge(s5["h2_lo"], 2 * (t - 1))
                        for k in range(KT):
                            mm = pe.transpose(bank[2 * (t % 2) + k // 4][:, (k % 4) * P:(k % 4 + 1) * P],
                                              xn[:, t % 2, k * P:(k + 1) * P], ident[:, :])
                        mm.then_inc(s5["xt5_ready"], 1)

            with ExitStack() as c5b:
                UPC = 2 + SEQ + 2 + DEC
                NCH = [(0, 364), (364, 728), (728, UPC - 2)]
                ghi = sb("ghi", [P, 2, T], F32R, c5b)
                glo = sb("glo", [P, 2, T], F32R, c5b)
                up = sb("up", [P, 2, UPC], c=c5b)
                cvg = sb("cvg", [P, 3, 364], c=c5b)
                cvv = sb("cvv", [P, 2, 364], c=c5b)
                gsig = sb("gsig", [P, 2, 364], c=c5b)
                raw5 = ([sem("raw5_in0"), sem("raw5_in1")], sem("hi5_done"), sem("lo5_done"))
                up_init, up_ready, up_ev, up_state, up_tail = (sem("up_init"), sem("up_ready"), sem("up_ev"),
                                                              sem("up_state"), sem("up_tail"))
                c2_done, c1_done, cv_done = sem("c2_done"), sem("c1_done"), sem("cv_done")
                gsig_done, silu_done, g_done, g_hi_done, g_lo_done = (sem("gsig_done"), sem("silu_done"), sem("g_done"),
                                                                     sem("g_hi_done"), sem("g_lo_done"))
                dn_ready, dn_ev = sem("dn_ready"), sem("dn_ev")
                y_ready, y_out, fgain_in = sem("y_ready"), [sem("y_out0"), sem("y_out1")], sem("fgain_in")
                ft_ready, ft_done, ft_out = sem("ft_ready"), sem("ft_done"), sem("ft_out")
                fss_done, fsd_done, frs_done = sem("fss_done"), sem("fsd_done"), sem("frs_done")
                w_of = [(whi[:, s, :], wlo[:, s, :]) for s in range(5)] + [(w5hi[:, :], w5lo[:, :])]
                PREP5, LAST5 = (0, 4, 5, 1, 2, 3), (4, 5)
                yst = up[:, :, 0:D]
                ysq = cvg[:, :, :].rearrange("p a n -> p (a n)")[:, 0:D]
                frow = cvv[:, :, :].rearrange("p a n -> p (a n)")[0:2 * FT, 0:4 * P].rearrange("p (w c) -> p w c", w=4)

                def pieces(c):
                    c0, c1_ = CHUNKS[c]
                    return [(c0, c1_, 0)] if c1_ <= SEQ else [(c0, SEQ, 0), (SEQ, c1_, 2)]

                def tile_at(tau, i):
                    return FT * (tau % 2) + 2 * i + tau // 2

                def steps(i, last):
                    for tau in (1, 2, 3):
                        for c in range(3):
                            yield i, tau, c
                    if not last:
                        for c in range(3):
                            yield i + 1, 0, c

                block = c5b.enter_context(nc.Block())

                @block.sync
                def _(sp):
                    def round_(i, slots):
                        for k, what in enumerate(slots):
                            send_ffn_weights(sp, raw5, 6 * i + k, k % 2, what, i if what >= 4 else i + 1)

                    sp.dma_start(gain[:, :], a["final_g"].rearrange("(a n) -> a n", a=1).to_broadcast([P, D])
                                 ).then_inc(fgain_in, 16)
                    round_(0, PREP5)
                    with sp.Fori(1, NF - 1) as i:
                        round_(i, PREP5)
                    round_(NF - 1, LAST5)
                    for t in range(NT):
                        sp.wait_ge(y_ready, t + 1)
                        if t < NT - 1:
                            sp.dma_start(o["y_prompt"][0, P * t:P * t + P, :], yst[:, t % 2, :]).then_inc(y_out[t % 2], 16)
                        else:
                            sp.dma_start(o["y_sample"][0], yst[64:P, t % 2, :]).then_inc(y_out[t % 2], 16)
                    sp.wait_ge(ft_done, 1)
                    for x, name in enumerate(("ffn_conv_prompt", "ffn_conv_sample")):
                        for r in range(2):
                            sp.dma_start(o[name][0, 0, r].rearrange("(n c) -> n c", c=P),
                                         frow[:, 2 * x + r, :]).then_inc(ft_out, 16)
                    sp.wait_ge(ft_out, 64)
                    sp.wait_ge(y_out[0], 16 * ((NT + 1) // 2))
                    sp.wait_ge(y_out[1], 16 * (NT // 2))

                @block.gpsimd
                def _(pool):
                    pool.memset(up[:, :, 0:2], 0.0).then_inc(up_init, 1)

                    def g_lo(i, j, c):
                        pool.wait_ge(g_hi_done, 6 * i + 3 * j + c + 1)
                        for x0, x1_, sh in pieces(c):
                            n0 = sh - NCH[c][0]
                            ins = pool.tensor_tensor(glo[:, j, x0:x1_], cvv[:, (3 * j + c) % 2, x0 + n0:x1_ + n0],
                                                     ghi[:, j, x0:x1_].bitcast(F32), ALU.subtract)
                        ins.then_inc(g_lo_done, 1)

                    def window(i, slots):
                        def prep(k):
                            if k < len(slots):
                                w_hi, w_lo = w_of[slots[k]]
                                make_lo(pool, raw5, 6 * i + k, k % 2, w_lo, w_hi)

                        prep(0)
                        prep(1)
                        g_lo(i, 0, 0)
                        prep(2)
                        g_lo(i, 0, 1)
                        g_lo(i, 0, 2)
                        prep(3)
                        prep(4)
                        for c in range(3):
                            g_lo(i, 1, c)
                        prep(5)

                    with pool.Fori(0, NF - 1) as i:
                        window(i, PREP5)
                    window(NF - 1, LAST5)

                @block.scalar
                def _(act):
                    def copy_up(i, tau, c):
                        c0, c1_ = CHUNKS[c]
                        x = tau % 2
                        act.wait_ge(up_ready, 12 * i + 3 * tau + c + 1)
                        need = 12 * i + 3 * (tau - 2) + min(c + 2, 3)
                        if later(i) or tau >= 2:
                            act.wait_ge(cv_done, need)
                        if c == 2 and (later(i) or tau >= 2):
                            act.wait_ge(up_tail, 8 * i + 2 * tau - 2)
                        for x0, x1_, sh in pieces(c):
                            ins = act.activation(up[:, x, x0 + sh + 2:x1_ + sh + 2],
                                                 bank[(3 * tau + c) % 4][:, x0 - c0:x1_ - c0], ACT.Copy)
                        ins.then_inc(up_ev, 1)
                        if c == 1:
                            act.activation(up[:, x, SEQ + 2:SEQ + 4], ffn_state[:, :, ds(tile_at(tau, i), 1)]
                                           .rearrange("p w a -> p (w a)"), ACT.Copy).then_inc(up_state, 1)
                        if c == 2:
                            act.wait_ge(up_ev, 12 * i + 3 * tau + 3)
                            for y, first in enumerate((SEQ, UPC - 2)):
                                act.activation(ftail[:, 2 * y:2 * y + 2, ds(tile_at(tau, i), 1)].rearrange("p w a -> p (w a)"),
                                               up[:, x, first:first + 2], ACT.Copy).then_inc(up_tail, 1)

                    def gate_sig(i, j, c):
                        n, r = NCH[c][1] - NCH[c][0], 6 * i + 3 * j + c
                        act.wait_ge(cv_done, 12 * i + 6 * j + c + 1)
                        if later(r - 1):
                            act.wait_ge(silu_done, r - 1)
                        act.activation(gsig[:, (3 * j + c) % 2, 0:n], cvg[:, c, 0:n], ACT.Sigmoid).then_inc(gsig_done, 1)

                    def g_hi(i, j, c):
                        act.wait_ge(g_done, 6 * i + 3 * j + c + 1)
                        if j == 0 and c == 0 and later(i):
                            act.wait_ge(dn_ready, 18 * i)
                        for x0, x1_, sh in pieces(c):
                            n0 = sh - NCH[c][0]
                            ins = act.activation(ghi[:, j, x0:x1_], cvv[:, (3 * j + c) % 2, x0 + n0:x1_ + n0], ACT.Copy)
                        ins.then_inc(g_hi_done, 1)

                    def gating(i, tau, c):
                        if tau % 2:
                            g_hi(i, tau // 2, c)
                        else:
                            gate_sig(i, tau // 2, c)

                    def prep(i, k, s):
                        if s < 4:
                            act.wait_ge(up_ready, 12 * i + 3 * s + 3)
                        elif later(i):
                            act.wait_ge(dn_ready, 18 * i)
                        make_hi(act, raw5, 3 * i + k // 2 + 1, 6 * i + k, k % 2, w_of[s][0])

                    PREP_AT = {(1, 0): 0, (1, 1): 1, (1, 2): 2, (2, 0): 3, (3, 0): 4, (0, 0): 5}

                    def window(i, slots, last=False):
                        before = (i, 0, 2)
                        for step in steps(i, last):
                            gating(*before)
                            copy_up(*step)
                            before = step
                            k = PREP_AT.get(step[1:], 9)
                            if k < len(slots):
                                prep(i, k, slots[k])
                        if last:
                            gating(*before)

                    act.wait_ge(up_init, 1)
                    for c in range(3):
                        if c:
                            gating(0, 0, c - 1)
                        copy_up(0, 0, c)
                    window(0, PREP5)
                    with act.Fori(1, NF - 1) as i:
                        window(i, PREP5)
                    window(NF - 1, LAST5, True)
                    act.wait_ge(g_done, 6 * NF)
                    for t in range(NT):
                        act.wait_ge(dn_ev, 18 * (NF - 1) + 2 * t + 2)
                        if t:
                            act.wait_ge(fss_done, t)
                        act.activation(ysq, x1[:, t, :], ACT.Square, accum_out=ss5[:, NT + t:NT + t + 1]).then_inc(fss_done, 1)
                        act.wait_ge(fss_done, t + 1)
                        act.activation(sd5[:, NT + t:NT + t + 1], ss5[:, NT + t:NT + t + 1], ACT.Sqrt, bias=epst[:, 0:1],
                                       scale=1.0 / D).then_inc(fsd_done, 1)
                    act.wait_ge(ft_ready, 1)
                    act.wait_ge(g_lo_done, 6 * NF)
                    act.activation(frow, bank[0][0:2 * FT, :].rearrange("p (w c) -> p w c", w=4), ACT.Copy).then_inc(ft_done, 1)

                @block.vector
                def _(dve):
                    def conv(i, tau, c):
                        n0, n1 = NCH[c]
                        n, at, r = n1 - n0, 12 * i + 3 * tau + c, 6 * i + 3 * (tau // 2) + c
                        tile = tile_at(tau, i)
                        dve.wait_ge(up_ev, at + 1)
                        if c == 2:
                            dve.wait_ge(up_state, 4 * i + tau + 1)
                        if tau % 2 == 0:
                            dst = cvg[:, c, 0:n]
                            if later(i) or tau >= 2:
                                dve.wait_ge(g_done, r - 2)
                        else:
                            dst = cvv[:, (3 * (tau // 2) + c) % 2, 0:n]
                            if later(r - 1):
                                dve.wait_ge(g_lo_done, r - 1)

                        def w(k):
                            return ffw[:, k, ds(tile, 1)]

                        src = up[:, tau % 2, :]
                        dve.tensor_scalar(dst, src[:, n0 + 2:n1 + 2], w(2), prm[:, ds(PRM_FDB + tile, 1)],
                                          ALU.mult, ALU.add).then_inc(c2_done, 1)
                        dve.wait_ge(c2_done, at + 1)
                        dve.scalar_tensor_tensor(out=dst, in0=src[:, n0 + 1:n1 + 1], scalar=w(1), in1=dst, op0=ALU.mult,
                                                 op1=ALU.add).then_inc(c1_done, 1)
                        dve.wait_ge(c1_done, at + 1)
                        dve.scalar_tensor_tensor(out=dst, in0=src[:, n0:n1], scalar=w(0), in1=dst, op0=ALU.mult,
                                                 op1=ALU.add).then_inc(cv_done, 1)

                    def silu(i, j, c):
                        n, r = NCH[c][1] - NCH[c][0], 6 * i + 3 * j + c
                        dve.wait_ge(gsig_done, r + 1)
                        dve.wait_ge(cv_done, 12 * i + 6 * j + c + 1)
                        dve.tensor_tensor(cvg[:, c, 0:n], cvg[:, c, 0:n], gsig[:, (3 * j + c) % 2, 0:n],
                                          ALU.mult).then_inc(silu_done, 1)

                    def product(i, j, c):
                        n, r, x = NCH[c][1] - NCH[c][0], 6 * i + 3 * j + c, (3 * j + c) % 2
                        dve.wait_ge(silu_done, r + 1)
                        dve.wait_ge(cv_done, 12 * i + 6 * j + 3 + c + 1)
                        dve.tensor_tensor(cvv[:, x, 0:n], cvv[:, x, 0:n], cvg[:, c, 0:n], ALU.mult).then_inc(g_done, 1)

                    def window(i, last=False):
                        before = (i, 0, 2)
                        for step in steps(i, last):
                            if before[1] % 2 == 0:
                                silu(before[0], before[1] // 2, before[2])
                            conv(*step)
                            if step[1] % 2:
                                product(step[0], step[1] // 2, step[2])
                            before = step

                    def final_norm(t):
                        dve.wait_ge(fsd_done, t + 1)
                        dve.reciprocal(rs5[:, NT + t:NT + t + 1], sd5[:, NT + t:NT + t + 1]).then_inc(frs_done, 1)
                        dve.wait_ge(frs_done, t + 1)
                        dve.wait_ge(dn_ev, 18 * (NF - 1) + 2 * t + 2)
                        if t >= 2:
                            dve.wait_ge(y_out[t % 2], 16 * (t // 2))
                        dve.scalar_tensor_tensor(out=yst[:, t % 2, :], in0=x1[:, t, :], scalar=rs5[:, NT + t:NT + t + 1],
                                                 in1=gain[:, :], op0=ALU.mult, op1=ALU.mult).then_inc(y_ready, 1)

                    for c in range(3):
                        if c:
                            silu(0, 0, c - 1)
                        conv(0, 0, c)
                    window(0)
                    for d in range(18):
                        down_add(dve, d, 0, dn_ready, dn_ev)
                    with dve.Fori(1, NF - 1) as i:
                        window(i)
                        for d in range(18):
                            down_add(dve, d, i, dn_ready, dn_ev)
                    window(NF - 1, True)
                    dve.wait_ge(cv_done, 12 * NF)
                    dve.wait_ge(up_tail, 8 * NF)
                    dve.wait_ge(fgain_in, 16)
                    for d in range(18):
                        down_add(dve, d, NF - 1, dn_ready, dn_ev)
                        if d % 2 and d >= 3:
                            final_norm(d // 2 - 1)
                    final_norm(NT - 1)

                @block.tensor
                def _(pe):
                    def up_job(i, tau, c):
                        c0, c1_ = CHUNKS[c]
                        job = 12 * i + 3 * tau + c
                        if c == 0 and later(i):
                            pe.wait_ge(raw5[2], 6 * (i - 1) + PREP5.index(tau) + 1)
                        if later(job, 4):
                            pe.wait_ge(up_ev, job - 3)
                        w_hi, w_lo = w_of[tau]
                        for k in range(KT):
                            ws = slice(P * k, P * k + P)
                            for n, (w, x) in enumerate(split_passes(w_hi, w_lo, h2hi, h2lo)):
                                mm = pe.matmul(bank[(3 * tau + c) % 4][:, 0:c1_ - c0], w[:, ws], x[:, k, c0:c1_],
                                               start=(k == 0 and n == 0), stop=(k == KT - 1 and n == 2))
                        mm.then_inc(up_ready, 1)

                    def window(i, last=False):
                        for step in steps(i, last):
                            up_job(*step)
                        slots = LAST5 if last else PREP5
                        for d in range(18):
                            down_job(pe, d, (ghi, glo), w_of[4:6], i, dn_ev, dn_ready, g_lo_done, lambda c: 6 * i + 4 + c,
                                     raw5[2], 6 * i + slots.index(5) + 1)

                    for c in range(3):
                        up_job(0, 0, c)
                    window(0)
                    with pe.Fori(1, NF - 1) as i:
                        window(i)
                    window(NF - 1, True)
                    pe.wait_ge(up_ev, 12 * NF)
                    pe.wait_ge(up_tail, 8 * NF)
                    for w in range(4):
                        mm = pe.transpose(bank[0][0:2 * FT, P * w:P * w + P], ftail[:, w, :], ident[:, :])
                    mm.then_inc(ft_ready, 1)


_INS = ["x_prompt", "x_sample", "cache_sb_k", "cache_sb_v", "state_conv", "state_ffn_conv", "norm1_g", "w_in", "b_in",
        "q_norm_g", "k_norm_g", "w_attn_out", "dw_w", "dw_b", "cn_g", "cn_b", "w_conv_out", "b_conv_out", "w_out",
        "norm2_g", "w_up", "ffn_dw_w", "ffn_dw_b", "w_down", "final_g"]
_OUTS = {
    "y_prompt": (1, SEQ, D), "y_sample": (1, DEC, D),
    "k_prompt": (1, 1, SEQ, H, DH), "v_prompt": (1, 1, SEQ, H, DH),
    "k_sample": (1, 1, DEC, H, DH), "v_sample": (1, 1, DEC, H, DH),
    "conv_prompt": (1, 1, CW - 1, CC), "conv_sample": (1, 1, CW - 1, CC),
    "ffn_conv_prompt": (1, 1, FW - 1, 2 * FF), "ffn_conv_sample": (1, 1, FW - 1, 2 * FF),
}
_SCRATCH = {"o": (PAIRS, P, T), "c": (PAIRS, P, T), "gate": (2 * KT, P, T)}


def kernel(**inputs):
    import numpy as _np
    import concourse.bacc as _bacc
    from concourse.bass_utils import run_bass_kernel_spmd as _run

    nc = _bacc.Bacc("TRN2", target_bir_lowering=False, num_devices=1)
    arrays, a = {}, {}
    for name in _INS:
        arrays[f"in_{name}"] = _np.ascontiguousarray(inputs[name])
        a[name] = nc.dram_tensor(f"in_{name}", arrays[f"in_{name}"].shape, F32, kind="ExternalInput").ap()
    o = {n: nc.dram_tensor(f"out_{n}", s, F32, kind="ExternalOutput").ap() for n, s in _OUTS.items()}
    scr = {n: nc.dram_tensor(f"scr_{n}", s, F32, kind="Internal").ap() for n, s in _SCRATCH.items()}
    build(nc, a, o, scr)
    r = _run(nc, [arrays], core_ids=[0])
    return tuple(r.results[0][f"out_{n}"] for n in _OUTS)
```

```python
from contextlib import ExitStack

import concourse.bass as bass
from concourse import mybir
from concourse.bass import ds

F32 = mybir.dt.float32
F32R = mybir.dt.float32r
BF16 = mybir.dt.bfloat16
ALU = mybir.AluOpType
ACT = mybir.ActivationFunctionType
AX_X = mybir.AxisListType.X

P = 128
D = 1024
SEQ, DEC, PAST = 1024, 64, 2048
T = SEQ + DEC
H, DH = 8, 64
AW = H * DH
CC, CW = 512, 31
FF, FW = 2816, 3
KT = D // P
NT = (T + P - 1) // P
PAIRS = H // 2
TOK = [P * t for t in range(NT - 1)] + [T - P]
CHUNKS = [(0, 364), (364, 728), (728, T)]
EPS = 1e-6
QB = 64
NB = T // QB
UCOLS = CW - 1 + T + CW - 1
U_SAMPLE = CW - 1 + SEQ
COUT = SEQ + CW - 1 + DEC
NSLOT = 5


def attention_units():
    units = []
    for i in range(NB - 1):
        keys = P * (i // 2 + 1)
        cuts = list(range(0, keys, 512)) + [keys]
        spans = list(zip(cuts[:-1], cuts[1:]))[::-1]
        for n, (a, b) in enumerate(spans):
            units.append((i, a, b - a, n == 0, n == len(spans) - 1, None, i % 2 if n == 0 else None))
    units.append((NB - 1, T - P, P, True, False, None, 2))
    for c in range(PAST // 512)[::-1]:
        units.append((NB - 1, 512 * c, 512, False, c == 0, c, None))
    return units


UNITS = attention_units()
NU = len(UNITS)
NS = NU + 4
PASTS = [u for u, x in enumerate(UNITS) if x[5] is not None]
ACT_EVACS = ["k0", "k1", "k2"]
WT_JOBS = ["k0", "k1", "k2", "q0", "q1", "q2"]
for _s in range(NS):
    if _s + 1 in PASTS:
        ACT_EVACS.append(f"past{PASTS.index(_s + 1)}")
        WT_JOBS.append(f"past{PASTS.index(_s + 1)}")
    if 0 <= _s - 2 < NU:
        ACT_EVACS.append(f"w{_s - 2}")
        WT_JOBS.append(f"w{_s - 2}")
NEV, NWT = len(ACT_EVACS), len(WT_JOBS)


def build(nc, a, o, scr):
    ctx = ExitStack()
    with ctx:
        def sb(name, shape, dt=F32, c=ctx):
            return c.enter_context(nc.sbuf_tensor(name, shape, dt))

        def sem(name):
            return ctx.enter_context(nc.semaphore(name))

        bank = [ctx.enter_context(nc.psum_tensor(f"bank{i}", [P, 512], F32)) for i in range(8)]
        ident = sb("ident", [P, P])
        identb = sb("identb", [P, P], BF16)
        maskb = sb("maskb", [P, 3, P], BF16)
        prm = sb("prm", [P, 88])
        dww = sb("dww", [P, 4, CW])
        ffw = sb("ffw", [P, FW, 44])
        epst = sb("epst", [P, 1])
        conv_state = sb("conv_state", [P, 4, CW - 1])
        ffn_state = sb("ffn_state", [P, 2, 44])
        PRM_BIN, PRM_DWB, PRM_CNG, PRM_CNB, PRM_BCO, PRM_FDB = 0, 24, 28, 32, 36, 44
        wraw = sb("wraw", [P, 2, KT * P])
        whi = sb("whi", [P, NSLOT, KT * P], F32R)
        wlo = sb("wlo", [P, NSLOT, KT * P], F32R)
        hctx = ctx.enter_context(ExitStack())
        hhi = sb("hhi", [P, KT, T], F32R, hctx)
        hlo = sb("hlo", [P, KT, T], F32R, hctx)
        w_in = a["w_in"][0].rearrange("(k p) n -> p k n", p=P)

        def gate_col(g):
            return 3 * AW + 2 * CC + D * (g % 2) + P * (g // 2)

        def gate_bias(g):
            at = PRM_BIN + 8 + KT * (g % 2) + g // 2
            return prm[:, at:at + 1]

        def later(n, least=1):
            return not isinstance(n, int) or n >= least

        def split_passes(x_hi, x_lo, y_hi, y_lo):
            return ((x_hi, y_hi), (x_hi, y_lo), (x_lo, y_hi))

        qctx = ctx.enter_context(ExitStack())
        stage = sb("stage", [P, NT, 3 * P], c=qctx)
        bqkv = sb("bqkv", [P, 3 * P], c=qctx)
        gqk = sb("gqk", [P, 2 * P], c=qctx)
        ssq = sb("ssq", [P, NT * 4], c=qctx)
        junk = sb("junk", [P, 4, DH], c=qctx)
        raw_in = [sem(f"raw_in{i}") for i in range(2)]
        hi_done, lo_done = sem("hi_done"), sem("lo_done")
        g_in2, b_in2 = sem("g_in2"), sem("b_in2")
        pj_ready, qkv_ev, stat_done = sem("pj_ready"), sem("qkv_ev"), sem("stat_done")
        b_ev, a_ev, kv_out, v_copy, wt_ready = sem("b_ev"), sem("a_ev"), sem("kv_out"), sem("v_copy"), sem("wt_ready")
        gate_ev = sem("gate_ev")
        PJ, XB = bank[0:2], bank[2:6]
        PREP_BEFORE_RAW = [0, -1, 1, 2, 3]
        RAW_USES = ((3, {0: 0, 2: 1, 4: 2}), (2, {1: 0, 3: 1}))

        def load_slot(sp, s, p, col):
            need = PREP_BEFORE_RAW[s] + 5 * p
            if later(need):
                sp.wait_ge(lo_done, need)
            sp.dma_start(wraw[:, s % 2, :].rearrange("p (k n) -> p k n", k=KT),
                         w_in[:, :, ds(col, P)]).then_inc(raw_in[s % 2], 16)

        def load_qkv(sp, s, p):
            load_slot(sp, s, p, AW * s + P * p)

        def load_ab(sp, x, p):
            load_slot(sp, 3 + x, p, 3 * AW + CC * (1 - x) + P * p)

        def load_bias(sp, p):
            sp.dma_start(bqkv[:, :].rearrange("p (x c) -> p x c", x=3),
                         a["b_in"][0, 0:3 * AW].rearrange("(x n) -> x n", x=3)[:, ds(P * p, P)]
                         .partition_broadcast(P)).then_inc(b_in2, 16)

        def slot_lo(pool, s, p):
            pool.wait_ge(hi_done, 5 * p + s + 1)
            pool.tensor_tensor(wlo[:, s, :], wraw[:, s % 2, :], whi[:, s, :].bitcast(F32),
                               ALU.subtract).then_inc(lo_done, 1)

        def slot_hi(act, s, p):
            per, at = RAW_USES[s % 2]
            act.wait_ge(raw_in[s % 2], 16 * (per * p + at[s] + 1))
            if isinstance(p, int) and p == 5:
                act.wait_ge(pj_ready, 15 * PAIRS + 3 * s + 3)
            elif later(p):
                act.wait_ge(pj_ready, 15 * p - 6 if s < 3 else 15 * p)
            act.activation(whi[:, s, :], wraw[:, s % 2, :], ACT.Copy).then_inc(hi_done, 1)

        def qkv_stats(act, p, t):
            act.wait_ge(qkv_ev, NT * p + t + 1)
            if t > 0 or later(p):
                act.wait_ge(stat_done, NT * p + t)
            for g in range(4):
                ins = act.activation(junk[:, g, :], stage[:, t, DH * g:DH * g + DH], ACT.Square,
                                     accum_out=ssq[:, 4 * t + g:4 * t + g + 1])
            ins.then_inc(stat_done, 1)

        def qkv_evac(dve, p, t):
            dve.wait_ge(pj_ready, 15 * p + t + 1)
            if t == 0:
                dve.wait_ge(b_in2, 16 * p + 16)
                if later(p):
                    dve.wait_ge(kv_out, 64 * p)
                    dve.wait_ge(v_copy, p)
                    dve.wait_ge(wt_ready, NWT * (p - 1) + 6)
            dve.tensor_tensor(stage[:, t, :], PJ[t % 2][:, 0:3 * P], bqkv[:, :], ALU.add).then_inc(qkv_ev, 1)

        def qkv_half(pe, p, t, half):
            if half == 0:
                if t == 0:
                    pe.wait_ge(lo_done, 5 * p + 3)
                if t >= 2:
                    pe.wait_ge(qkv_ev, NT * p + t - 1)
                elif later(p):
                    pe.wait_ge(a_ev, 3 * p)
                    pe.wait_ge(b_ev, 3 * p)
            tok = slice(TOK[t], TOK[t] + P)
            for k in range(4 * half, 4 * half + 4):
                ws = slice(P * k, P * k + P)
                for n, (x, w) in enumerate(split_passes(hhi, hlo, whi, wlo)):
                    mm = pe.matmul(PJ[t % 2][:, 0:3 * P], x[:, k, tok], w[:, 0:3, ws],
                                   start=(k == 0 and n == 0), stop=(k == KT - 1 and n == 2))
            if half:
                mm.then_inc(pj_ready, 1)

        with ExitStack() as c1:
            xt = sb("xt", [P, 3, D], c=c1)
            sq = sb("sq", [P, 2, D], c=c1)
            g1 = sb("g1", [P, D], c=c1)
            ss = sb("ss1", [P, NT], c=c1)
            sd = sb("sd1", [P, NT], c=c1)
            rs = sb("rs1", [P, NT], c=c1)
            prm_rows = sb("prm_rows", [88, P], c=c1)
            dww_rows = sb("dww_rows", [CW, CC], c=c1)
            ffw_rows = sb("ffw_rows", [44, FW, P], c=c1)
            fst_rows = sb("fst_rows", [44, 2, P], c=c1)
            cst_rows = sb("cst_rows", [CW - 1, CC], c=c1)
            x_in = [sem(f"x_in{i}") for i in range(3)]
            par_in, g_in = sem("par_in"), sem("g_in")
            const_done, maskf_done = sem("const_done"), sem("maskf_done")
            maskf = sb("maskf", [P, 3, P], c=c1)
            sq_done, sd_done, rs_done1 = sem("sq_done"), sem("sd_done"), sem("rs_done1")
            xn_done, xt_ready = sem("xn_done"), sem("xt_ready")
            h_hi_done, h_lo_done = sem("h_hi_done"), sem("h_lo_done")
            par_ready, par_done = sem("par_ready"), sem("par_done")

            block = c1.enter_context(nc.Block())

            @block.sync
            def _(sp):
                def load_x(t):
                    if t >= 3:
                        sp.wait_ge(xt_ready, t - 2)
                    if t < NT - 1:
                        sp.dma_start(xt[:, t % 3, :], a["x_prompt"][0, P * t:P * t + P, :]).then_inc(x_in[t % 3], 16)
                    else:
                        sp.dma_start(xt[0:64, t % 3, :], a["x_prompt"][0, SEQ - 64:SEQ, :]).then_inc(x_in[t % 3], 16)
                        sp.dma_start(xt[64:P, t % 3, :], a["x_sample"][0]).then_inc(x_in[t % 3], 16)

                load_x(0)
                load_qkv(sp, 0, 0)
                sp.dma_start(g1[:, :], a["norm1_g"][0:1, :].to_broadcast([P, D])).then_inc(g_in, 16)
                load_x(1)
                load_qkv(sp, 1, 0)
                load_x(2)
                load_bias(sp, 0)
                rows = lambda ap, n: ap.rearrange("(r c) -> r c", r=n)
                sp.dma_start(prm_rows[0:24, :], rows(a["b_in"][0, 3 * AW:], 24)).then_inc(par_in, 16)
                sp.dma_start(prm_rows[24:28, :], rows(a["dw_b"][0], 4)).then_inc(par_in, 16)
                sp.dma_start(prm_rows[28:32, :], rows(a["cn_g"][0], 4)).then_inc(par_in, 16)
                sp.dma_start(prm_rows[32:36, :], rows(a["cn_b"][0], 4)).then_inc(par_in, 16)
                sp.dma_start(prm_rows[36:44, :], rows(a["b_conv_out"][0], 8)).then_inc(par_in, 16)
                sp.dma_start(prm_rows[44:88, :], rows(a["ffn_dw_b"][0], 44)).then_inc(par_in, 16)
                sp.dma_start(dww_rows[:, :], a["dw_w"][0]).then_inc(par_in, 16)
                sp.dma_start(ffw_rows[:, :, :], a["ffn_dw_w"][0].rearrange("w (r c) -> r w c", c=P)).then_inc(par_in, 16)
                sp.dma_start(fst_rows[:, :, :], a["state_ffn_conv"][0, 0].rearrange("w (r c) -> r w c", c=P)).then_inc(par_in, 16)
                sp.dma_start(cst_rows[:, :], a["state_conv"][0, 0]).then_inc(par_in, 16)
                for t in range(3, NT):
                    load_x(t)
                    if t == 3:
                        load_qkv(sp, 2, 0)
                    elif t in (5, 6):
                        load_ab(sp, t - 5, 0)
                for x, name in enumerate(("q_norm_g", "k_norm_g")):
                    for hd in range(2):
                        sp.dma_start(gqk[:, P * x + DH * hd:P * x + DH * hd + DH],
                                     a[name][0:1, :].to_broadcast([P, DH])).then_inc(g_in2, 16)
                load_qkv(sp, 0, 1)
                load_qkv(sp, 1, 1)

            @block.gpsimd
            def _(pool):
                pool.memset(ident[:, :], 0.0).then_inc(maskf_done, 1)
                pool.memset(maskf[:, :, :], 0.0).then_inc(maskf_done, 1)
                pool.memset(epst[:, :], EPS).then_inc(maskf_done, 1)
                pool.wait_ge(maskf_done, 3)
                pool.affine_select(out=ident[:, :], in_=ident[:, :], compare_op=ALU.not_equal, fill=1.0, base=0,
                                   pattern=[[-1, P]], channel_multiplier=1).then_inc(maskf_done, 1)
                for half in range(2):
                    rows = slice(64 * half, 64 * half + 64)
                    for m, first in enumerate((0, 64, 64)):
                        pool.wait_ge(maskf_done, 4 + 3 * half + m)
                        pool.affine_select(out=maskf[rows, m, :], in_=maskf[rows, m, :], compare_op=ALU.is_gt,
                                           fill=-1e30, base=first, pattern=[[-1, P]],
                                           channel_multiplier=1).then_inc(maskf_done, 1)
                pool.wait_ge(maskf_done, 10)
                pool.memset(maskf[:, 2, 0:64], -1e30).then_inc(maskf_done, 1)
                for s in range(5):
                    slot_lo(pool, s, 0)

            def hi_parts(act, t):
                for j in range(2):
                    act.wait_ge(xt_ready, t + 1)
                    new = 64 if t == NT - 1 else 0
                    act.activation(hhi[:, 4 * j:4 * j + 4, TOK[t] + new:TOK[t] + P],
                                   XB[2 * (t % 2) + j][:, :].rearrange("p (k t) -> p k t", k=4)[:, :, new:],
                                   ACT.Copy).then_inc(h_hi_done, 1)

            @block.scalar
            def _(act):
                for t in range(NT):
                    act.wait_ge(x_in[t % 3], 16 * (t // 3 + 1 + (t == NT - 1)))
                    if t >= 2:
                        act.wait_ge(sq_done, t - 1)
                    act.activation(sq[:, t % 2, :], xt[:, t % 3, :], ACT.Square,
                                   accum_out=ss[:, t:t + 1]).then_inc(sq_done, 1)
                    act.wait_ge(sq_done, t + 1)
                    act.wait_ge(maskf_done, 3)
                    act.activation(sd[:, t:t + 1], ss[:, t:t + 1], ACT.Sqrt, bias=epst[:, 0:1],
                                   scale=1.0 / D).then_inc(sd_done, 1)
                    if t >= 1:
                        hi_parts(act, t - 1)
                    if t in (0, 1, 2, 4, 6):
                        slot_hi(act, (0, 1, 2, 4, 6).index(t), 0)
                    if t >= 4:
                        qkv_stats(act, 0, t - 4)
                hi_parts(act, NT - 1)
                for t in range(NT - 4, NT - 1):
                    qkv_stats(act, 0, t)

            @block.vector
            def _(dve):
                def lo_parts(t):
                    for j in range(2):
                        dve.wait_ge(h_hi_done, 2 * t + j + 1)
                        new = 64 if t == NT - 1 else 0
                        dve.tensor_tensor(hlo[:, 4 * j:4 * j + 4, TOK[t] + new:TOK[t] + P],
                                          XB[2 * (t % 2) + j][:, :].rearrange("p (k t) -> p k t", k=4)[:, :, new:],
                                          hhi[:, 4 * j:4 * j + 4, TOK[t] + new:TOK[t] + P].bitcast(F32),
                                          ALU.subtract).then_inc(h_lo_done, 1)

                def parameters():
                    dve.wait_ge(maskf_done, 11)
                    dve.tensor_copy(identb[:, :], ident[:, :]).then_inc(const_done, 1)
                    dve.tensor_copy(maskb[:, :, :], maskf[:, :, :]).then_inc(const_done, 1)
                    dve.wait_ge(par_ready, 1)
                    b4, b5 = bank[6], bank[7]
                    dve.tensor_copy(prm[:, :], b4[:, 0:88]).then_inc(par_done, 1)
                    dve.tensor_copy(ffw[:, :, :], b4[:, 88:220].rearrange("p (w r) -> p w r", w=3)).then_inc(par_done, 1)
                    dve.tensor_copy(ffn_state[:, :, :], b4[:, 220:308].rearrange("p (w r) -> p w r", w=2)).then_inc(par_done, 1)
                    dve.tensor_copy(dww[:, :, :], b5[:, 0:128].rearrange("p (k w) -> p k w", k=4)[:, :, 0:CW]).then_inc(par_done, 1)
                    dve.tensor_copy(conv_state[:, :, :],
                                    b5[:, 128:256].rearrange("p (k w) -> p k w", k=4)[:, :, 0:CW - 1]).then_inc(par_done, 1)

                dve.wait_ge(g_in, 16)
                for t in range(NT):
                    dve.wait_ge(sd_done, t + 1)
                    dve.reciprocal(rs[:, t:t + 1], sd[:, t:t + 1]).then_inc(rs_done1, 1)
                    dve.wait_ge(rs_done1, t + 1)
                    dve.scalar_tensor_tensor(out=xt[:, t % 3, :], in0=xt[:, t % 3, :], scalar=rs[:, t:t + 1],
                                             in1=g1[:, :], op0=ALU.mult, op1=ALU.mult).then_inc(xn_done, 1)
                    if t >= 1:
                        lo_parts(t - 1)
                    if t >= 3:
                        qkv_evac(dve, 0, t - 3)
                    if t == 6:
                        parameters()
                lo_parts(NT - 1)
                for t in range(NT - 3, NT):
                    qkv_evac(dve, 0, t)

            @block.tensor
            def _(pe):
                def parameters():
                    pe.wait_ge(par_in, 160)
                    b4, b5 = bank[6], bank[7]
                    pe.transpose(b4[:, 0:88], prm_rows[:, :], ident[0:88, 0:88])
                    for w in range(FW):
                        pe.transpose(b4[:, 88 + 44 * w:132 + 44 * w], ffw_rows[:, w, :], ident[0:44, 0:44])
                    for w in range(2):
                        pe.transpose(b4[:, 220 + 44 * w:264 + 44 * w], fst_rows[:, w, :], ident[0:44, 0:44])
                    for k in range(4):
                        pe.transpose(b5[:, 32 * k:32 * k + CW], dww_rows[:, P * k:P * k + P], ident[0:CW, 0:CW])
                        mm = pe.transpose(b5[:, 128 + 32 * k:128 + 32 * k + CW - 1], cst_rows[:, P * k:P * k + P],
                                          ident[0:CW - 1, 0:CW - 1])
                    mm.then_inc(par_ready, 1)

                pe.wait_ge(maskf_done, 4)
                for t in range(NT):
                    pe.wait_ge(xn_done, t + 1)
                    if t >= 2:
                        pe.wait_ge(h_lo_done, 2 * (t - 1))
                    for k in range(KT):
                        mm = pe.transpose(XB[2 * (t % 2) + k // 4][:, (k % 4) * P:(k % 4 + 1) * P],
                                          xt[:, t % 3, k * P:(k + 1) * P], ident[:, :])
                    mm.then_inc(xt_ready, 1)
                    if t == 4:
                        parameters()
                    if t >= 1:
                        pe.wait_ge(h_lo_done, 2 * t)
                        for half in range(2):
                            qkv_half(pe, 0, t - 1, half)
                pe.wait_ge(h_lo_done, 2 * NT)
                for half in range(2):
                    qkv_half(pe, 0, NT - 1, half)

        with ExitStack() as c2:
            vnew = sb("vnew", [P, NT, P], c=c2)
            kT = sb("kT", [P, T], c=c2)
            qz = sb("qz", [P, NB, P], c=c2)
            kpast = sb("kpast", [P, 4, 4, P], c=c2)
            kTpast = sb("kTpast", [P, 2, 512], c=c2)
            vpast = sb("vpast", [P, 2, 4, P], c=c2)
            sg = sb("sg", [P, 2, 512], c=c2)
            sn = sb("sn", [P, 2, 513], c=c2)
            run = sb("run", [P, 2, 513], c=c2)
            wT = sb("wT", [P, 2, 512], c=c2)
            o_sb = sb("o_sb", [P, T], c=c2)
            u = sb("u", [P, 2, UCOLS], c=c2)
            c_sb = sb("c_sb", [P, COUT], c=c2)
            sigb = sb("sigb", [P, 364], c=c2)
            bias_b = sb("bias_b", [P, 1], c=c2)
            sdq = sb("sdq", [P, NT * 4], c=c2)
            rsq = sb("rsq", [P, NT * 4], c=c2)
            utail = sb("utail", [P, 4, 2 * (CW - 1)], c=c2)

            init_done = sem("init_done")
            kp_in = [sem(f"kp_in{i}") for i in range(4)]
            vp_in = [sem(f"vp_in{i}") for i in range(2)]
            sdq_done, rsq_done, m1_done, norm_done = sem("sdq_done"), sem("rsq_done"), sem("m1_done"), sem("norm_done")
            gate_out2 = sem("gate_out2")
            bias_b_done = sem("bias_b_done")
            u_state, act_ev, q_ev = sem("u_state"), sem("act_ev"), sem("q_ev")
            z_ready, sig_done, scan_done, w_done = sem("z_ready"), sem("sig_done"), sem("scan_done"), sem("w_done")
            av_done, o_ev, tap_done, spill = sem("av_done"), sem("o_ev"), sem("tap_done"), sem("spill")
            tail_ready, tail_done, tail_out = sem("tail_ready"), sem("tail_done"), sem("tail_out")

            ctail = c_sb[0:CW - 1, 0:2 * CC]
            ZB, WB, OB = bank[2:4], bank[4:6], bank[6:8]
            AB_STEP = {18: 0, 19: 1, 20: 2, 21: 3, 22: 4, 24: 5, 26: 6, 28: 7, 29: 8, 30: 9, 31: 10, 32: 11}
            B_EVAC_STEP, A_EVAC_STEP = {20: 0, 25: 1, 31: 2}, {22: 0, 29: 1, 32: 2}
            NORM_STEP = {21: 0, 23: 1, 25: 2}
            TAP_STEP, _n = {}, 0
            for _s in range(3, 29):
                _k = 2 if _s < 8 else 1
                TAP_STEP[_s] = range(_n, _n + _k)
                _n += _k
            assert _n == CW
            gst2 = stage[:, :, :].rearrange("p t n -> p (t n)")[:, 0:3 * T].rearrange("p (r t) -> p r t", r=3)
            block = c2.enter_context(nc.Block())

            @block.sync
            def _(sp):
                def load_past(p, j, kv):
                    x = j if kv == "k" else j % 2
                    if kv == "k" and later(p):
                        sp.wait_ge(wt_ready, NWT * (p - 1) + WT_JOBS.index(f"past{j}") + 1)
                    elif kv == "v" and j >= 2:
                        sp.wait_ge(av_done, NU * p + PASTS[j % 2] + 1)
                    elif kv == "v" and later(p):
                        sp.wait_ge(av_done, NU * (p - 1) + PASTS[j + 2] + 1)
                    dst, cache, s_in = (kpast, "cache_sb_k", kp_in) if kv == "k" else (vpast, "cache_sb_v", vp_in)
                    src = a[cache][0, 0].rearrange("(b r) h d -> r b (h d)", r=P)
                    sp.dma_start(dst[:, x, :, :], src[:, 4 * (3 - j):4 * (3 - j) + 4, ds(P * p, P)]
                                 ).then_inc(s_in[x], 16)

                def store_kv(p):
                    sp.wait_ge(norm_done, 3 * p + 3)
                    for x, name in ((1, "k"), (2, "v")):
                        dst = o[f"{name}_prompt"][0, 0].rearrange("(t r) h d -> r t (h d)", r=P)
                        sp.dma_start(dst[:, :, ds(P * p, P)], stage[:, 0:NT - 1, P * x:P * x + P]).then_inc(kv_out, 16)
                        dst = o[f"{name}_sample"][0, 0].rearrange("t h d -> t (h d)")
                        sp.dma_start(dst[:, ds(P * p, P)], stage[64:P, NT - 1, P * x:P * x + P]).then_inc(kv_out, 16)

                def store_oc(p):
                    sp.wait_ge(tap_done, CW * p + CW)
                    dst = scr["c"][ds(p, 1)].rearrange("a p t -> (a p) t")
                    sp.dma_start(dst[:, 0:SEQ], c_sb[:, 0:SEQ]).then_inc(spill, 16)
                    sp.dma_start(dst[:, SEQ:T], c_sb[:, U_SAMPLE:COUT]).then_inc(spill, 16)
                    sp.wait_ge(o_ev, 5 * p + 5)
                    sp.dma_start(scr["o"][ds(p, 1)].rearrange("a p t -> (a p) t"), o_sb[:, :]).then_inc(spill, 16)

                def window(p):
                    load_bias(sp, p + 1)
                    for x in range(2):
                        load_ab(sp, x, p + 1)
                    for j in range(4):
                        load_past(p, j, "k")
                    for j in range(2):
                        load_past(p, j, "v")
                    for s in range(3):
                        if p < PAIRS - 2:
                            load_qkv(sp, s, p + 2)
                        else:
                            load_slot(sp, s, 4, gate_col(s))
                    store_kv(p + 1)
                    for j in (2, 3):
                        load_past(p, j, "v")
                    store_oc(p)

                def last_window():
                    for s in (3, 4):
                        load_slot(sp, s, 4, gate_col(s))
                    for j in range(4):
                        load_past(3, j, "k")
                    for j in range(2):
                        load_past(3, j, "v")
                    for g in range(5):
                        load_slot(sp, g, 5, gate_col(5 + g))
                        if g == 4:
                            for j in (2, 3):
                                load_past(3, j, "v")
                        sp.wait_ge(gate_ev, 3 * g + 3)
                        sp.dma_start(scr["gate"][g], gst2[:, g % 3, :]).then_inc(gate_out2, 16)
                    store_oc(3)

                load_qkv(sp, 2, 1)
                store_kv(0)
                for p in range(PAIRS - 1):
                    window(p)
                last_window()
                sp.wait_ge(gate_out2, 16 * 5)
                sp.wait_ge(kv_out, 64 * PAIRS)
                sp.wait_ge(spill, 48 * PAIRS)
                sp.wait_ge(tail_done, 2)
                sp.dma_start(o["conv_prompt"][0, 0], ctail[:, 0:CC]).then_inc(tail_out, 16)
                sp.dma_start(o["conv_sample"][0, 0], ctail[:, CC:2 * CC]).then_inc(tail_out, 16)
                sp.wait_ge(tail_out, 32)

            @block.gpsimd
            def _(pool):
                pool.memset(qz[:, :, :], 0.0).then_inc(init_done, 1)
                pool.memset(sn[:, :, 512:513], 1.0).then_inc(init_done, 1)
                pool.memset(u[:, :, 0:CW - 1], 0.0).then_inc(init_done, 1)
                for s in range(3):
                    slot_lo(pool, s, 1)
                with pool.Fori(0, 3) as p:
                    for s in (3, 4):
                        slot_lo(pool, s, p + 1)
                    for s in range(3):
                        slot_lo(pool, s, p + 2)
                for s in (3, 4):
                    slot_lo(pool, s, 4)
                for s in range(5):
                    slot_lo(pool, s, 5)

            @block.scalar
            def _(act):
                def b_evac(p, c):
                    c0, c1_ = CHUNKS[c]
                    act.wait_ge(pj_ready, 15 * p + 10 + 2 * c)
                    need = 3 * p + c
                    if later(need):
                        act.wait_ge(a_ev, need)
                    act.wait_ge(bias_b_done, p + 1)
                    act.activation(sigb[:, 0:c1_ - c0], PJ[(9 + 2 * c) % 2][:, 0:c1_ - c0], ACT.Sigmoid,
                                   bias=bias_b[:, :]).then_inc(b_ev, 1)

                def state(p):
                    if later(p, 2):
                        act.wait_ge(tap_done, CW * (p - 1))
                    act.activation(u[:, ds(p % 2, 1), U_SAMPLE:U_SAMPLE + CW - 1].rearrange("p a t -> p (a t)"),
                                   conv_state[:, ds(p, 1), :].rearrange("p a t -> p (a t)"), ACT.Copy).then_inc(u_state, 1)

                def tails(p):
                    act.wait_ge(a_ev, 3 * p + 3)
                    act.wait_ge(u_state, 3 * p + 1)
                    for x, first in enumerate((SEQ, UCOLS - (CW - 1))):
                        act.activation(utail[:, ds(p, 1), (CW - 1) * x:(CW - 1) * (x + 1)].rearrange("p a t -> p (a t)"),
                                       u[:, ds(p % 2, 1), first:first + CW - 1].rearrange("p a t -> p (a t)"),
                                       ACT.Copy).then_inc(u_state, 1)

                def roots(p):
                    act.wait_ge(stat_done, NT * p + NT)
                    act.activation(sdq[:, :], ssq[:, :], ACT.Sqrt, bias=epst[:, 0:1], scale=1.0 / DH).then_inc(sdq_done, 1)

                def copy_v(p):
                    act.wait_ge(qkv_ev, NT * p + NT)
                    if later(p):
                        act.wait_ge(av_done, NU * (p - 1) + PASTS[0])
                    act.activation(vnew[:, :, :], stage[:, :, 2 * P:3 * P], ACT.Copy).then_inc(v_copy, 1)

                def k_evac(p, j):
                    act.wait_ge(wt_ready, NWT * p + j + 1)
                    if later(p):
                        act.wait_ge(z_ready, NU * p)
                    t0, b0, n = (512 * j, 0, 512) if j < 2 else (SEQ, P - DEC, DEC)
                    act.activation(kT[:, t0:t0 + n], WB[j % 2][:, b0:b0 + n], ACT.Copy).then_inc(act_ev, 1)

                def sig(p, s):
                    n = UNITS[s][2]
                    act.wait_ge(z_ready, NU * p + s + 1)
                    if s >= 2:
                        act.wait_ge(wt_ready, NWT * p + WT_JOBS.index(f"w{s - 2}") + 1)
                    z = ZB[s % 2][:, 0:n]
                    act.activation(sn[:, s % 2, 512 - n:512], z, ACT.Sigmoid, scale=-DH ** -0.5)
                    act.activation(sg[:, s % 2, 0:n], z, ACT.Sigmoid, scale=DH ** -0.5).then_inc(sig_done, 1)

                def w_evac(p, s):
                    n = UNITS[s][2]
                    act.wait_ge(wt_ready, NWT * p + WT_JOBS.index(f"w{s}") + 1)
                    need = NU * p + s - 1
                    if later(need):
                        act.wait_ge(av_done, need if s >= 1 else NU * p)
                    act.activation(wT[:, s % 2, 0:n], WB[WT_JOBS.index(f"w{s}") % 2][:, 0:n], ACT.Copy).then_inc(act_ev, 1)

                def past_evac(p, j):
                    n = WT_JOBS.index(f"past{j}")
                    act.wait_ge(wt_ready, NWT * p + n + 1)
                    if j >= 2:
                        act.wait_ge(z_ready, NU * p + PASTS[j - 2] + 1)
                    act.activation(kTpast[:, j % 2, :], WB[n % 2][:, :], ACT.Copy).then_inc(act_ev, 1)

                def o_evac(p, g):
                    last = max(x for x in range(NU) if UNITS[x][0] // 4 == g)
                    nb = 4 if g < 4 else 1
                    act.wait_ge(av_done, NU * p + last + 1)
                    if g == 0 and (later(p)):
                        act.wait_ge(spill, 48 * p)
                    for hd in range(2):
                        r = slice(DH * hd, DH * hd + DH)
                        ins = act.activation(o_sb[r, 256 * g:256 * g + QB * nb].rearrange("p (b q) -> p b q", b=nb),
                                             OB[g % 2][r, 0:P * nb].rearrange("p (b q) -> p b q", b=nb)
                                             [:, :, QB * hd:QB * hd + QB], ACT.Copy)
                    ins.then_inc(o_ev, 1)

                def gate_evac(n):
                    g, c = n // 3, n % 3
                    c0, c1_ = CHUNKS[c]
                    act.wait_ge(pj_ready, 15 * PAIRS + n + 1)
                    if n == 0:
                        act.wait_ge(kv_out, 64 * PAIRS)
                        act.wait_ge(v_copy, PAIRS)
                        act.wait_ge(wt_ready, NWT * (PAIRS - 1) + 6)
                    if c == 0 and g >= 3:
                        act.wait_ge(gate_out2, 16 * (g - 2))
                    act.activation(gst2[:, g % 3, c0:c1_], PJ[n % 2][:, 0:c1_ - c0], ACT.Sigmoid,
                                   bias=gate_bias(g)).then_inc(gate_ev, 1)

                def attention(p, s):
                    if s + 1 in PASTS:
                        past_evac(p, PASTS.index(s + 1))
                    if s < NU:
                        sig(p, s)
                    if 0 <= s - 2 < NU:
                        w_evac(p, s - 2)
                    if s >= 4 and UNITS[s - 4][4] and (UNITS[s - 4][0] % 4 == 3 or UNITS[s - 4][0] == NB - 1):
                        o_evac(p, UNITS[s - 4][0] // 4)
                    if s == 1:
                        tails(p)

                def window(p):
                    for s in range(NS):
                        attention(p, s)
                        if s in (1, 3):
                            slot_hi(act, 3 + s // 2, p + 1)
                        if s >= 3 and s % 2 == 1 and (s - 3) // 2 < NT:
                            qkv_stats(act, p + 1, (s - 3) // 2)
                        if s == 20:
                            roots(p + 1)
                        if s in B_EVAC_STEP:
                            b_evac(p + 1, B_EVAC_STEP[s])
                        if s in (21, 22, 23):
                            slot_hi(act, s - 21, p + 2)
                        if s == 26:
                            state(p + 1)
                        if s == 29:
                            copy_v(p + 1)
                        if s == 30:
                            k_evac(p + 1, 0)
                        if s == 31:
                            k_evac(p + 1, 1)
                            k_evac(p + 1, 2)

                def last_window():
                    for s in range(NS):
                        attention(3, s)
                        if s in (1, 3):
                            slot_hi(act, 3 + s // 2, 4)
                        if s >= 2 and s % 2 == 0 and (s - 2) // 2 < 15:
                            gate_evac((s - 2) // 2)
                        if s in (8, 14, 20, 26, 31):
                            slot_hi(act, (8, 14, 20, 26, 31).index(s), 5)

                act.wait_ge(init_done, 3)
                qkv_stats(act, 0, NT - 1)
                roots(0)
                for s in range(2):
                    slot_hi(act, s, 1)
                b_evac(0, 0)
                copy_v(0)
                for j in range(3):
                    k_evac(0, j)
                slot_hi(act, 2, 1)
                b_evac(0, 1)
                state(0)
                b_evac(0, 2)
                window(0)
                with act.Fori(1, PAIRS - 1) as p:
                    window(p)
                last_window()
                for x in range(2):
                    act.wait_ge(tail_ready, 1)
                    act.wait_ge(spill, 48 * PAIRS)
                    act.activation(ctail[:, CC * x:CC * x + CC], WB[x][0:CW - 1, :], ACT.Copy).then_inc(tail_done, 1)

            @block.vector
            def _(dve):
                def next_bias(p):
                    if later(p):
                        dve.wait_ge(b_ev, 3 * p)
                    bias = prm[:, ds(PRM_BIN + 4 + p, 1)]
                    dve.tensor_tensor(bias_b[:, :], bias, bias, ALU.max).then_inc(bias_b_done, 1)

                def a_evac(p, c):
                    c0, c1_ = CHUNKS[c]
                    dve.wait_ge(pj_ready, 15 * p + 11 + 2 * c)
                    dve.wait_ge(b_ev, 3 * p + c + 1)
                    if c == 0 and later(p, 2):
                        dve.wait_ge(u_state, 3 * (p - 1))
                        dve.wait_ge(tap_done, CW * (p - 1))
                    bias = prm[:, ds(PRM_BIN + p, 1)]
                    parts = [(c0, c1_)] if c1_ <= SEQ else [(c0, SEQ), (SEQ, c1_)]
                    for x0, x1 in parts:
                        at = x0 + (CW - 1 if x0 < SEQ else 2 * (CW - 1))
                        ins = dve.scalar_tensor_tensor(
                            out=u[:, ds(p % 2, 1), at:at + x1 - x0].rearrange("p a t -> p (a t)"),
                            in0=PJ[(10 + 2 * c) % 2][:, x0 - c0:x1 - c0], scalar=bias, in1=sigb[:, x0 - c0:x1 - c0],
                            op0=ALU.add, op1=ALU.mult)
                    ins.then_inc(a_ev, 1)

                def tap(p, k):
                    if k == 0:
                        dve.wait_ge(a_ev, 3 * p + 3)
                        dve.wait_ge(u_state, 3 * p + 1)
                        if later(p):
                            dve.wait_ge(spill, 48 * p)
                    x = u[:, ds(p % 2, 1), k:k + COUT].rearrange("p a t -> p (a t)")
                    w = dww[:, ds(p, 1), k:k + 1].rearrange("p a t -> p (a t)")
                    if k == 0:
                        dve.tensor_scalar(c_sb[:, :], x, w, prm[:, ds(PRM_DWB + p, 1)], ALU.mult, ALU.add).then_inc(tap_done, 1)
                    else:
                        dve.wait_ge(tap_done, CW * p + k)
                        dve.scalar_tensor_tensor(out=c_sb[:, :], in0=x, scalar=w, in1=c_sb[:, :], op0=ALU.mult,
                                                 op1=ALU.add).then_inc(tap_done, 1)

                def norm(p, third):
                    if third == 0:
                        dve.wait_ge(sdq_done, p + 1)
                        if later(p):
                            dve.wait_ge(m1_done, 3 * p)
                        dve.reciprocal(rsq[:, :], sdq[:, :]).then_inc(rsq_done, 1)
                        dve.wait_ge(rsq_done, p + 1)
                        dve.wait_ge(qkv_ev, NT * p + NT)
                        if isinstance(p, int) and p == 0:
                            dve.wait_ge(g_in2, 64)
                    t0 = 3 * third
                    x = stage[:, t0:t0 + 3, 0:2 * P].rearrange("p t (g d) -> p t g d", d=DH)
                    dve.tensor_tensor(x, x, rsq[:, 4 * t0:4 * t0 + 12].rearrange("p (t g) -> p t g", g=4).unsqueeze(3)
                                      .to_broadcast([P, 3, 4, DH]), ALU.mult).then_inc(m1_done, 1)
                    dve.wait_ge(m1_done, 3 * p + third + 1)
                    y = stage[:, t0:t0 + 3, 0:2 * P]
                    dve.tensor_tensor(y, y, gqk[:, :].unsqueeze(1).to_broadcast([P, 3, 2 * P]), ALU.mult).then_inc(norm_done, 1)

                def q_evac(p, j):
                    dve.wait_ge(wt_ready, NWT * p + 4 + j)
                    if later(p):
                        dve.wait_ge(z_ready, NU * p)
                    b = WB[(3 + j) % 2]
                    for hd in range(2):
                        r = slice(DH * hd, DH * hd + DH)
                        if j < 2:
                            out = qz[r, 8 * j:8 * j + 8, QB * hd:QB * hd + QB]
                            src = b[r, :].rearrange("p (b q) -> p b q", b=8)
                        else:
                            out, src = qz[r, NB - 1, QB * hd:QB * hd + QB], b[r, 64:P]
                        ins = dve.tensor_copy(out, src)
                    ins.then_inc(q_ev, 1)

                def weights(p, s):
                    n, first = UNITS[s][2], UNITS[s][3]
                    dve.wait_ge(sig_done, NU * p + s + 1)
                    x = sn[:, s % 2, 512 - n:513][:, ::-1]
                    if s >= 2 or later(p):
                        dve.wait_ge(w_done, NU * p + max(s - 1, 0))
                    init = 1.0 if first else run[:, (s - 1) % 2, 512 - UNITS[s - 1][2]:513 - UNITS[s - 1][2]]
                    dve.tensor_tensor_scan(run[:, s % 2, 512 - n:513][:, ::-1], x, x, init, ALU.mult,
                                           ALU.min).then_inc(scan_done, 1)
                    dve.wait_ge(scan_done, NU * p + s + 1)
                    dve.tensor_tensor(sg[:, s % 2, 0:n], sg[:, s % 2, 0:n], run[:, s % 2, 513 - n:513],
                                      ALU.mult).then_inc(w_done, 1)

                def attention(p, s):
                    if s < NU:
                        weights(p, s)
                    for k in TAP_STEP.get(s, ()):
                        tap(p, k)

                def window(p):
                    for s in range(NS):
                        attention(p, s)
                        if s == 0:
                            next_bias(p + 1)
                        if s >= 2 and s % 2 == 0 and (s - 2) // 2 < NT:
                            qkv_evac(dve, p + 1, (s - 2) // 2)
                        if s in NORM_STEP:
                            norm(p + 1, NORM_STEP[s])
                        if s == 31:
                            q_evac(p + 1, 0)
                        if s == 32:
                            q_evac(p + 1, 1)
                            q_evac(p + 1, 2)
                        if s in A_EVAC_STEP:
                            a_evac(p + 1, A_EVAC_STEP[s])

                dve.wait_ge(init_done, 3)
                next_bias(0)
                for third in range(3):
                    norm(0, third)
                a_evac(0, 0)
                a_evac(0, 1)
                for j in range(3):
                    q_evac(0, j)
                a_evac(0, 2)
                window(0)
                with dve.Fori(1, PAIRS - 1) as p:
                    window(p)
                for s in range(NS):
                    attention(3, s)

            @block.tensor
            def _(pe):
                def free(n, p):
                    if n < 2:
                        if later(p):
                            pe.wait_ge(act_ev, NEV * p)
                        return
                    job = WT_JOBS[n - 2]
                    if job[0] == "q":
                        pe.wait_ge(q_ev, 3 * p + int(job[1:]) + 1)
                    else:
                        pe.wait_ge(act_ev, NEV * p + ACT_EVACS.index(job) + 1)

                def ab_half(p, n, half):
                    if half == 0:
                        if n == 0:
                            pe.wait_ge(lo_done, 5 * p + 5)
                        if n < 2:
                            pe.wait_ge(qkv_ev, NT * p + 8 + n)
                        elif n % 2 == 0:
                            pe.wait_ge(b_ev, 3 * p + n // 2)
                        else:
                            pe.wait_ge(a_ev, 3 * p + n // 2)
                    c0, c1_ = CHUNKS[n // 2]
                    slot = 3 + n % 2
                    for k in range(4 * half, 4 * half + 4):
                        ws = slice(P * k, P * k + P)
                        for i, (w, x) in enumerate(split_passes(whi, wlo, hhi, hlo)):
                            mm = pe.matmul(PJ[(9 + n) % 2][:, 0:c1_ - c0], w[:, slot, ws], x[:, k, c0:c1_],
                                           start=(k == 0 and i == 0), stop=(k == KT - 1 and i == 2))
                    if half:
                        mm.then_inc(pj_ready, 1)

                def qk_transposes(p, n):
                    if n == 0:
                        pe.wait_ge(norm_done, 3 * p + 3)
                    free(n, p)
                    x, j = 1 - n // 3, n % 3
                    tiles = range(4 * j, 4 * j + 4) if j < 2 else [NT - 1]
                    for i, t in enumerate(tiles):
                        mm = pe.transpose(WB[n % 2][:, P * i:P * i + P], stage[:, t, P * x:P * x + P], ident[:, :])
                    mm.then_inc(wt_ready, 1)

                def gate_half(n, half):
                    g, c = n // 3, n % 3
                    c0, c1_ = CHUNKS[c]
                    if half == 0:
                        if c == 0:
                            pe.wait_ge(lo_done, 5 * 4 + g + 1)
                        if n < 2:
                            pe.wait_ge(a_ev, 3 * PAIRS)
                            pe.wait_ge(b_ev, 3 * PAIRS)
                        else:
                            pe.wait_ge(gate_ev, n - 1)
                    for k in range(4 * half, 4 * half + 4):
                        ws = slice(P * k, P * k + P)
                        for i, (w, x) in enumerate(split_passes(whi, wlo, hhi, hlo)):
                            mm = pe.matmul(PJ[n % 2][:, 0:c1_ - c0], w[:, g, ws], x[:, k, c0:c1_],
                                           start=(k == 0 and i == 0), stop=(k == KT - 1 and i == 2))
                    if half:
                        mm.then_inc(pj_ready, 1)

                def past_transposes(p, j):
                    n = WT_JOBS.index(f"past{j}")
                    free(n, p)
                    pe.wait_ge(kp_in[j], 16 * (p + 1))
                    for b in range(4):
                        mm = pe.transpose(WB[n % 2][:, P * b:P * b + P], kpast[:, j, b, :], ident[:, :])
                    mm.then_inc(wt_ready, 1)

                def scores(p, s):
                    i, k0, n, first, last, past, mask = UNITS[s]
                    if s >= 2:
                        pe.wait_ge(sig_done, NU * p + s - 1)
                    elif later(p):
                        pe.wait_ge(sig_done, NU * p)
                    if s == 0:
                        pe.wait_ge(act_ev, NEV * p + 3)
                        pe.wait_ge(q_ev, 3 * p + 3)
                    if past is None:
                        keys = kT[:, k0:k0 + n]
                    else:
                        j = PASTS.index(s)
                        pe.wait_ge(act_ev, NEV * p + ACT_EVACS.index(f"past{j}") + 1)
                        keys = kTpast[:, j % 2, :]
                    mm = pe.matmul(ZB[s % 2][:, 0:n], qz[:, i, :], keys, start=True, stop=True)
                    if mask is not None:
                        mm = pe.matmul(ZB[s % 2][:, n - P:n], identb[:, :], maskb[:, mask, :], start=False, stop=True,
                                       skip_group_check=True)
                    mm.then_inc(z_ready, 1)

                def w_transposes(p, s):
                    n = WT_JOBS.index(f"w{s}")
                    free(n, p)
                    pe.wait_ge(w_done, NU * p + s + 1)
                    for b in range(UNITS[s][2] // P):
                        mm = pe.transpose(WB[n % 2][:, P * b:P * b + P], sg[:, s % 2, P * b:P * b + P], ident[:, :])
                    mm.then_inc(wt_ready, 1)

                def outputs(p, s):
                    i, k0, n, first, last, past, mask = UNITS[s]
                    g = i // 4
                    pe.wait_ge(act_ev, NEV * p + ACT_EVACS.index(f"w{s}") + 1)
                    if s == 0:
                        pe.wait_ge(v_copy, p + 1)
                    if past is not None:
                        j = PASTS.index(s)
                        pe.wait_ge(vp_in[j % 2], 16 * (2 * p + j // 2 + 1))
                    if i % 4 == 0 and first:
                        need = 5 * p + max(g - 1, 0)
                        if later(need):
                            pe.wait_ge(o_ev, need)
                    nb = n // P
                    for b in range(nb):
                        if past is not None:
                            v = vpast[:, PASTS.index(s) % 2, b, :]
                        else:
                            v = vnew[:, k0 // P + b if k0 < T - P else NT - 1, :]
                        mm = pe.matmul(OB[g % 2][:, P * (i % 4):P * (i % 4) + P], v, wT[:, s % 2, P * b:P * b + P],
                                       start=(first and b == 0), stop=(last and b == nb - 1))
                    mm.then_inc(av_done, 1)

                def window(p, last=False):
                    for s in range(NS):
                        if s + 1 in PASTS:
                            past_transposes(p, PASTS.index(s + 1))
                        if s < NU:
                            scores(p, s)
                        if 0 <= s - 2 < NU:
                            w_transposes(p, s - 2)
                        if not last and s in (NS - 3, NS - 2, NS - 1):
                            qk_transposes(p + 1, 2 * (s - NS + 3))
                        if 0 <= s - 3 < NU:
                            outputs(p, s - 3)
                        if last:
                            if s < 30:
                                gate_half(s // 2, s % 2)
                        elif s < 18:
                            qkv_half(pe, p + 1, s // 2, s % 2)
                        elif s in AB_STEP:
                            ab_half(p + 1, AB_STEP[s] // 2, AB_STEP[s] % 2)
                        if not last and s in (NS - 3, NS - 2, NS - 1):
                            qk_transposes(p + 1, 2 * (s - NS + 3) + 1)

                pe.wait_ge(init_done, 3)
                for n in range(3):
                    for h in range(4):
                        ab_half(0, 2 * n + h // 2, h % 2)
                    if n < 2:
                        for x in range(3):
                            qk_transposes(0, 3 * n + x)
                window(0)
                with pe.Fori(1, PAIRS - 1) as p:
                    window(p)
                window(3, True)
                pe.wait_ge(act_ev, NEV * PAIRS)
                pe.wait_ge(u_state, 3 * PAIRS)
                for x in range(2):
                    for m in range(4):
                        mm = pe.transpose(WB[x][0:CW - 1, P * m:P * m + P],
                                          utail[:, m, (CW - 1) * x:(CW - 1) * (x + 1)], ident[:, :])
                mm.then_inc(tail_ready, 1)

        qctx.close()

        c_bytes = 4 * 4 * T
        top = nc.sbuf_usable_end

        def pinned(name, nth):
            return nc.alloc_sbuf_tensor_at(name, [P, 4, T], F32R, offset=(top - (nth + 1) * c_bytes) // 32 * 32)

        NG = 2 * KT
        FIRST_FFN = [(0, 0), (1, 1), (2, 2), (3, 3)]
        w_out = a["w_out"][0].rearrange("(k p) n -> p k n", p=P)
        w_up = a["w_up"][0].rearrange("(k p) n -> p k n", p=P)
        w_down = a["w_down"][0].rearrange("(k p) n -> p k n", p=P)
        w_ac = [a["w_attn_out"][0].rearrange("(k p) n -> p k n", p=P), a["w_conv_out"][0].rearrange("(k p) n -> p k n", p=P)]

        def send_raw(sp, sems, n, parity, halves):
            if later(n, 2):
                sp.wait_ge(sems[2], n - 1)
            for h, src in enumerate(halves):
                dst = wraw[:, parity, 512 * h:512 * h + 512]
                if len(src.shape) == 3:
                    dst = dst.rearrange("p (k n) -> p k n", n=P)
                sp.dma_start(dst, src).then_inc(sems[0][parity], 16)

        def k_halves(w, col):
            return [w[:, 0:4, ds(col, P)], w[:, 4:8, ds(col, P)]]

        def send_out_weights(sp, sems, n, parity, k, i):
            if k < 2:
                send_raw(sp, sems, n, parity, [w[:, :, ds(P * (2 * i + k), P)] for w in w_ac])
            else:
                rows = w_out[:, ds(2 * i + k - 2, 1), :].rearrange("p k n -> p (k n)")
                send_raw(sp, sems, n, parity, [rows[:, 0:512], rows[:, 512:D]])

        def send_ffn_weights(sp, sems, n, parity, what, i):
            if what < 4:
                send_raw(sp, sems, n, parity, k_halves(w_up, FF * (what % 2) + P * (2 * i + what // 2)))
            else:
                rows = w_down[:, ds(2 * i + what - 4, 1), :].rearrange("p k n -> p (k n)")
                send_raw(sp, sems, n, parity, [rows[:, 0:512], rows[:, 512:D]])

        def make_hi(act, sems, raw_count, n, parity, dst):
            act.wait_ge(sems[0][parity], 32 * raw_count)
            act.activation(dst, wraw[:, parity, :], ACT.Copy).then_inc(sems[1], 1)

        def make_lo(pool, sems, n, parity, dst, hi):
            pool.wait_ge(sems[1], n + 1)
            pool.tensor_tensor(dst, wraw[:, parity, :], hi.bitcast(F32), ALU.subtract).then_inc(sems[2], 1)

        with ExitStack() as c3:
            chi, clo = pinned("chi", 0), pinned("clo", 1)
            craw = sb("craw", [P, 4, T], c=c3)
            gst = sb("gst", [P, 2, T], c=c3)
            csq = sb("csq", [P, 4, 364], c=c3)
            csig = sb("csig", [P, 4, 364], c=c3)
            crs = sb("crs", [P, T], c=c3)
            ones = sb("ones", [P, P], c=c3)
            raw3 = ([sem("raw3_in0"), sem("raw3_in1")], sem("hi3_done"), sem("lo3_done"))
            c_in, ones_done, g_ready, g_ev = sem("c_in"), sem("ones_done"), sem("g_ready"), sem("g_ev")
            gate_out = [sem("gate_out0"), sem("gate_out1")]
            mean_ready, xc_done, csq_done, var_ready = sem("mean_ready"), sem("xc_done"), sem("csq_done"), sem("var_ready")
            csd_done, crs_done, cn_done, csig_done = sem("csd_done"), sem("crs_done"), sem("cn_done"), sem("csig_done")
            caff_done, cact_done, chi_done, clo_done = sem("caff_done"), sem("cact_done"), sem("chi_done"), sem("clo_done")
            PREP3 = [(g % 5, 3 * (g - 9)) for g in range(10, NG)] + [(1, 21), (2, 24), (3, 27), (4, 30)]
            block = c3.enter_context(nc.Block())

            @block.sync
            def _(sp):
                for m in range(4):
                    sp.dma_start(craw[:, m, :], scr["c"][m]).then_inc(c_in, 16)
                n = 0
                for g in range(NG - 5):
                    while n < len(PREP3) and n < g + 3:
                        if n < NG - 10:
                            send_raw(sp, raw3, n, n % 2, k_halves(w_in, gate_col(10 + n)))
                        else:
                            send_out_weights(sp, raw3, n, n % 2, n - (NG - 10), 0)
                        n += 1
                    sp.wait_ge(g_ev, 3 * g + 3)
                    sp.dma_start(scr["gate"][g + 5], gst[:, g % 2, :]).then_inc(gate_out[g % 2], 16)
                sp.wait_ge(gate_out[0], 16 * 6)
                sp.wait_ge(gate_out[1], 16 * 5)

            @block.gpsimd
            def _(pool):
                pool.memset(ones[:, :], 1.0 / CC).then_inc(ones_done, 1)

                def c_lo(c):
                    c0, c1_ = CHUNKS[c]
                    pool.wait_ge(chi_done, c + 1)
                    pool.tensor_tensor(clo[:, :, c0:c1_], craw[:, :, c0:c1_], chi[:, :, c0:c1_].bitcast(F32),
                                       ALU.subtract).then_inc(clo_done, 1)

                for n, (slot, _need) in enumerate(PREP3):
                    make_lo(pool, raw3, n, n % 2, wlo[:, slot, :], whi[:, slot, :])
                    if n in (6, 7, 8):
                        c_lo(n - 6)

            @block.scalar
            def _(act):
                def gate_evac(j):
                    g, c = j // 3, j % 3
                    c0, c1_ = CHUNKS[c]
                    act.wait_ge(g_ready, j + 1)
                    if c == 0 and g >= 2:
                        act.wait_ge(gate_out[g % 2], 16 * (g // 2))
                    act.activation(gst[:, g % 2, c0:c1_], bank[j % 4][:, 0:c1_ - c0], ACT.Sigmoid,
                                   bias=gate_bias(g + 5)).then_inc(g_ev, 1)

                def squares(c):
                    c0, c1_ = CHUNKS[c]
                    act.wait_ge(xc_done, c + 1)
                    if c:
                        act.wait_ge(var_ready, c)
                    act.activation(csq[:, :, 0:c1_ - c0], craw[:, :, c0:c1_], ACT.Square).then_inc(csq_done, 1)

                def roots():
                    for c, (c0, c1_) in enumerate(CHUNKS):
                        act.wait_ge(var_ready, c + 1)
                        act.activation(crs[:, c0:c1_], bank[4 + c][:, 0:c1_ - c0], ACT.Sqrt,
                                       bias=epst[:, 0:1]).then_inc(csd_done, 1)

                def sigmoids(c):
                    c0, c1_ = CHUNKS[c]
                    act.wait_ge(cn_done, c + 1)
                    if c:
                        act.wait_ge(cact_done, c)
                    for m in range(4):
                        ins = act.activation(csig[:, m, 0:c1_ - c0], craw[:, m, c0:c1_], ACT.Sigmoid,
                                             scale=prm[:, PRM_CNG + m:PRM_CNG + m + 1],
                                             bias=prm[:, PRM_CNB + m:PRM_CNB + m + 1])
                    ins.then_inc(csig_done, 1)

                def c_hi(c):
                    c0, c1_ = CHUNKS[c]
                    act.wait_ge(cact_done, c + 1)
                    act.activation(chi[:, :, c0:c1_], craw[:, :, c0:c1_], ACT.Copy).then_inc(chi_done, 1)

                for j in range(3 * (NG - 5)):
                    gate_evac(j)
                    if j in (4, 6, 8):
                        squares((j - 4) // 2)
                    if j == 12:
                        roots()
                    if j in (18, 22, 26):
                        sigmoids((j - 18) // 4)
                    if j in (21, 25, 29):
                        c_hi((j - 21) // 4)
                    if j % 3 == 2 and j // 3 < len(PREP3) - 4:
                        n = j // 3
                        act.wait_ge(g_ready, PREP3[n][1])
                        make_hi(act, raw3, n // 2 + 1, n, n % 2, whi[:, PREP3[n][0], :])
                    if j in (22, 25, 28, 31):
                        n = NG - 10 + (j - 22) // 3
                        act.wait_ge(g_ready, PREP3[n][1])
                        make_hi(act, raw3, n // 2 + 1, n, n % 2, whi[:, PREP3[n][0], :])

            @block.vector
            def _(dve):
                dve.wait_ge(c_in, 64)
                for c, (c0, c1_) in enumerate(CHUNKS):
                    dve.wait_ge(mean_ready, c + 1)
                    x = craw[:, :, c0:c1_]
                    dve.tensor_tensor(x, x, bank[4 + c][:, 0:c1_ - c0].unsqueeze(1).to_broadcast([P, 4, c1_ - c0]),
                                      ALU.subtract).then_inc(xc_done, 1)
                for c, (c0, c1_) in enumerate(CHUNKS):
                    dve.wait_ge(csd_done, c + 1)
                    dve.reciprocal(crs[:, c0:c1_], crs[:, c0:c1_]).then_inc(crs_done, 1)
                    dve.wait_ge(crs_done, c + 1)
                    x = craw[:, :, c0:c1_]
                    dve.tensor_tensor(x, x, crs[:, c0:c1_].unsqueeze(1).to_broadcast([P, 4, c1_ - c0]),
                                      ALU.mult).then_inc(cn_done, 1)
                for c, (c0, c1_) in enumerate(CHUNKS):
                    dve.wait_ge(csig_done, c + 1)
                    dve.wait_ge(cn_done, c + 1)
                    for m in range(4):
                        ins = dve.tensor_scalar(craw[:, m, c0:c1_], craw[:, m, c0:c1_],
                                                prm[:, PRM_CNG + m:PRM_CNG + m + 1], prm[:, PRM_CNB + m:PRM_CNB + m + 1],
                                                ALU.mult, ALU.add)
                    ins.then_inc(caff_done, 1)
                    dve.wait_ge(caff_done, c + 1)
                    dve.tensor_tensor(craw[:, :, c0:c1_], craw[:, :, c0:c1_], csig[:, :, 0:c1_ - c0],
                                      ALU.mult).then_inc(cact_done, 1)

            @block.tensor
            def _(pe):
                def gate_job(j):
                    g, c = j // 3, j % 3
                    c0, c1_ = CHUNKS[c]
                    if c == 0 and g >= 5:
                        pe.wait_ge(raw3[2], g - 4)
                    if j >= 4:
                        pe.wait_ge(g_ev, j - 3)
                    for k in range(KT):
                        ws = slice(P * k, P * k + P)
                        for i, (w, x) in enumerate(split_passes(whi, wlo, hhi, hlo)):
                            mm = pe.matmul(bank[j % 4][:, 0:c1_ - c0], w[:, g % 5, ws], x[:, k, c0:c1_],
                                           start=(k == 0 and i == 0), stop=(k == KT - 1 and i == 2))
                    mm.then_inc(g_ready, 1)

                def channel_mean(c, src, lo, done, need):
                    c0, c1_ = CHUNKS[c]
                    pe.wait_ge(done, need)
                    for m in range(4):
                        mm = pe.matmul(bank[4 + c][:, 0:c1_ - c0], ones[:, :], src[:, m, lo:lo + c1_ - c0],
                                       start=(m == 0), stop=(m == 3))
                    return mm

                pe.wait_ge(ones_done, 1)
                for j in range(3 * (NG - 5)):
                    gate_job(j)
                    if j == 0:
                        for c in range(3):
                            channel_mean(c, craw, CHUNKS[c][0], c_in, 64).then_inc(mean_ready, 1)
                    if j in (5, 7, 9):
                        c = (j - 5) // 2
                        channel_mean(c, csq, 0, csq_done, c + 1).then_inc(var_ready, 1)

        hctx.close()

        x1 = sb("x1", [P, NT, D])
        CH_OF_TOK = [next(c for c in range(3) if CHUNKS[c][1] >= t0 + P) for t0 in TOK]

        def down_job(pe, d, acts, w_slots, i, down_ev, down_ready, lo_sem, lo_need, w_sem, w_need):
            t, half = d // 2, d % 2
            if d == 0:
                pe.wait_ge(w_sem, w_need)
            if half == 0:
                pe.wait_ge(lo_sem, lo_need(CH_OF_TOK[t]))
            if d >= 4:
                pe.wait_ge(down_ev, 18 * i + d - 3)
            elif later(i):
                pe.wait_ge(down_ev, 18 * i)
            x_hi, x_lo = acts
            for k in range(2):
                w_hi, w_lo = w_slots[k]
                for n, (x, w) in enumerate(split_passes(x_hi, x_lo, w_hi, w_lo)):
                    mm = pe.matmul(bank[4 + d % 4][:, :], x[:, k, TOK[t]:TOK[t] + P], w[:, 512 * half:512 * half + 512],
                                   start=(k == 0 and n == 0), stop=(k == 1 and n == 2))
            mm.then_inc(down_ready, 1)

        def down_add(dve, d, i, down_ready, down_ev):
            t, half = d // 2, d % 2
            dve.wait_ge(down_ready, 18 * i + d + 1)
            if later(i):
                dve.wait_ge(down_ev, 18 * i + d - 17)
            y = x1[:, t, 512 * half:512 * half + 512]
            dve.tensor_tensor(y, bank[4 + d % 4][:, :], y, ALU.add).then_inc(down_ev, 1)

        with ExitStack() as c4:
            ohi = sb("ohi", [P, 4, T], F32R, c4)
            olo = sb("olo", [P, 4, T], F32R, c4)
            mhi = sb("mhi", [P, 2, T], F32R, c4)
            mlo = sb("mlo", [P, 2, T], F32R, c4)
            oraw = sb("oraw", [P, 2, T], c=c4)
            gch = sb("gch", [P, 3, 2, 364], c=c4)
            mixa = sb("mixa", [P, 2, 364], c=c4)
            mixc = sb("mixc", [P, 2, 364], c=c4)
            raw4 = ([sem("raw4_in0"), sem("raw4_in1")], sem("hi4_done"), sem("lo4_done"))
            x1_in, o_hi_done, o_lo_done = sem("x1_in"), sem("o_hi_done"), sem("o_lo_done")
            o_in = [sem("o_in0"), sem("o_in1")]
            gch_in = [sem(f"gch_in{c}") for c in range(3)]
            ac_ready, ac_ev, mix_done, m_hi_done, m_lo_done = (sem("ac_ready"), sem("ac_ev"), sem("mix_done"),
                                                              sem("m_hi_done"), sem("m_lo_done"))
            dn4_ready, dn4_ev = sem("dn4_ready"), sem("dn4_ev")
            NI = KT // 2
            block = c4.enter_context(nc.Block())

            @block.sync
            def _(sp):
                def send_gates(i, j, c):
                    c0, c1_ = CHUNKS[c]
                    if j == 1:
                        sp.wait_ge(ac_ev, 12 * i + 2 * c + 2)
                    elif later(i):
                        sp.wait_ge(ac_ev, 12 * i + 2 * c - 4)
                    sp.dma_start(gch[:, c, :, 0:c1_ - c0],
                                 scr["gate"][ds(4 * i + 2 * j, 2)].rearrange("g p t -> p g t")[:, :, c0:c1_]
                                 ).then_inc(gch_in[c], 16)

                def round_(i, last):
                    for j in range(2):
                        for c in range(3):
                            send_gates(i, j, c)
                    for k in range(4):
                        n = 4 * i + k
                        if last:
                            send_ffn_weights(sp, raw4, n, k % 2, FIRST_FFN[k][1], 0)
                        else:
                            send_out_weights(sp, raw4, n, k % 2, k, i + 1)

                for m in range(4):
                    if m >= 2:
                        sp.wait_ge(o_lo_done, m - 1)
                    sp.dma_start(oraw[:, m % 2, :], scr["o"][m]).then_inc(o_in[m % 2], 16)
                sp.dma_start(x1[:, 0:NT - 1, :], a["x_prompt"][0].rearrange("(t p) n -> p t n", p=P)).then_inc(x1_in, 16)
                sp.dma_start(x1[0:64, NT - 1, :], a["x_prompt"][0, SEQ - 64:SEQ, :]).then_inc(x1_in, 16)
                sp.dma_start(x1[64:P, NT - 1, :], a["x_sample"][0]).then_inc(x1_in, 16)
                round_(0, False)
                with sp.Fori(1, NI - 1) as i:
                    round_(i, False)
                round_(NI - 1, True)

            @block.gpsimd
            def _(pool):
                for m in range(4):
                    pool.wait_ge(o_hi_done, m + 1)
                    pool.tensor_tensor(olo[:, m, :], oraw[:, m % 2, :], ohi[:, m, :].bitcast(F32),
                                       ALU.subtract).then_inc(o_lo_done, 1)

                def round_(i, slots):
                    for j in range(2):
                        for c, (c0, c1_) in enumerate(CHUNKS):
                            pool.wait_ge(m_hi_done, 6 * i + 3 * j + c + 1)
                            pool.tensor_tensor(mlo[:, j, c0:c1_], mixa[:, (3 * j + c) % 2, 0:c1_ - c0],
                                               mhi[:, j, c0:c1_].bitcast(F32), ALU.subtract).then_inc(m_lo_done, 1)
                    for k, slot in enumerate(slots):
                        make_lo(pool, raw4, 4 * i + k, k % 2, wlo[:, slot, :], whi[:, slot, :])

                with pool.Fori(0, NI - 1) as i:
                    round_(i, (1, 2, 3, 4))
                round_(NI - 1, [x[0] for x in FIRST_FFN])

            @block.scalar
            def _(act):
                for m in range(4):
                    act.wait_ge(o_in[m % 2], 16 * (m // 2 + 1))
                    act.activation(ohi[:, m, :], oraw[:, m % 2, :], ACT.Copy).then_inc(o_hi_done, 1)

                def prepare(i, k, slot):
                    if slot in (1, 2):
                        act.wait_ge(ac_ready, 12 * i + 6 * slot)
                    elif slot > 2:
                        act.wait_ge(dn4_ready, 18 * i + 18)
                    make_hi(act, raw4, 2 * i + k // 2 + 1, 4 * i + k, k % 2, whi[:, slot, :])

                def round_(i, slots):
                    for j in range(2):
                        for c, (c0, c1_) in enumerate(CHUNKS):
                            act.wait_ge(mix_done, 6 * i + 3 * j + c + 1)
                            if j == 0 and c == 0 and (later(i)):
                                act.wait_ge(dn4_ready, 18 * i)
                            act.activation(mhi[:, j, c0:c1_], mixa[:, (3 * j + c) % 2, 0:c1_ - c0],
                                           ACT.Copy).then_inc(m_hi_done, 1)
                    for k, slot in enumerate(slots):
                        prepare(i, k, slot)

                round_(0, (1, 2, 3, 4))
                with act.Fori(1, NI - 1) as i:
                    round_(i, (1, 2, 3, 4))
                round_(NI - 1, [x[0] for x in FIRST_FFN])

            @block.vector
            def _(dve):
                def mix(i, j, c):
                    c0, c1_ = CHUNKS[c]
                    n, b, x = c1_ - c0, (3 * j + c) * 2, (3 * j + c) % 2
                    dve.wait_ge(gch_in[c], 16 * (2 * i + j + 1))
                    dve.wait_ge(ac_ready, 12 * i + b + 1)
                    need = 6 * i + 3 * j + c - 1
                    if later(need):
                        dve.wait_ge(m_lo_done, need)
                        dve.wait_ge(mix_done, need + 1)
                    dve.scalar_tensor_tensor(out=mixc[:, x, 0:n], in0=bank[b % 4][:, 0:n],
                                             scalar=prm[:, ds(PRM_BCO + 2 * i + j, 1)], in1=gch[:, c, 1, 0:n],
                                             op0=ALU.add, op1=ALU.mult).then_inc(ac_ev, 1)
                    dve.wait_ge(ac_ready, 12 * i + b + 2)
                    dve.tensor_tensor(mixa[:, x, 0:n], bank[(b + 1) % 4][:, 0:n], gch[:, c, 0, 0:n],
                                      ALU.mult).then_inc(ac_ev, 1)
                    dve.wait_ge(ac_ev, 12 * i + b + 2)
                    dve.tensor_tensor(mixa[:, x, 0:n], mixa[:, x, 0:n], mixc[:, x, 0:n], ALU.add).then_inc(mix_done, 1)

                def round_(i):
                    for j in range(2):
                        for c in range(3):
                            mix(i, j, c)
                    if isinstance(i, int) and i == 0:
                        dve.wait_ge(x1_in, 48)
                    for d in range(18):
                        down_add(dve, d, i, dn4_ready, dn4_ev)

                round_(0)
                with dve.Fori(1, NI) as i:
                    round_(i)

            @block.tensor
            def _(pe):
                def branch_job(i, b):
                    j, c, attn = b // 6, b // 2 % 3, b % 2
                    c0, c1_ = CHUNKS[c]
                    if c == 0 and attn == 0 and (later(i)):
                        pe.wait_ge(raw4[2], 4 * i - 3 + j)
                    if b >= 4:
                        pe.wait_ge(ac_ev, 12 * i + b - 3)
                    elif later(i):
                        pe.wait_ge(ac_ev, 12 * i)
                    x_hi, x_lo = (ohi, olo) if attn else (chi, clo)
                    for k in range(4):
                        if attn and isinstance(i, int) and i == 0 and b == 1:
                            pe.wait_ge(o_lo_done, k + 1)
                        ws = slice(P * k + (0 if attn else 512), P * k + (0 if attn else 512) + P)
                        for n, (w, x) in enumerate(split_passes(whi, wlo, x_hi, x_lo)):
                            mm = pe.matmul(bank[b % 4][:, 0:c1_ - c0], w[:, 1 + j, ws], x[:, k, c0:c1_],
                                           start=(k == 0 and n == 0), stop=(k == 3 and n == 2))
                    mm.then_inc(ac_ready, 1)

                def round_(i):
                    for b in range(12):
                        branch_job(i, b)
                    slots = [(whi[:, 3 + k, :], wlo[:, 3 + k, :]) for k in range(2)]
                    for d in range(18):
                        down_job(pe, d, (mhi, mlo), slots, i, dn4_ev, dn4_ready, m_lo_done,
                                 lambda c: 6 * i + 4 + c, raw4[2], 4 * i)

                round_(0)
                with pe.Fori(1, NI) as i:
                    round_(i)

        FT = FF // P
        NF = FT // 2
        with ExitStack() as c5:
            h2hi = sb("h2hi", [P, KT, T], F32R, c5)
            h2lo = sb("h2lo", [P, KT, T], F32R, c5)
            w5hi = sb("w5hi", [P, D], F32R, c5)
            w5lo = sb("w5lo", [P, D], F32R, c5)
            gain = sb("gain", [P, D], c=c5)
            ftail = sb("ftail", [P, 4, 2 * FT], c=c5)
            ss5, sd5, rs5 = sb("ss5", [P, 2 * NT], c=c5), sb("sd5", [P, 2 * NT], c=c5), sb("rs5", [P, 2 * NT], c=c5)
            s5 = {n: sem(n) for n in ("gain_in", "ss_done", "sd5_done", "rs5_done", "xn5_done", "xt5_ready", "h2_hi", "h2_lo")}

            with ExitStack() as c5a:
                xn = sb("xn", [P, 2, D], c=c5a)
                sq5 = sb("sq5", [P, 2, D], c=c5a)
                block = c5a.enter_context(nc.Block())

                @block.sync
                def _(sp):
                    sp.dma_start(gain[:, :], a["norm2_g"][0:1, :].to_broadcast([P, D])).then_inc(s5["gain_in"], 16)
                    sp.wait_ge(s5["gain_in"], 16)

                def hi_parts5(act, t):
                    new = 64 if t == NT - 1 else 0
                    for j in range(2):
                        act.wait_ge(s5["xt5_ready"], t + 1)
                        act.activation(h2hi[:, 4 * j:4 * j + 4, TOK[t] + new:TOK[t] + P],
                                       XB[2 * (t % 2) + j][:, :].rearrange("p (k t) -> p k t", k=4)[:, :, new:],
                                       ACT.Copy).then_inc(s5["h2_hi"], 1)

                @block.scalar
                def _(act):
                    for t in range(NT):
                        if t >= 2:
                            act.wait_ge(s5["ss_done"], t - 1)
                        act.activation(sq5[:, t % 2, :], x1[:, t, :], ACT.Square,
                                       accum_out=ss5[:, t:t + 1]).then_inc(s5["ss_done"], 1)
                        act.wait_ge(s5["ss_done"], t + 1)
                        act.activation(sd5[:, t:t + 1], ss5[:, t:t + 1], ACT.Sqrt, bias=epst[:, 0:1],
                                       scale=1.0 / D).then_inc(s5["sd5_done"], 1)
                        if t:
                            hi_parts5(act, t - 1)
                    hi_parts5(act, NT - 1)

                @block.vector
                def _(dve):
                    def lo_parts5(t):
                        new = 64 if t == NT - 1 else 0
                        for j in range(2):
                            dve.wait_ge(s5["h2_hi"], 2 * t + j + 1)
                            at = slice(TOK[t] + new, TOK[t] + P)
                            dve.tensor_tensor(h2lo[:, 4 * j:4 * j + 4, at],
                                              XB[2 * (t % 2) + j][:, :].rearrange("p (k t) -> p k t", k=4)[:, :, new:],
                                              h2hi[:, 4 * j:4 * j + 4, at].bitcast(F32), ALU.subtract
                                              ).then_inc(s5["h2_lo"], 1)

                    dve.wait_ge(s5["gain_in"], 16)
                    for t in range(NT):
                        dve.wait_ge(s5["sd5_done"], t + 1)
                        dve.reciprocal(rs5[:, t:t + 1], sd5[:, t:t + 1]).then_inc(s5["rs5_done"], 1)
                        dve.wait_ge(s5["rs5_done"], t + 1)
                        if t >= 2:
                            dve.wait_ge(s5["xt5_ready"], t - 1)
                        dve.scalar_tensor_tensor(out=xn[:, t % 2, :], in0=x1[:, t, :], scalar=rs5[:, t:t + 1],
                                                 in1=gain[:, :], op0=ALU.mult, op1=ALU.mult).then_inc(s5["xn5_done"], 1)
                        if t:
                            lo_parts5(t - 1)
                    lo_parts5(NT - 1)

                @block.tensor
                def _(pe):
                    for t in range(NT):
                        pe.wait_ge(s5["xn5_done"], t + 1)
                        if t >= 2:
                            pe.wait_ge(s5["h2_lo"], 2 * (t - 1))
                        for k in range(KT):
                            mm = pe.transpose(XB[2 * (t % 2) + k // 4][:, (k % 4) * P:(k % 4 + 1) * P],
                                              xn[:, t % 2, k * P:(k + 1) * P], ident[:, :])
                        mm.then_inc(s5["xt5_ready"], 1)

            with ExitStack() as c5b:
                UPC = 2 + SEQ + 2 + DEC
                NCH = [(0, 364), (364, 728), (728, UPC - 2)]
                ghi = sb("ghi", [P, 2, T], F32R, c5b)
                glo = sb("glo", [P, 2, T], F32R, c5b)
                up = sb("up", [P, 2, UPC], c=c5b)
                cvg = sb("cvg", [P, 3, 364], c=c5b)
                cvv = sb("cvv", [P, 2, 364], c=c5b)
                gsig = sb("gsig", [P, 2, 364], c=c5b)
                raw5 = ([sem("raw5_in0"), sem("raw5_in1")], sem("hi5_done"), sem("lo5_done"))
                up_init, up_ready, up_ev, up_state, up_tail = (sem("up_init"), sem("up_ready"), sem("up_ev"),
                                                              sem("up_state"), sem("up_tail"))
                c2_done, c1_done, cv_done = sem("c2_done"), sem("c1_done"), sem("cv_done")
                gsig_done, silu_done, g_done, g_hi_done, g_lo_done = (sem("gsig_done"), sem("silu_done"), sem("g_done"),
                                                                     sem("g_hi_done"), sem("g_lo_done"))
                dn_ready, dn_ev = sem("dn_ready"), sem("dn_ev")
                y_ready, y_out, fgain_in = sem("y_ready"), [sem("y_out0"), sem("y_out1")], sem("fgain_in")
                ft_ready, ft_done, ft_out = sem("ft_ready"), sem("ft_done"), sem("ft_out")
                fss_done, fsd_done, frs_done = sem("fss_done"), sem("fsd_done"), sem("frs_done")
                w_of = [(whi[:, s, :], wlo[:, s, :]) for s in range(5)] + [(w5hi[:, :], w5lo[:, :])]
                PREP5, LAST5 = (0, 4, 5, 1, 2, 3), (4, 5)
                yst = up[:, :, 0:D]
                ysq = cvg[:, :, :].rearrange("p a n -> p (a n)")[:, 0:D]
                frow = cvv[:, :, :].rearrange("p a n -> p (a n)")[0:2 * FT, 0:4 * P].rearrange("p (w c) -> p w c", w=4)

                def pieces(c):
                    c0, c1_ = CHUNKS[c]
                    return [(c0, c1_, 0)] if c1_ <= SEQ else [(c0, SEQ, 0), (SEQ, c1_, 2)]

                def tile_at(tau, i):
                    return FT * (tau % 2) + 2 * i + tau // 2

                def steps(i, last):
                    for tau in (1, 2, 3):
                        for c in range(3):
                            yield i, tau, c
                    if not last:
                        for c in range(3):
                            yield i + 1, 0, c

                block = c5b.enter_context(nc.Block())

                @block.sync
                def _(sp):
                    def round_(i, slots):
                        for k, what in enumerate(slots):
                            send_ffn_weights(sp, raw5, 6 * i + k, k % 2, what, i if what >= 4 else i + 1)

                    sp.dma_start(gain[:, :], a["final_g"].rearrange("(a n) -> a n", a=1).to_broadcast([P, D])
                                 ).then_inc(fgain_in, 16)
                    round_(0, PREP5)
                    with sp.Fori(1, NF - 1) as i:
                        round_(i, PREP5)
                    round_(NF - 1, LAST5)
                    for t in range(NT):
                        sp.wait_ge(y_ready, t + 1)
                        if t < NT - 1:
                            sp.dma_start(o["y_prompt"][0, P * t:P * t + P, :], yst[:, t % 2, :]).then_inc(y_out[t % 2], 16)
                        else:
                            sp.dma_start(o["y_sample"][0], yst[64:P, t % 2, :]).then_inc(y_out[t % 2], 16)
                    sp.wait_ge(ft_done, 1)
                    for x, name in enumerate(("ffn_conv_prompt", "ffn_conv_sample")):
                        for r in range(2):
                            sp.dma_start(o[name][0, 0, r].rearrange("(n c) -> n c", c=P),
                                         frow[:, 2 * x + r, :]).then_inc(ft_out, 16)
                    sp.wait_ge(ft_out, 64)
                    sp.wait_ge(y_out[0], 16 * ((NT + 1) // 2))
                    sp.wait_ge(y_out[1], 16 * (NT // 2))

                @block.gpsimd
                def _(pool):
                    pool.memset(up[:, :, 0:2], 0.0).then_inc(up_init, 1)

                    def g_lo(i, j, c):
                        pool.wait_ge(g_hi_done, 6 * i + 3 * j + c + 1)
                        for x0, x1_, sh in pieces(c):
                            n0 = sh - NCH[c][0]
                            ins = pool.tensor_tensor(glo[:, j, x0:x1_], cvv[:, (3 * j + c) % 2, x0 + n0:x1_ + n0],
                                                     ghi[:, j, x0:x1_].bitcast(F32), ALU.subtract)
                        ins.then_inc(g_lo_done, 1)

                    def window(i, slots):
                        def prep(k):
                            if k < len(slots):
                                w_hi, w_lo = w_of[slots[k]]
                                make_lo(pool, raw5, 6 * i + k, k % 2, w_lo, w_hi)

                        prep(0)
                        prep(1)
                        g_lo(i, 0, 0)
                        prep(2)
                        g_lo(i, 0, 1)
                        g_lo(i, 0, 2)
                        prep(3)
                        prep(4)
                        for c in range(3):
                            g_lo(i, 1, c)
                        prep(5)

                    with pool.Fori(0, NF - 1) as i:
                        window(i, PREP5)
                    window(NF - 1, LAST5)

                @block.scalar
                def _(act):
                    def copy_up(i, tau, c):
                        c0, c1_ = CHUNKS[c]
                        x = tau % 2
                        act.wait_ge(up_ready, 12 * i + 3 * tau + c + 1)
                        need = 12 * i + 3 * (tau - 2) + min(c + 2, 3)
                        if later(i) or tau >= 2:
                            act.wait_ge(cv_done, need)
                        if c == 2 and (later(i) or tau >= 2):
                            act.wait_ge(up_tail, 8 * i + 2 * tau - 2)
                        for x0, x1_, sh in pieces(c):
                            ins = act.activation(up[:, x, x0 + sh + 2:x1_ + sh + 2],
                                                 bank[(3 * tau + c) % 4][:, x0 - c0:x1_ - c0], ACT.Copy)
                        ins.then_inc(up_ev, 1)
                        if c == 1:
                            act.activation(up[:, x, SEQ + 2:SEQ + 4], ffn_state[:, :, ds(tile_at(tau, i), 1)]
                                           .rearrange("p w a -> p (w a)"), ACT.Copy).then_inc(up_state, 1)
                        if c == 2:
                            act.wait_ge(up_ev, 12 * i + 3 * tau + 3)
                            for y, first in enumerate((SEQ, UPC - 2)):
                                act.activation(ftail[:, 2 * y:2 * y + 2, ds(tile_at(tau, i), 1)].rearrange("p w a -> p (w a)"),
                                               up[:, x, first:first + 2], ACT.Copy).then_inc(up_tail, 1)

                    def gate_sig(i, j, c):
                        n, r = NCH[c][1] - NCH[c][0], 6 * i + 3 * j + c
                        act.wait_ge(cv_done, 12 * i + 6 * j + c + 1)
                        if later(r - 1):
                            act.wait_ge(silu_done, r - 1)
                        act.activation(gsig[:, (3 * j + c) % 2, 0:n], cvg[:, c, 0:n], ACT.Sigmoid).then_inc(gsig_done, 1)

                    def g_hi(i, j, c):
                        act.wait_ge(g_done, 6 * i + 3 * j + c + 1)
                        if j == 0 and c == 0 and later(i):
                            act.wait_ge(dn_ready, 18 * i)
                        for x0, x1_, sh in pieces(c):
                            n0 = sh - NCH[c][0]
                            ins = act.activation(ghi[:, j, x0:x1_], cvv[:, (3 * j + c) % 2, x0 + n0:x1_ + n0], ACT.Copy)
                        ins.then_inc(g_hi_done, 1)

                    def gating(i, tau, c):
                        if tau % 2:
                            g_hi(i, tau // 2, c)
                        else:
                            gate_sig(i, tau // 2, c)

                    def prep(i, k, s):
                        if s < 4:
                            act.wait_ge(up_ready, 12 * i + 3 * s + 3)
                        elif later(i):
                            act.wait_ge(dn_ready, 18 * i)
                        make_hi(act, raw5, 3 * i + k // 2 + 1, 6 * i + k, k % 2, w_of[s][0])

                    PREP_AT = {(1, 0): 0, (1, 1): 1, (1, 2): 2, (2, 0): 3, (3, 0): 4, (0, 0): 5}

                    def window(i, slots, last=False):
                        before = (i, 0, 2)
                        for step in steps(i, last):
                            gating(*before)
                            copy_up(*step)
                            before = step
                            k = PREP_AT.get(step[1:], 9)
                            if k < len(slots):
                                prep(i, k, slots[k])
                        if last:
                            gating(*before)

                    act.wait_ge(up_init, 1)
                    for c in range(3):
                        if c:
                            gating(0, 0, c - 1)
                        copy_up(0, 0, c)
                    window(0, PREP5)
                    with act.Fori(1, NF - 1) as i:
                        window(i, PREP5)
                    window(NF - 1, LAST5, True)
                    act.wait_ge(g_done, 6 * NF)
                    for t in range(NT):
                        act.wait_ge(dn_ev, 18 * (NF - 1) + 2 * t + 2)
                        if t:
                            act.wait_ge(fss_done, t)
                        act.activation(ysq, x1[:, t, :], ACT.Square, accum_out=ss5[:, NT + t:NT + t + 1]).then_inc(fss_done, 1)
                        act.wait_ge(fss_done, t + 1)
                        act.activation(sd5[:, NT + t:NT + t + 1], ss5[:, NT + t:NT + t + 1], ACT.Sqrt, bias=epst[:, 0:1],
                                       scale=1.0 / D).then_inc(fsd_done, 1)
                    act.wait_ge(ft_ready, 1)
                    act.wait_ge(g_lo_done, 6 * NF)
                    act.activation(frow, bank[0][0:2 * FT, :].rearrange("p (w c) -> p w c", w=4), ACT.Copy).then_inc(ft_done, 1)

                @block.vector
                def _(dve):
                    def conv(i, tau, c):
                        n0, n1 = NCH[c]
                        n, at, r = n1 - n0, 12 * i + 3 * tau + c, 6 * i + 3 * (tau // 2) + c
                        tile = tile_at(tau, i)
                        dve.wait_ge(up_ev, at + 1)
                        if c == 2:
                            dve.wait_ge(up_state, 4 * i + tau + 1)
                        if tau % 2 == 0:
                            dst = cvg[:, c, 0:n]
                            if later(i) or tau >= 2:
                                dve.wait_ge(g_done, r - 2)
                        else:
                            dst = cvv[:, (3 * (tau // 2) + c) % 2, 0:n]
                            if later(r - 1):
                                dve.wait_ge(g_lo_done, r - 1)

                        def w(k):
                            return ffw[:, k, ds(tile, 1)]

                        src = up[:, tau % 2, :]
                        dve.tensor_scalar(dst, src[:, n0 + 2:n1 + 2], w(2), prm[:, ds(PRM_FDB + tile, 1)],
                                          ALU.mult, ALU.add).then_inc(c2_done, 1)
                        dve.wait_ge(c2_done, at + 1)
                        dve.scalar_tensor_tensor(out=dst, in0=src[:, n0 + 1:n1 + 1], scalar=w(1), in1=dst, op0=ALU.mult,
                                                 op1=ALU.add).then_inc(c1_done, 1)
                        dve.wait_ge(c1_done, at + 1)
                        dve.scalar_tensor_tensor(out=dst, in0=src[:, n0:n1], scalar=w(0), in1=dst, op0=ALU.mult,
                                                 op1=ALU.add).then_inc(cv_done, 1)

                    def silu(i, j, c):
                        n, r = NCH[c][1] - NCH[c][0], 6 * i + 3 * j + c
                        dve.wait_ge(gsig_done, r + 1)
                        dve.wait_ge(cv_done, 12 * i + 6 * j + c + 1)
                        dve.tensor_tensor(cvg[:, c, 0:n], cvg[:, c, 0:n], gsig[:, (3 * j + c) % 2, 0:n],
                                          ALU.mult).then_inc(silu_done, 1)

                    def product(i, j, c):
                        n, r, x = NCH[c][1] - NCH[c][0], 6 * i + 3 * j + c, (3 * j + c) % 2
                        dve.wait_ge(silu_done, r + 1)
                        dve.wait_ge(cv_done, 12 * i + 6 * j + 3 + c + 1)
                        dve.tensor_tensor(cvv[:, x, 0:n], cvv[:, x, 0:n], cvg[:, c, 0:n], ALU.mult).then_inc(g_done, 1)

                    def window(i, last=False):
                        before = (i, 0, 2)
                        for step in steps(i, last):
                            if before[1] % 2 == 0:
                                silu(before[0], before[1] // 2, before[2])
                            conv(*step)
                            if step[1] % 2:
                                product(step[0], step[1] // 2, step[2])
                            before = step

                    def final_norm(t):
                        dve.wait_ge(fsd_done, t + 1)
                        dve.reciprocal(rs5[:, NT + t:NT + t + 1], sd5[:, NT + t:NT + t + 1]).then_inc(frs_done, 1)
                        dve.wait_ge(frs_done, t + 1)
                        dve.wait_ge(dn_ev, 18 * (NF - 1) + 2 * t + 2)
                        if t >= 2:
                            dve.wait_ge(y_out[t % 2], 16 * (t // 2))
                        dve.scalar_tensor_tensor(out=yst[:, t % 2, :], in0=x1[:, t, :], scalar=rs5[:, NT + t:NT + t + 1],
                                                 in1=gain[:, :], op0=ALU.mult, op1=ALU.mult).then_inc(y_ready, 1)

                    for c in range(3):
                        if c:
                            silu(0, 0, c - 1)
                        conv(0, 0, c)
                    window(0)
                    for d in range(18):
                        down_add(dve, d, 0, dn_ready, dn_ev)
                    with dve.Fori(1, NF - 1) as i:
                        window(i)
                        for d in range(18):
                            down_add(dve, d, i, dn_ready, dn_ev)
                    window(NF - 1, True)
                    dve.wait_ge(cv_done, 12 * NF)
                    dve.wait_ge(up_tail, 8 * NF)
                    dve.wait_ge(fgain_in, 16)
                    for d in range(18):
                        down_add(dve, d, NF - 1, dn_ready, dn_ev)
                        if d % 2 and d >= 3:
                            final_norm(d // 2 - 1)
                    final_norm(NT - 1)

                @block.tensor
                def _(pe):
                    def up_job(i, tau, c):
                        c0, c1_ = CHUNKS[c]
                        job = 12 * i + 3 * tau + c
                        if c == 0 and later(i):
                            pe.wait_ge(raw5[2], 6 * (i - 1) + PREP5.index(tau) + 1)
                        if later(job, 4):
                            pe.wait_ge(up_ev, job - 3)
                        w_hi, w_lo = w_of[tau]
                        for k in range(KT):
                            ws = slice(P * k, P * k + P)
                            for n, (w, x) in enumerate(split_passes(w_hi, w_lo, h2hi, h2lo)):
                                mm = pe.matmul(bank[(3 * tau + c) % 4][:, 0:c1_ - c0], w[:, ws], x[:, k, c0:c1_],
                                               start=(k == 0 and n == 0), stop=(k == KT - 1 and n == 2))
                        mm.then_inc(up_ready, 1)

                    def window(i, last=False):
                        for step in steps(i, last):
                            up_job(*step)
                        slots = LAST5 if last else PREP5
                        for d in range(18):
                            down_job(pe, d, (ghi, glo), w_of[4:6], i, dn_ev, dn_ready, g_lo_done, lambda c: 6 * i + 4 + c,
                                     raw5[2], 6 * i + slots.index(5) + 1)

                    for c in range(3):
                        up_job(0, 0, c)
                    window(0)
                    with pe.Fori(1, NF - 1) as i:
                        window(i)
                    window(NF - 1, True)
                    pe.wait_ge(up_ev, 12 * NF)
                    pe.wait_ge(up_tail, 8 * NF)
                    for w in range(4):
                        mm = pe.transpose(bank[0][0:2 * FT, P * w:P * w + P], ftail[:, w, :], ident[:, :])
                    mm.then_inc(ft_ready, 1)


_INS = ["x_prompt", "x_sample", "cache_sb_k", "cache_sb_v", "state_conv", "state_ffn_conv", "norm1_g", "w_in", "b_in",
        "q_norm_g", "k_norm_g", "w_attn_out", "dw_w", "dw_b", "cn_g", "cn_b", "w_conv_out", "b_conv_out", "w_out",
        "norm2_g", "w_up", "ffn_dw_w", "ffn_dw_b", "w_down", "final_g"]
_OUTS = {
    "y_prompt": (1, SEQ, D), "y_sample": (1, DEC, D),
    "k_prompt": (1, 1, SEQ, H, DH), "v_prompt": (1, 1, SEQ, H, DH),
    "k_sample": (1, 1, DEC, H, DH), "v_sample": (1, 1, DEC, H, DH),
    "conv_prompt": (1, 1, CW - 1, CC), "conv_sample": (1, 1, CW - 1, CC),
    "ffn_conv_prompt": (1, 1, FW - 1, 2 * FF), "ffn_conv_sample": (1, 1, FW - 1, 2 * FF),
}
_SCRATCH = {"o": (PAIRS, P, T), "c": (PAIRS, P, T), "gate": (2 * KT, P, T)}


def kernel(**inputs):
    import numpy as _np
    import concourse.bacc as _bacc
    from concourse.bass_utils import run_bass_kernel_spmd as _run

    nc = _bacc.Bacc("TRN2", target_bir_lowering=False, num_devices=1)
    arrays, a = {}, {}
    for name in _INS:
        arrays[f"in_{name}"] = _np.ascontiguousarray(inputs[name])
        a[name] = nc.dram_tensor(f"in_{name}", arrays[f"in_{name}"].shape, F32, kind="ExternalInput").ap()
    o = {n: nc.dram_tensor(f"out_{n}", s, F32, kind="ExternalOutput").ap() for n, s in _OUTS.items()}
    scr = {n: nc.dram_tensor(f"scr_{n}", s, F32, kind="Internal").ap() for n, s in _SCRATCH.items()}
    build(nc, a, o, scr)
    r = _run(nc, [arrays], core_ids=[0])
    return tuple(r.results[0][f"out_{n}"] for n in _OUTS)
```

```python
from contextlib import ExitStack

import concourse.bass as bass
from concourse import mybir
from concourse.bass import ds

F32 = mybir.dt.float32
F32R = mybir.dt.float32r
BF16 = mybir.dt.bfloat16
ALU = mybir.AluOpType
ACT = mybir.ActivationFunctionType

P = 128
D = 1024
SEQ, DEC, PAST = 1024, 64, 2048
T = SEQ + DEC
H, DH = 8, 64
AW = H * DH
CC, CW = 512, 31
FF, FW = 2816, 3
KT = D // P
NT = (T + P - 1) // P
PAIRS = H // 2
TOK = [P * t for t in range(NT - 1)] + [T - P]
CHUNKS = [(0, 364), (364, 728), (728, T)]
EPS = 1e-6
QB = 64
NB = T // QB
UCOLS = CW - 1 + T + CW - 1
U_SAMPLE = CW - 1 + SEQ
COUT = SEQ + CW - 1 + DEC
NSLOT = 5


def attention_units():
    units = []
    for i in range(NB - 1):
        keys = P * (i // 2 + 1)
        cuts = list(range(0, keys, 512)) + [keys]
        spans = list(zip(cuts[:-1], cuts[1:]))[::-1]
        for n, (a, b) in enumerate(spans):
            units.append((i, a, b - a, n == 0, n == len(spans) - 1, None, i % 2 if n == 0 else None))
    units.append((NB - 1, T - P, P, True, False, None, 2))
    for c in range(PAST // 512)[::-1]:
        units.append((NB - 1, 512 * c, 512, False, c == 0, c, None))
    return units


UNITS = attention_units()
NU = len(UNITS)
NS = NU + 4
PASTS = [u for u, x in enumerate(UNITS) if x[5] is not None]
ACT_EVACS = ["k0", "k1", "k2"]
WT_JOBS = ["k0", "k1", "k2", "q0", "q1", "q2"]
for _s in range(NS):
    if _s + 1 in PASTS:
        ACT_EVACS.append(f"past{PASTS.index(_s + 1)}")
        WT_JOBS.append(f"past{PASTS.index(_s + 1)}")
    if 0 <= _s - 2 < NU:
        ACT_EVACS.append(f"w{_s - 2}")
        WT_JOBS.append(f"w{_s - 2}")
NEV, NWT = len(ACT_EVACS), len(WT_JOBS)


def build(nc, a, o, scr):
    ctx = ExitStack()
    with ctx:
        def sb(name, shape, dt=F32, c=ctx):
            return c.enter_context(nc.sbuf_tensor(name, shape, dt))

        def sem(name):
            return ctx.enter_context(nc.semaphore(name))

        bank = [ctx.enter_context(nc.psum_tensor(f"bank{i}", [P, 512], F32)) for i in range(8)]
        ident = sb("ident", [P, P])
        identb = sb("identb", [P, P], BF16)
        maskb = sb("maskb", [P, 3, P], BF16)
        prm = sb("prm", [P, 88])
        dww = sb("dww", [P, 4, CW])
        ffw = sb("ffw", [P, FW, 44])
        epst = sb("epst", [P, 1])
        conv_state = sb("conv_state", [P, 4, CW - 1])
        ffn_state = sb("ffn_state", [P, 2, 44])
        PRM_BIN, PRM_DWB, PRM_CNG, PRM_CNB, PRM_BCO, PRM_FDB = 0, 24, 28, 32, 36, 44
        utail = sb("utail", [P, 4, 2 * (CW - 1)])
        wraw = sb("wraw", [P, 2, KT * P])
        whi = sb("whi", [P, NSLOT, KT * P], F32R)
        wlo = sb("wlo", [P, NSLOT, KT * P], F32R)
        hctx = ctx.enter_context(ExitStack())
        hhi = sb("hhi", [P, KT, T], F32R, hctx)
        hlo = sb("hlo", [P, KT, T], F32R, hctx)
        w_in = a["w_in"][0].rearrange("(k p) n -> p k n", p=P)

        def gate_col(g):
            return 3 * AW + 2 * CC + D * (g % 2) + P * (g // 2)

        def gate_bias(g):
            at = PRM_BIN + 8 + KT * (g % 2) + g // 2
            return prm[:, at:at + 1]

        def later(n, least=1):
            return not isinstance(n, int) or n >= least

        def split_passes(x_hi, x_lo, y_hi, y_lo):
            return ((x_hi, y_hi), (x_hi, y_lo), (x_lo, y_hi))

        qctx = ctx.enter_context(ExitStack())
        stage = sb("stage", [P, NT, 3 * P], c=qctx)
        bqkv = sb("bqkv", [P, 3 * P], c=qctx)
        gqk = sb("gqk", [P, 2 * P], c=qctx)
        ssq = sb("ssq", [P, NT * 4], c=qctx)
        junk = sb("junk", [P, 4, DH], c=qctx)
        raw_in = [sem(f"raw_in{i}") for i in range(2)]
        hi_done, lo_done = sem("hi_done"), sem("lo_done")
        g_in2, b_in2 = sem("g_in2"), sem("b_in2")
        pj_ready, qkv_ev, stat_done = sem("pj_ready"), sem("qkv_ev"), sem("stat_done")
        b_ev, a_ev, kv_out, v_copy, wt_ready = sem("b_ev"), sem("a_ev"), sem("kv_out"), sem("v_copy"), sem("wt_ready")
        gate_ev, gate_out2, spill = sem("gate_ev"), sem("gate_out2"), sem("spill")
        PJ, XB = bank[0:2], bank[2:6]
        PREP_BEFORE_RAW = [0, -1, 1, 2, 3]
        RAW_USES = ((3, {0: 0, 2: 1, 4: 2}), (2, {1: 0, 3: 1}))

        def load_slot(sp, s, p, col):
            need = PREP_BEFORE_RAW[s] + 5 * p
            if later(need):
                sp.wait_ge(lo_done, need)
            sp.dma_start(wraw[:, s % 2, :].rearrange("p (k n) -> p k n", k=KT),
                         w_in[:, :, ds(col, P)]).then_inc(raw_in[s % 2], 16)

        def load_qkv(sp, s, p):
            load_slot(sp, s, p, AW * s + P * p)

        def load_ab(sp, x, p):
            load_slot(sp, 3 + x, p, 3 * AW + CC * (1 - x) + P * p)

        def load_bias(sp, p):
            sp.dma_start(bqkv[:, :].rearrange("p (x c) -> p x c", x=3),
                         a["b_in"][0, 0:3 * AW].rearrange("(x n) -> x n", x=3)[:, ds(P * p, P)]
                         .partition_broadcast(P)).then_inc(b_in2, 16)

        def slot_lo(pool, s, p):
            pool.wait_ge(hi_done, 5 * p + s + 1)
            pool.tensor_tensor(wlo[:, s, :], wraw[:, s % 2, :], whi[:, s, :].bitcast(F32),
                               ALU.subtract).then_inc(lo_done, 1)

        def slot_hi(act, s, p):
            per, at = RAW_USES[s % 2]
            act.wait_ge(raw_in[s % 2], 16 * (per * p + at[s] + 1))
            if isinstance(p, int) and p == 5:
                act.wait_ge(pj_ready, 15 * PAIRS + 3 * s + 3)
            elif later(p):
                act.wait_ge(pj_ready, 15 * p - 6 if s < 3 else 15 * p)
            act.activation(whi[:, s, :], wraw[:, s % 2, :], ACT.Copy).then_inc(hi_done, 1)

        def qkv_stats(act, p, t):
            act.wait_ge(qkv_ev, NT * p + t + 1)
            if t > 0 or later(p):
                act.wait_ge(stat_done, NT * p + t)
            for g in range(4):
                ins = act.activation(junk[:, g, :], stage[:, t, DH * g:DH * g + DH], ACT.Square,
                                     accum_out=ssq[:, 4 * t + g:4 * t + g + 1])
            ins.then_inc(stat_done, 1)

        def qkv_evac(dve, p, t):
            dve.wait_ge(pj_ready, 15 * p + t + 1)
            if t == 0:
                dve.wait_ge(b_in2, 16 * p + 16)
                if later(p):
                    dve.wait_ge(kv_out, 64 * p)
                    dve.wait_ge(v_copy, p)
                    dve.wait_ge(wt_ready, NWT * (p - 1) + 6)
            dve.tensor_tensor(stage[:, t, :], PJ[t % 2][:, 0:3 * P], bqkv[:, :], ALU.add).then_inc(qkv_ev, 1)

        def qkv_half(pe, p, t, half):
            if half == 0:
                if t == 0:
                    pe.wait_ge(lo_done, 5 * p + 3)
                if t >= 2:
                    pe.wait_ge(qkv_ev, NT * p + t - 1)
                elif later(p):
                    pe.wait_ge(a_ev, 3 * p)
                    pe.wait_ge(b_ev, 3 * p)
            tok = slice(TOK[t], TOK[t] + P)
            for k in range(4 * half, 4 * half + 4):
                ws = slice(P * k, P * k + P)
                for n, (x, w) in enumerate(split_passes(hhi, hlo, whi, wlo)):
                    mm = pe.matmul(PJ[t % 2][:, 0:3 * P], x[:, k, tok], w[:, 0:3, ws],
                                   start=(k == 0 and n == 0), stop=(k == KT - 1 and n == 2))
            if half:
                mm.then_inc(pj_ready, 1)

        with ExitStack() as c1:
            xt = sb("xt", [P, 3, D], c=c1)
            sq = sb("sq", [P, 2, D], c=c1)
            g1 = sb("g1", [P, D], c=c1)
            ss = sb("ss1", [P, NT], c=c1)
            sd = sb("sd1", [P, NT], c=c1)
            rs = sb("rs1", [P, NT], c=c1)
            prm_rows = sb("prm_rows", [88, P], c=c1)
            dww_rows = sb("dww_rows", [CW, CC], c=c1)
            ffw_rows = sb("ffw_rows", [44, FW, P], c=c1)
            fst_rows = sb("fst_rows", [44, 2, P], c=c1)
            cst_rows = sb("cst_rows", [CW - 1, CC], c=c1)
            x_in = [sem(f"x_in{i}") for i in range(3)]
            par_in, g_in = sem("par_in"), sem("g_in")
            const_done, maskf_done = sem("const_done"), sem("maskf_done")
            maskf = sb("maskf", [P, 3, P], c=c1)
            sq_done, sd_done, rs_done1 = sem("sq_done"), sem("sd_done"), sem("rs_done1")
            xn_done, xt_ready = sem("xn_done"), sem("xt_ready")
            h_hi_done, h_lo_done = sem("h_hi_done"), sem("h_lo_done")
            par_ready, par_done = sem("par_ready"), sem("par_done")

            block = c1.enter_context(nc.Block())

            @block.sync
            def _(sp):
                def load_x(t):
                    if t >= 3:
                        sp.wait_ge(xt_ready, t - 2)
                    if t < NT - 1:
                        sp.dma_start(xt[:, t % 3, :], a["x_prompt"][0, P * t:P * t + P, :]).then_inc(x_in[t % 3], 16)
                    else:
                        sp.dma_start(xt[0:64, t % 3, :], a["x_prompt"][0, SEQ - 64:SEQ, :]).then_inc(x_in[t % 3], 16)
                        sp.dma_start(xt[64:P, t % 3, :], a["x_sample"][0]).then_inc(x_in[t % 3], 16)

                load_x(0)
                load_qkv(sp, 0, 0)
                sp.dma_start(g1[:, :], a["norm1_g"][0:1, :].to_broadcast([P, D])).then_inc(g_in, 16)
                load_x(1)
                load_qkv(sp, 1, 0)
                load_x(2)
                load_bias(sp, 0)
                load_qkv(sp, 2, 0)
                load_x(3)
                rows = lambda ap, n: ap.rearrange("(r c) -> r c", r=n)
                sp.dma_start(prm_rows[0:24, :], rows(a["b_in"][0, 3 * AW:], 24)).then_inc(par_in, 16)
                sp.dma_start(prm_rows[24:28, :], rows(a["dw_b"][0], 4)).then_inc(par_in, 16)
                sp.dma_start(prm_rows[28:32, :], rows(a["cn_g"][0], 4)).then_inc(par_in, 16)
                sp.dma_start(prm_rows[32:36, :], rows(a["cn_b"][0], 4)).then_inc(par_in, 16)
                sp.dma_start(prm_rows[36:44, :], rows(a["b_conv_out"][0], 8)).then_inc(par_in, 16)
                sp.dma_start(prm_rows[44:88, :], rows(a["ffn_dw_b"][0], 44)).then_inc(par_in, 16)
                sp.dma_start(dww_rows[:, :], a["dw_w"][0]).then_inc(par_in, 16)
                sp.dma_start(ffw_rows[:, :, :], a["ffn_dw_w"][0].rearrange("w (r c) -> r w c", c=P)
                                ).then_inc(par_in, 16)
                sp.dma_start(fst_rows[:, :, :], a["state_ffn_conv"][0, 0].rearrange("w (r c) -> r w c", c=P)
                                ).then_inc(par_in, 16)
                sp.dma_start(cst_rows[:, :], a["state_conv"][0, 0]).then_inc(par_in, 16)
                for t in range(4, NT):
                    load_x(t)
                    if t in (5, 6):
                        load_ab(sp, t - 5, 0)
                for x, name in enumerate(("q_norm_g", "k_norm_g")):
                    for hd in range(2):
                        sp.dma_start(gqk[:, P * x + DH * hd:P * x + DH * hd + DH],
                                     a[name][0:1, :].to_broadcast([P, DH])).then_inc(g_in2, 16)
                load_qkv(sp, 0, 1)
                load_qkv(sp, 1, 1)

            @block.gpsimd
            def _(pool):
                pool.memset(ident[:, :], 0.0).then_inc(maskf_done, 1)
                pool.memset(maskf[:, :, :], 0.0).then_inc(maskf_done, 1)
                pool.memset(epst[:, :], EPS).then_inc(maskf_done, 1)
                pool.wait_ge(maskf_done, 3)
                pool.affine_select(out=ident[:, :], in_=ident[:, :], compare_op=ALU.not_equal, fill=1.0, base=0,
                                   pattern=[[-1, P]], channel_multiplier=1).then_inc(maskf_done, 1)
                for half in range(2):
                    rows = slice(64 * half, 64 * half + 64)
                    for m, first in enumerate((0, 64, 64)):
                        pool.wait_ge(maskf_done, 4 + 3 * half + m)
                        pool.affine_select(out=maskf[rows, m, :], in_=maskf[rows, m, :], compare_op=ALU.is_gt,
                                           fill=-1e30, base=first, pattern=[[-1, P]],
                                           channel_multiplier=1).then_inc(maskf_done, 1)
                pool.wait_ge(maskf_done, 10)
                pool.memset(maskf[:, 2, 0:64], -1e30).then_inc(maskf_done, 1)
                for s in range(5):
                    slot_lo(pool, s, 0)

            def hi_parts(act, t):
                for j in range(2):
                    act.wait_ge(xt_ready, t + 1)
                    new = 64 if t == NT - 1 else 0
                    act.activation(hhi[:, 4 * j:4 * j + 4, TOK[t] + new:TOK[t] + P],
                                   XB[2 * (t % 2) + j][:, :].rearrange("p (k t) -> p k t", k=4)[:, :, new:],
                                   ACT.Copy).then_inc(h_hi_done, 1)

            @block.scalar
            def _(act):
                for t in range(NT):
                    act.wait_ge(x_in[t % 3], 16 * (t // 3 + 1 + (t == NT - 1)))
                    if t >= 2:
                        act.wait_ge(sq_done, t - 1)
                    act.activation(sq[:, t % 2, :], xt[:, t % 3, :], ACT.Square,
                                   accum_out=ss[:, t:t + 1]).then_inc(sq_done, 1)
                    act.wait_ge(sq_done, t + 1)
                    act.wait_ge(maskf_done, 3)
                    act.activation(sd[:, t:t + 1], ss[:, t:t + 1], ACT.Sqrt, bias=epst[:, 0:1],
                                   scale=1.0 / D).then_inc(sd_done, 1)
                    if t in (0, 1, 2, 4, 6):
                        slot_hi(act, (0, 1, 2, 4, 6).index(t), 0)
                    if t >= 1:
                        hi_parts(act, t - 1)
                    if t >= 5:
                        qkv_stats(act, 0, t - 5)
                hi_parts(act, NT - 1)
                for t in range(NT - 5, NT - 1):
                    qkv_stats(act, 0, t)

            @block.vector
            def _(dve):
                def lo_parts(t):
                    for j in range(2):
                        dve.wait_ge(h_hi_done, 2 * t + j + 1)
                        new = 64 if t == NT - 1 else 0
                        dve.tensor_tensor(hlo[:, 4 * j:4 * j + 4, TOK[t] + new:TOK[t] + P],
                                          XB[2 * (t % 2) + j][:, :].rearrange("p (k t) -> p k t", k=4)[:, :, new:],
                                          hhi[:, 4 * j:4 * j + 4, TOK[t] + new:TOK[t] + P].bitcast(F32),
                                          ALU.subtract).then_inc(h_lo_done, 1)

                def parameters():
                    dve.wait_ge(maskf_done, 11)
                    dve.tensor_copy(identb[:, :], ident[:, :]).then_inc(const_done, 1)
                    dve.tensor_copy(maskb[:, :, :], maskf[:, :, :]).then_inc(const_done, 1)
                    dve.wait_ge(par_ready, 1)
                    b4, b5 = bank[6], bank[7]
                    dve.tensor_copy(prm[:, :], b4[:, 0:88]).then_inc(par_done, 1)
                    dve.tensor_copy(ffw[:, :, :], b4[:, 88:220].rearrange("p (w r) -> p w r", w=3)
                                    ).then_inc(par_done, 1)
                    dve.tensor_copy(ffn_state[:, :, :], b4[:, 220:308].rearrange("p (w r) -> p w r", w=2)
                                    ).then_inc(par_done, 1)
                    dve.tensor_copy(dww[:, :, :], b5[:, 0:128].rearrange("p (k w) -> p k w", k=4)[:, :, 0:CW]
                                    ).then_inc(par_done, 1)
                    dve.tensor_copy(conv_state[:, :, :],
                                    b5[:, 128:256].rearrange("p (k w) -> p k w", k=4)[:, :, 0:CW - 1]
                                                    ).then_inc(par_done, 1)

                dve.wait_ge(g_in, 16)
                for t in range(NT):
                    dve.wait_ge(sd_done, t + 1)
                    dve.reciprocal(rs[:, t:t + 1], sd[:, t:t + 1]).then_inc(rs_done1, 1)
                    dve.wait_ge(rs_done1, t + 1)
                    dve.scalar_tensor_tensor(out=xt[:, t % 3, :], in0=xt[:, t % 3, :], scalar=rs[:, t:t + 1],
                                             in1=g1[:, :], op0=ALU.mult, op1=ALU.mult).then_inc(xn_done, 1)
                    if t >= 1:
                        lo_parts(t - 1)
                    if t >= 4:
                        qkv_evac(dve, 0, t - 4)
                    if t == 6:
                        parameters()
                lo_parts(NT - 1)
                for t in range(NT - 4, NT):
                    qkv_evac(dve, 0, t)

            @block.tensor
            def _(pe):
                def parameters():
                    pe.wait_ge(par_in, 160)
                    b4, b5 = bank[6], bank[7]
                    pe.transpose(b4[:, 0:88], prm_rows[:, :], ident[0:88, 0:88])
                    for w in range(FW):
                        pe.transpose(b4[:, 88 + 44 * w:132 + 44 * w], ffw_rows[:, w, :], ident[0:44, 0:44])
                    for w in range(2):
                        pe.transpose(b4[:, 220 + 44 * w:264 + 44 * w], fst_rows[:, w, :], ident[0:44, 0:44])
                    for k in range(4):
                        pe.transpose(b5[:, 32 * k:32 * k + CW], dww_rows[:, P * k:P * k + P], ident[0:CW, 0:CW])
                        mm = pe.transpose(b5[:, 128 + 32 * k:128 + 32 * k + CW - 1], cst_rows[:, P * k:P * k + P],
                                          ident[0:CW - 1, 0:CW - 1])
                    mm.then_inc(par_ready, 1)

                def qkv_job(t):
                    pe.wait_ge(h_lo_done, 2 * t + 2)
                    for half in range(2):
                        qkv_half(pe, 0, t, half)

                pe.wait_ge(maskf_done, 4)
                for t in range(NT):
                    pe.wait_ge(xn_done, t + 1)
                    if t >= 2:
                        pe.wait_ge(h_lo_done, 2 * (t - 1))
                    for k in range(KT):
                        mm = pe.transpose(XB[2 * (t % 2) + k // 4][:, (k % 4) * P:(k % 4 + 1) * P],
                                          xt[:, t % 3, k * P:(k + 1) * P], ident[:, :])
                    mm.then_inc(xt_ready, 1)
                    if t == 4:
                        parameters()
                    if t >= 2:
                        qkv_job(t - 2)
                qkv_job(NT - 2)
                qkv_job(NT - 1)

        with ExitStack() as c2:
            vnew = sb("vnew", [P, NT, P], c=c2)
            kT = sb("kT", [P, T], c=c2)
            qz = sb("qz", [P, NB, P], c=c2)
            kpast = sb("kpast", [P, 4, 4, P], c=c2)
            kTpast = sb("kTpast", [P, 2, 512], c=c2)
            vpast = sb("vpast", [P, 2, 4, P], c=c2)
            sg = sb("sg", [P, 2, 512], c=c2)
            sn = sb("sn", [P, 2, 513], c=c2)
            run = sb("run", [P, 2, 513], c=c2)
            wT = sb("wT", [P, 2, 512], c=c2)
            o_sb = sb("o_sb", [P, T], c=c2)
            u = sb("u", [P, 2, UCOLS], c=c2)
            c_sb = sb("c_sb", [P, COUT], c=c2)
            sigb = sb("sigb", [P, 364], c=c2)
            bias_b = sb("bias_b", [P, 1], c=c2)
            sdq = sb("sdq", [P, NT * 4], c=c2)
            rsq = sb("rsq", [P, NT * 4], c=c2)

            init_done = sem("init_done")
            kp_in = [sem(f"kp_in{i}") for i in range(4)]
            vp_in = [sem(f"vp_in{i}") for i in range(2)]
            sdq_done, rsq_done, m1_done, norm_done = sem("sdq_done"), sem("rsq_done"), sem("m1_done"), sem("norm_done")
            bias_b_done = sem("bias_b_done")
            u_state, act_ev, q_ev = sem("u_state"), sem("act_ev"), sem("q_ev")
            z_ready, sig_done, scan_done, w_done = sem("z_ready"), sem("sig_done"), sem("scan_done"), sem("w_done")
            av_done, o_ev, tap_done = sem("av_done"), sem("o_ev"), sem("tap_done")

            ZB, WB, OB = bank[2:4], bank[4:6], bank[6:8]
            AB_STEP = {18: 0, 19: 1, 20: 2, 21: 3, 22: 4, 24: 5, 26: 6, 28: 7, 29: 8, 30: 9, 31: 10, 32: 11}
            B_EVAC_STEP, A_EVAC_STEP = {20: 0, 25: 1, 31: 2}, {22: 0, 29: 1, 32: 2}
            NORM_STEP = {21: 0, 23: 1, 25: 2}
            TAP_STEP, _n = {}, 0
            for _s in range(3, 29):
                _k = 2 if _s < 8 else 1
                TAP_STEP[_s] = range(_n, _n + _k)
                _n += _k
            assert _n == CW
            gst2 = stage[:, :, :].rearrange("p t n -> p (t n)")[:, 0:3 * T].rearrange("p (r t) -> p r t", r=3)
            block = c2.enter_context(nc.Block())

            @block.sync
            def _(sp):
                def load_past(p, j, kv):
                    x = j if kv == "k" else j % 2
                    if kv == "k" and later(p):
                        sp.wait_ge(wt_ready, NWT * (p - 1) + WT_JOBS.index(f"past{j}") + 1)
                    elif kv == "v" and j >= 2:
                        sp.wait_ge(av_done, NU * p + PASTS[j % 2] + 1)
                    elif kv == "v" and later(p):
                        sp.wait_ge(av_done, NU * (p - 1) + PASTS[j + 2] + 1)
                    dst, cache, s_in = (kpast, "cache_sb_k", kp_in) if kv == "k" else (vpast, "cache_sb_v", vp_in)
                    src = a[cache][0, 0].rearrange("(b r) h d -> r b (h d)", r=P)
                    sp.dma_start(dst[:, x, :, :], src[:, 4 * (3 - j):4 * (3 - j) + 4, ds(P * p, P)]
                                 ).then_inc(s_in[x], 16)

                def store_kv(p):
                    sp.wait_ge(norm_done, 3 * p + 3)
                    for x, name in ((1, "k"), (2, "v")):
                        dst = o[f"{name}_prompt"][0, 0].rearrange("(t r) h d -> r t (h d)", r=P)
                        sp.dma_start(dst[:, :, ds(P * p, P)], stage[:, 0:NT - 1, P * x:P * x + P]).then_inc(kv_out, 16)
                        dst = o[f"{name}_sample"][0, 0].rearrange("t h d -> t (h d)")
                        sp.dma_start(dst[:, ds(P * p, P)], stage[64:P, NT - 1, P * x:P * x + P]).then_inc(kv_out, 16)

                def store_oc(p):
                    sp.wait_ge(tap_done, CW * p + CW)
                    dst = scr["c"][ds(p, 1)].rearrange("a p t -> (a p) t")
                    sp.dma_start(dst[:, 0:SEQ], c_sb[:, 0:SEQ]).then_inc(spill, 16)
                    sp.dma_start(dst[:, SEQ:T], c_sb[:, U_SAMPLE:COUT]).then_inc(spill, 16)
                    sp.wait_ge(o_ev, 5 * p + 5)
                    sp.dma_start(scr["o"][ds(p, 1)].rearrange("a p t -> (a p) t"), o_sb[:, :]).then_inc(spill, 16)

                def window(p):
                    load_bias(sp, p + 1)
                    for x in range(2):
                        load_ab(sp, x, p + 1)
                    for j in range(4):
                        load_past(p, j, "k")
                    for j in range(2):
                        load_past(p, j, "v")
                    for s in range(3):
                        if p < PAIRS - 2:
                            load_qkv(sp, s, p + 2)
                        else:
                            load_slot(sp, s, 4, gate_col(s))
                    store_kv(p + 1)
                    for j in (2, 3):
                        load_past(p, j, "v")
                    store_oc(p)

                def last_window():
                    for s in (3, 4):
                        load_slot(sp, s, 4, gate_col(s))
                    for j in range(4):
                        load_past(3, j, "k")
                    for j in range(2):
                        load_past(3, j, "v")
                    for g in range(5):
                        load_slot(sp, g, 5, gate_col(5 + g))
                        if g == 4:
                            for j in (2, 3):
                                load_past(3, j, "v")
                        if g == 4:
                            break
                        sp.wait_ge(gate_ev, 3 * g + 3)
                        sp.dma_start(scr["gate"][g], gst2[:, g % 3, :]).then_inc(gate_out2, 16)
                    store_oc(3)

                load_qkv(sp, 2, 1)
                store_kv(0)
                for p in range(PAIRS - 1):
                    window(p)
                last_window()

            @block.gpsimd
            def _(pool):
                pool.memset(qz[:, :, :], 0.0).then_inc(init_done, 1)
                pool.memset(sn[:, :, 512:513], 1.0).then_inc(init_done, 1)
                pool.memset(u[:, :, 0:CW - 1], 0.0).then_inc(init_done, 1)
                for s in range(3):
                    slot_lo(pool, s, 1)
                with pool.Fori(0, 3) as p:
                    for s in (3, 4):
                        slot_lo(pool, s, p + 1)
                    for s in range(3):
                        slot_lo(pool, s, p + 2)
                for s in (3, 4):
                    slot_lo(pool, s, 4)
                for s in range(4):
                    slot_lo(pool, s, 5)

            @block.scalar
            def _(act):
                def b_evac(p, c):
                    c0, c1_ = CHUNKS[c]
                    act.wait_ge(pj_ready, 15 * p + 10 + 2 * c)
                    need = 3 * p + c
                    if later(need):
                        act.wait_ge(a_ev, need)
                    act.wait_ge(bias_b_done, p + 1)
                    act.activation(sigb[:, 0:c1_ - c0], PJ[(9 + 2 * c) % 2][:, 0:c1_ - c0], ACT.Sigmoid,
                                   bias=bias_b[:, :]).then_inc(b_ev, 1)

                def state(p):
                    if later(p, 2):
                        act.wait_ge(tap_done, CW * (p - 1))
                    act.activation(u[:, ds(p % 2, 1), U_SAMPLE:U_SAMPLE + CW - 1].rearrange("p a t -> p (a t)"),
                                   conv_state[:, ds(p, 1), :].rearrange("p a t -> p (a t)"), ACT.Copy
                                                   ).then_inc(u_state, 1)

                def tails(p):
                    act.wait_ge(a_ev, 3 * p + 3)
                    act.wait_ge(u_state, 3 * p + 1)
                    for x, first in enumerate((SEQ, UCOLS - (CW - 1))):
                        act.activation(utail[:, ds(p, 1), (CW - 1) * x:(CW - 1) * (x + 1)].rearrange("p a t -> p (a t)"),
                                       u[:, ds(p % 2, 1), first:first + CW - 1].rearrange("p a t -> p (a t)"),
                                       ACT.Copy).then_inc(u_state, 1)

                def roots(p):
                    act.wait_ge(stat_done, NT * p + NT)
                    act.activation(sdq[:, :], ssq[:, :], ACT.Sqrt, bias=epst[:, 0:1], scale=1.0 / DH
                                    ).then_inc(sdq_done, 1)

                def copy_v(p):
                    act.wait_ge(qkv_ev, NT * p + NT)
                    if later(p):
                        act.wait_ge(av_done, NU * (p - 1) + PASTS[0])
                    act.activation(vnew[:, :, :], stage[:, :, 2 * P:3 * P], ACT.Copy).then_inc(v_copy, 1)

                def k_evac(p, j):
                    act.wait_ge(wt_ready, NWT * p + j + 1)
                    if later(p):
                        act.wait_ge(z_ready, NU * p)
                    t0, b0, n = (512 * j, 0, 512) if j < 2 else (SEQ, P - DEC, DEC)
                    act.activation(kT[:, t0:t0 + n], WB[j % 2][:, b0:b0 + n], ACT.Copy).then_inc(act_ev, 1)

                def sig(p, s):
                    n = UNITS[s][2]
                    act.wait_ge(z_ready, NU * p + s + 1)
                    if s >= 2:
                        act.wait_ge(wt_ready, NWT * p + WT_JOBS.index(f"w{s - 2}") + 1)
                    z = ZB[s % 2][:, 0:n]
                    act.activation(sn[:, s % 2, 512 - n:512], z, ACT.Sigmoid, scale=-DH ** -0.5)
                    act.activation(sg[:, s % 2, 0:n], z, ACT.Sigmoid, scale=DH ** -0.5).then_inc(sig_done, 1)

                def w_evac(p, s):
                    n = UNITS[s][2]
                    act.wait_ge(wt_ready, NWT * p + WT_JOBS.index(f"w{s}") + 1)
                    need = NU * p + s - 1
                    if later(need):
                        act.wait_ge(av_done, need if s >= 1 else NU * p)
                    act.activation(wT[:, s % 2, 0:n], WB[WT_JOBS.index(f"w{s}") % 2][:, 0:n], ACT.Copy
                                    ).then_inc(act_ev, 1)

                def past_evac(p, j):
                    n = WT_JOBS.index(f"past{j}")
                    act.wait_ge(wt_ready, NWT * p + n + 1)
                    if j >= 2:
                        act.wait_ge(z_ready, NU * p + PASTS[j - 2] + 1)
                    act.activation(kTpast[:, j % 2, :], WB[n % 2][:, :], ACT.Copy).then_inc(act_ev, 1)

                def o_evac(p, g):
                    last = max(x for x in range(NU) if UNITS[x][0] // 4 == g)
                    nb = 4 if g < 4 else 1
                    act.wait_ge(av_done, NU * p + last + 1)
                    if g == 0 and later(p):
                        act.wait_ge(spill, 48 * p)
                    for hd in range(2):
                        r = slice(DH * hd, DH * hd + DH)
                        ins = act.activation(o_sb[r, 256 * g:256 * g + QB * nb].rearrange("p (b q) -> p b q", b=nb),
                                             OB[g % 2][r, 0:P * nb].rearrange("p (b q) -> p b q", b=nb)
                                             [:, :, QB * hd:QB * hd + QB], ACT.Copy)
                    ins.then_inc(o_ev, 1)

                def gate_evac(n):
                    g, c = n // 3, n % 3
                    c0, c1_ = CHUNKS[c]
                    act.wait_ge(pj_ready, 15 * PAIRS + n + 1)
                    if n == 0:
                        act.wait_ge(kv_out, 64 * PAIRS)
                        act.wait_ge(v_copy, PAIRS)
                        act.wait_ge(wt_ready, NWT * (PAIRS - 1) + 6)
                    if c == 0 and g >= 3:
                        act.wait_ge(gate_out2, 16 * (g - 2))
                    act.activation(gst2[:, g % 3, c0:c1_], PJ[n % 2][:, 0:c1_ - c0], ACT.Sigmoid,
                                   bias=gate_bias(g)).then_inc(gate_ev, 1)

                def attention(p, s):
                    if s + 1 in PASTS:
                        past_evac(p, PASTS.index(s + 1))
                    if s < NU:
                        sig(p, s)
                    if 0 <= s - 2 < NU:
                        w_evac(p, s - 2)
                    if s >= 4 and UNITS[s - 4][4] and (UNITS[s - 4][0] % 4 == 3 or UNITS[s - 4][0] == NB - 1):
                        o_evac(p, UNITS[s - 4][0] // 4)
                    if s == 1:
                        tails(p)

                def window(p):
                    for s in range(NS):
                        attention(p, s)
                        if s in (1, 3):
                            slot_hi(act, 3 + s // 2, p + 1)
                        if s >= 3 and s % 2 == 1 and (s - 3) // 2 < NT:
                            qkv_stats(act, p + 1, (s - 3) // 2)
                        if s == 20:
                            roots(p + 1)
                        if s in B_EVAC_STEP:
                            b_evac(p + 1, B_EVAC_STEP[s])
                        if s in (21, 22, 23):
                            slot_hi(act, s - 21, p + 2)
                        if s == 26:
                            state(p + 1)
                        if s == 29:
                            copy_v(p + 1)
                        if s == 30:
                            k_evac(p + 1, 0)
                        if s == 31:
                            k_evac(p + 1, 1)
                            k_evac(p + 1, 2)

                def last_window():
                    for s in range(NS):
                        attention(3, s)
                        if s in (1, 3):
                            slot_hi(act, 3 + s // 2, 4)
                        if s >= 5 and s % 2 == 1:
                            gate_evac((s - 5) // 2)
                        if s in (9, 15, 21, 27):
                            slot_hi(act, (s - 9) // 6, 5)
                    gate_evac(14)

                qkv_stats(act, 0, NT - 1)
                roots(0)
                for s in range(2):
                    slot_hi(act, s, 1)
                b_evac(0, 0)
                copy_v(0)
                for j in range(3):
                    k_evac(0, j)
                slot_hi(act, 2, 1)
                b_evac(0, 1)
                state(0)
                b_evac(0, 2)
                act.wait_ge(init_done, 3)
                window(0)
                with act.Fori(1, PAIRS - 1) as p:
                    window(p)
                last_window()

            @block.vector
            def _(dve):
                def next_bias(p):
                    if later(p):
                        dve.wait_ge(b_ev, 3 * p)
                    bias = prm[:, ds(PRM_BIN + 4 + p, 1)]
                    dve.tensor_tensor(bias_b[:, :], bias, bias, ALU.max).then_inc(bias_b_done, 1)

                def a_evac(p, c):
                    c0, c1_ = CHUNKS[c]
                    dve.wait_ge(pj_ready, 15 * p + 11 + 2 * c)
                    dve.wait_ge(b_ev, 3 * p + c + 1)
                    if c == 0 and later(p, 2):
                        dve.wait_ge(u_state, 3 * (p - 1))
                        dve.wait_ge(tap_done, CW * (p - 1))
                    bias = prm[:, ds(PRM_BIN + p, 1)]
                    parts = [(c0, c1_)] if c1_ <= SEQ else [(c0, SEQ), (SEQ, c1_)]
                    for x0, x1 in parts:
                        at = x0 + (CW - 1 if x0 < SEQ else 2 * (CW - 1))
                        ins = dve.scalar_tensor_tensor(
                            out=u[:, ds(p % 2, 1), at:at + x1 - x0].rearrange("p a t -> p (a t)"),
                            in0=PJ[(10 + 2 * c) % 2][:, x0 - c0:x1 - c0], scalar=bias, in1=sigb[:, x0 - c0:x1 - c0],
                            op0=ALU.add, op1=ALU.mult)
                    ins.then_inc(a_ev, 1)

                def tap(p, k):
                    if k == 0:
                        dve.wait_ge(a_ev, 3 * p + 3)
                        dve.wait_ge(u_state, 3 * p + 1)
                        if later(p):
                            dve.wait_ge(spill, 48 * p)
                    x = u[:, ds(p % 2, 1), k:k + COUT].rearrange("p a t -> p (a t)")
                    w = dww[:, ds(p, 1), k:k + 1].rearrange("p a t -> p (a t)")
                    if k == 0:
                        dve.tensor_scalar(c_sb[:, :], x, w, prm[:, ds(PRM_DWB + p, 1)], ALU.mult, ALU.add
                                        ).then_inc(tap_done, 1)
                    else:
                        dve.wait_ge(tap_done, CW * p + k)
                        dve.scalar_tensor_tensor(out=c_sb[:, :], in0=x, scalar=w, in1=c_sb[:, :], op0=ALU.mult,
                                                 op1=ALU.add).then_inc(tap_done, 1)

                def norm(p, third):
                    if third == 0:
                        dve.wait_ge(sdq_done, p + 1)
                        if later(p):
                            dve.wait_ge(m1_done, 3 * p)
                        dve.reciprocal(rsq[:, :], sdq[:, :]).then_inc(rsq_done, 1)
                        dve.wait_ge(rsq_done, p + 1)
                        dve.wait_ge(qkv_ev, NT * p + NT)
                        if isinstance(p, int) and p == 0:
                            dve.wait_ge(g_in2, 64)
                    t0 = 3 * third
                    x = stage[:, t0:t0 + 3, 0:2 * P].rearrange("p t (g d) -> p t g d", d=DH)
                    dve.tensor_tensor(x, x, rsq[:, 4 * t0:4 * t0 + 12].rearrange("p (t g) -> p t g", g=4).unsqueeze(3)
                                      .to_broadcast([P, 3, 4, DH]), ALU.mult).then_inc(m1_done, 1)
                    dve.wait_ge(m1_done, 3 * p + third + 1)
                    y = stage[:, t0:t0 + 3, 0:2 * P]
                    dve.tensor_tensor(y, y, gqk[:, :].unsqueeze(1).to_broadcast([P, 3, 2 * P]), ALU.mult
                                    ).then_inc(norm_done, 1)

                def q_evac(p, j):
                    dve.wait_ge(wt_ready, NWT * p + 4 + j)
                    if later(p):
                        dve.wait_ge(z_ready, NU * p)
                    b = WB[(3 + j) % 2]
                    for hd in range(2):
                        r = slice(DH * hd, DH * hd + DH)
                        if j < 2:
                            out = qz[r, 8 * j:8 * j + 8, QB * hd:QB * hd + QB]
                            src = b[r, :].rearrange("p (b q) -> p b q", b=8)
                        else:
                            out, src = qz[r, NB - 1, QB * hd:QB * hd + QB], b[r, 64:P]
                        ins = dve.tensor_copy(out, src)
                    ins.then_inc(q_ev, 1)

                def weights(p, s):
                    n, first = UNITS[s][2], UNITS[s][3]
                    dve.wait_ge(sig_done, NU * p + s + 1)
                    x = sn[:, s % 2, 512 - n:513][:, ::-1]
                    if s >= 2 or later(p):
                        dve.wait_ge(w_done, NU * p + max(s - 1, 0))
                    init = 1.0 if first else run[:, (s - 1) % 2, 512 - UNITS[s - 1][2]:513 - UNITS[s - 1][2]]
                    dve.tensor_tensor_scan(run[:, s % 2, 512 - n:513][:, ::-1], x, x, init, ALU.mult,
                                           ALU.min).then_inc(scan_done, 1)
                    dve.wait_ge(scan_done, NU * p + s + 1)
                    dve.tensor_tensor(sg[:, s % 2, 0:n], sg[:, s % 2, 0:n], run[:, s % 2, 513 - n:513],
                                      ALU.mult).then_inc(w_done, 1)

                def attention(p, s):
                    if s < NU:
                        weights(p, s)
                    for k in TAP_STEP.get(s, ()):
                        tap(p, k)

                def window(p):
                    for s in range(NS):
                        attention(p, s)
                        if s == 0:
                            next_bias(p + 1)
                        if s >= 2 and s % 2 == 0 and (s - 2) // 2 < NT:
                            qkv_evac(dve, p + 1, (s - 2) // 2)
                        if s in NORM_STEP:
                            norm(p + 1, NORM_STEP[s])
                        if s == 31:
                            q_evac(p + 1, 0)
                        if s == 32:
                            q_evac(p + 1, 1)
                            q_evac(p + 1, 2)
                        if s in A_EVAC_STEP:
                            a_evac(p + 1, A_EVAC_STEP[s])

                next_bias(0)
                for third in range(3):
                    norm(0, third)
                dve.wait_ge(init_done, 3)
                a_evac(0, 0)
                a_evac(0, 1)
                for j in range(3):
                    q_evac(0, j)
                a_evac(0, 2)
                window(0)
                with dve.Fori(1, PAIRS - 1) as p:
                    window(p)
                for s in range(NS):
                    attention(3, s)

            @block.tensor
            def _(pe):
                def free(n, p):
                    if n < 2:
                        if later(p):
                            pe.wait_ge(act_ev, NEV * p)
                        return
                    job = WT_JOBS[n - 2]
                    if job[0] == "q":
                        pe.wait_ge(q_ev, 3 * p + int(job[1:]) + 1)
                    else:
                        pe.wait_ge(act_ev, NEV * p + ACT_EVACS.index(job) + 1)

                def ab_half(p, n, half):
                    if half == 0:
                        if n == 0:
                            pe.wait_ge(lo_done, 5 * p + 5)
                        if n < 2:
                            pe.wait_ge(qkv_ev, NT * p + 8 + n)
                        elif n % 2 == 0:
                            pe.wait_ge(b_ev, 3 * p + n // 2)
                        else:
                            pe.wait_ge(a_ev, 3 * p + n // 2)
                    c0, c1_ = CHUNKS[n // 2]
                    slot = 3 + n % 2
                    for k in range(4 * half, 4 * half + 4):
                        ws = slice(P * k, P * k + P)
                        for i, (w, x) in enumerate(split_passes(whi, wlo, hhi, hlo)):
                            mm = pe.matmul(PJ[(9 + n) % 2][:, 0:c1_ - c0], w[:, slot, ws], x[:, k, c0:c1_],
                                           start=(k == 0 and i == 0), stop=(k == KT - 1 and i == 2))
                    if half:
                        mm.then_inc(pj_ready, 1)

                def qk_transposes(p, n):
                    if n == 0:
                        pe.wait_ge(norm_done, 3 * p + 3)
                    free(n, p)
                    x, j = 1 - n // 3, n % 3
                    tiles = range(4 * j, 4 * j + 4) if j < 2 else [NT - 1]
                    for i, t in enumerate(tiles):
                        mm = pe.transpose(WB[n % 2][:, P * i:P * i + P], stage[:, t, P * x:P * x + P], ident[:, :])
                    mm.then_inc(wt_ready, 1)

                def gate_half(n, half):
                    g, c = n // 3, n % 3
                    c0, c1_ = CHUNKS[c]
                    if half == 0:
                        if c == 0:
                            pe.wait_ge(lo_done, 5 * 4 + g + 1)
                        if n < 2:
                            pe.wait_ge(a_ev, 3 * PAIRS)
                            pe.wait_ge(b_ev, 3 * PAIRS)
                        else:
                            pe.wait_ge(gate_ev, n - 1)
                    for k in range(4 * half, 4 * half + 4):
                        ws = slice(P * k, P * k + P)
                        for i, (w, x) in enumerate(split_passes(whi, wlo, hhi, hlo)):
                            mm = pe.matmul(PJ[n % 2][:, 0:c1_ - c0], w[:, g, ws], x[:, k, c0:c1_],
                                           start=(k == 0 and i == 0), stop=(k == KT - 1 and i == 2))
                    if half:
                        mm.then_inc(pj_ready, 1)

                def past_transposes(p, j):
                    n = WT_JOBS.index(f"past{j}")
                    free(n, p)
                    pe.wait_ge(kp_in[j], 16 * (p + 1))
                    for b in range(4):
                        mm = pe.transpose(WB[n % 2][:, P * b:P * b + P], kpast[:, j, b, :], ident[:, :])
                    mm.then_inc(wt_ready, 1)

                def scores(p, s):
                    i, k0, n, first, last, past, mask = UNITS[s]
                    if s >= 2:
                        pe.wait_ge(sig_done, NU * p + s - 1)
                    elif later(p):
                        pe.wait_ge(sig_done, NU * p)
                    if s == 0:
                        pe.wait_ge(act_ev, NEV * p + 3)
                        pe.wait_ge(q_ev, 3 * p + 3)
                    if past is None:
                        keys = kT[:, k0:k0 + n]
                    else:
                        j = PASTS.index(s)
                        pe.wait_ge(act_ev, NEV * p + ACT_EVACS.index(f"past{j}") + 1)
                        keys = kTpast[:, j % 2, :]
                    mm = pe.matmul(ZB[s % 2][:, 0:n], qz[:, i, :], keys, start=True, stop=True)
                    if mask is not None:
                        mm = pe.matmul(ZB[s % 2][:, n - P:n], identb[:, :], maskb[:, mask, :], start=False, stop=True,
                                       skip_group_check=True)
                    mm.then_inc(z_ready, 1)

                def w_transposes(p, s):
                    n = WT_JOBS.index(f"w{s}")
                    free(n, p)
                    pe.wait_ge(w_done, NU * p + s + 1)
                    for b in range(UNITS[s][2] // P):
                        mm = pe.transpose(WB[n % 2][:, P * b:P * b + P], sg[:, s % 2, P * b:P * b + P], ident[:, :])
                    mm.then_inc(wt_ready, 1)

                def outputs(p, s):
                    i, k0, n, first, last, past, mask = UNITS[s]
                    g = i // 4
                    pe.wait_ge(act_ev, NEV * p + ACT_EVACS.index(f"w{s}") + 1)
                    if s == 0:
                        pe.wait_ge(v_copy, p + 1)
                    if past is not None:
                        j = PASTS.index(s)
                        pe.wait_ge(vp_in[j % 2], 16 * (2 * p + j // 2 + 1))
                    if i % 4 == 0 and first:
                        need = 5 * p + max(g - 1, 0)
                        if later(need):
                            pe.wait_ge(o_ev, need)
                    nb = n // P
                    for b in range(nb):
                        if past is not None:
                            v = vpast[:, PASTS.index(s) % 2, b, :]
                        else:
                            v = vnew[:, k0 // P + b if k0 < T - P else NT - 1, :]
                        mm = pe.matmul(OB[g % 2][:, P * (i % 4):P * (i % 4) + P], v, wT[:, s % 2, P * b:P * b + P],
                                       start=(first and b == 0), stop=(last and b == nb - 1))
                    mm.then_inc(av_done, 1)

                def window(p, last=False):
                    for s in range(NS):
                        if s + 1 in PASTS:
                            past_transposes(p, PASTS.index(s + 1))
                        if s < NU:
                            scores(p, s)
                        if 0 <= s - 2 < NU:
                            w_transposes(p, s - 2)
                        if not last and s in (NS - 3, NS - 2, NS - 1):
                            qk_transposes(p + 1, 2 * (s - NS + 3))
                        if 0 <= s - 3 < NU:
                            outputs(p, s - 3)
                        if last:
                            if s >= 3:
                                gate_half((s - 3) // 2, (s - 3) % 2)
                        elif s < 18:
                            qkv_half(pe, p + 1, s // 2, s % 2)
                        elif s in AB_STEP:
                            ab_half(p + 1, AB_STEP[s] // 2, AB_STEP[s] % 2)
                        if not last and s in (NS - 3, NS - 2, NS - 1):
                            qk_transposes(p + 1, 2 * (s - NS + 3) + 1)

                for n in range(3):
                    for h in range(4):
                        ab_half(0, 2 * n + h // 2, h % 2)
                    if n < 2:
                        for x in range(3):
                            qk_transposes(0, 3 * n + x)
                pe.wait_ge(init_done, 3)
                window(0)
                with pe.Fori(1, PAIRS - 1) as p:
                    window(p)
                window(3, True)

        qctx.close()

        c_bytes = 4 * 4 * T
        top = nc.sbuf_usable_end

        def pinned(name, nth):
            return nc.alloc_sbuf_tensor_at(name, [P, 4, T], F32R, offset=(top - (nth + 1) * c_bytes) // 32 * 32)

        oraw = nc.alloc_sbuf_tensor_at("oraw", [P, 4, T], F32, offset=(top - 3 * c_bytes) // 32 * 32)
        craw = nc.alloc_sbuf_tensor_at("craw", [P, 4, T], F32, offset=(top - 7 * c_bytes // 2) // 32 * 32)
        O_AT = (2, 3, 0, 1)
        gst = nc.alloc_sbuf_tensor_at("gst", [P, 2, T], F32, offset=(top - 4 * c_bytes) // 32 * 32)
        gate_out = [sem("gate_out0"), sem("gate_out1")]
        o_in = [sem(f"o_in{m}") for m in range(4)]

        NG = 2 * KT
        FIRST_FFN = [(0, 0), (1, 1), (2, 2), (3, 3)]
        w_out = a["w_out"][0].rearrange("(k p) n -> p k n", p=P)
        w_up = a["w_up"][0].rearrange("(k p) n -> p k n", p=P)
        w_down = a["w_down"][0].rearrange("(k p) n -> p k n", p=P)
        w_ac = [a["w_attn_out"][0].rearrange("(k p) n -> p k n", p=P), a["w_conv_out"][0].rearrange("(k p) n -> p k n", p=P)]

        def send_raw(sp, sems, n, parity, halves):
            if later(n, 2):
                sp.wait_ge(sems[2], n - 1)
            for h, src in enumerate(halves):
                dst = wraw[:, parity, 512 * h:512 * h + 512]
                if len(src.shape) == 3:
                    dst = dst.rearrange("p (k n) -> p k n", n=P)
                sp.dma_start(dst, src).then_inc(sems[0][parity], 16)

        def k_halves(w, col):
            return [w[:, 0:4, ds(col, P)], w[:, 4:8, ds(col, P)]]

        def send_out_weights(sp, sems, n, parity, k, i):
            if k < 2:
                send_raw(sp, sems, n, parity, [w[:, :, ds(P * (2 * i + k), P)] for w in w_ac])
            else:
                rows = w_out[:, ds(2 * i + k - 2, 1), :].rearrange("p k n -> p (k n)")
                send_raw(sp, sems, n, parity, [rows[:, 0:512], rows[:, 512:D]])

        def send_ffn_weights(sp, sems, n, parity, what, i):
            if what < 4:
                send_raw(sp, sems, n, parity, k_halves(w_up, FF * (what % 2) + P * (2 * i + what // 2)))
            else:
                rows = w_down[:, ds(2 * i + what - 4, 1), :].rearrange("p k n -> p (k n)")
                send_raw(sp, sems, n, parity, [rows[:, 0:512], rows[:, 512:D]])

        def make_hi(act, sems, raw_count, n, parity, dst):
            act.wait_ge(sems[0][parity], 32 * raw_count)
            act.activation(dst, wraw[:, parity, :], ACT.Copy).then_inc(sems[1], 1)

        def make_lo(pool, sems, n, parity, dst, hi):
            pool.wait_ge(sems[1], n + 1)
            pool.tensor_tensor(dst, wraw[:, parity, :], hi.bitcast(F32), ALU.subtract).then_inc(sems[2], 1)

        with ExitStack() as c3:
            chi, clo = pinned("chi", 0), pinned("clo", 1)
            csq = sb("csq", [P, 4, 364], c=c3)
            csig = sb("csig", [P, 4, 364], c=c3)
            crs = sb("crs", [P, T], c=c3)
            ones = sb("ones", [P, P], c=c3)
            raw3 = ([sem("raw3_in0"), sem("raw3_in1")], sem("hi3_done"), sem("lo3_done"))
            tail_ready, tail_done, tail_out = sem("tail_ready"), sem("tail_done"), sem("tail_out")
            ctail = csig[:, :, :].rearrange("p m n -> p (m n)")[0:CW - 1, 0:2 * CC]
            c_in, ones_done, g_ready, g_ev = sem("c_in"), sem("ones_done"), sem("g_ready"), sem("g_ev")
            chalf_done, csum_done, sqhalf_done, sqsum_done = (sem("chalf_done"), sem("csum_done"), sem("sqhalf_done"),
                                                              sem("sqsum_done"))
            mean_ready, xc_done, csq_done, var_ready = sem("mean_ready"), sem("xc_done"), sem("csq_done"), sem("var_ready")
            csd_done, crs_done, cn_done, csig_done = sem("csd_done"), sem("crs_done"), sem("cn_done"), sem("csig_done")
            caff_done, cact_done, chi_done, clo_done = sem("caff_done"), sem("cact_done"), sem("chi_done"), sem("clo_done")
            PREP3 = [(g % 5, 3 * (g - 9)) for g in range(10, NG)] + [(1, 21), (2, 24), (3, 27), (4, 30)]
            block = c3.enter_context(nc.Block())

            @block.sync
            def _(sp):
                sp.wait_ge(gate_ev, 15)
                sp.dma_start(scr["gate"][4], gst2[:, 1, :]).then_inc(gate_out2, 16)
                sp.wait_ge(spill, 48 * PAIRS)
                for m in range(4):
                    sp.dma_start(craw[:, m, :], scr["c"][m]).then_inc(c_in, 16)
                for m in range(2):
                    sp.dma_start(oraw[:, O_AT[m], :], scr["o"][m]).then_inc(o_in[m], 16)
                sp.wait_ge(lo_done, 30)
                n = 0
                for g in range(NG - 5):
                    while n < len(PREP3) and n < g + 3:
                        if n < NG - 10:
                            send_raw(sp, raw3, n, n % 2, k_halves(w_in, gate_col(10 + n)))
                        else:
                            send_out_weights(sp, raw3, n, n % 2, n - (NG - 10), 0)
                        n += 1
                    if g == NG - 6:
                        sp.wait_ge(clo_done, 3)
                        for m in range(2, 4):
                            sp.dma_start(oraw[:, O_AT[m], :], scr["o"][m]).then_inc(o_in[m], 16)
                        break
                    sp.wait_ge(g_ev, 3 * g + 3)
                    sp.dma_start(scr["gate"][g + 5], gst[:, g % 2, :]).then_inc(gate_out[g % 2], 16)
                    if g == 1:
                        sp.wait_ge(tail_done, 2)
                        sp.dma_start(o["conv_prompt"][0, 0], ctail[:, 0:CC]).then_inc(tail_out, 16)
                        sp.dma_start(o["conv_sample"][0, 0], ctail[:, CC:2 * CC]).then_inc(tail_out, 16)
                sp.wait_ge(kv_out, 64 * PAIRS)
                sp.wait_ge(gate_out2, 16 * 5)
                sp.wait_ge(tail_out, 32)

            @block.gpsimd
            def _(pool):
                pool.memset(ones[:, :], 1.0 / CC).then_inc(ones_done, 1)

                def c_lo(c):
                    c0, c1_ = CHUNKS[c]
                    pool.wait_ge(chi_done, c + 1)
                    pool.tensor_tensor(clo[:, :, c0:c1_], craw[:, :, c0:c1_], chi[:, :, c0:c1_].bitcast(F32),
                                       ALU.subtract).then_inc(clo_done, 1)

                slot_lo(pool, 4, 5)
                for n, (slot, _need) in enumerate(PREP3):
                    make_lo(pool, raw3, n, n % 2, wlo[:, slot, :], whi[:, slot, :])
                    if n in (6, 7, 8):
                        c_lo(n - 6)

            @block.scalar
            def _(act):
                def gate_evac(j):
                    g, c = j // 3, j % 3
                    c0, c1_ = CHUNKS[c]
                    act.wait_ge(g_ready, j + 1)
                    if c == 0 and g >= 2:
                        act.wait_ge(gate_out[g % 2], 16 * (g // 2))
                    act.activation(gst[:, g % 2, c0:c1_], bank[j % 4][:, 0:c1_ - c0], ACT.Sigmoid,
                                   bias=gate_bias(g + 5)).then_inc(g_ev, 1)

                def squares(c):
                    c0, c1_ = CHUNKS[c]
                    act.wait_ge(xc_done, c + 1)
                    if c:
                        act.wait_ge(var_ready, c)
                    act.activation(csq[:, :, 0:c1_ - c0], craw[:, :, c0:c1_], ACT.Square).then_inc(csq_done, 1)

                def roots():
                    for c, (c0, c1_) in enumerate(CHUNKS):
                        act.wait_ge(var_ready, c + 1)
                        act.activation(crs[:, c0:c1_], bank[4 + c][:, 0:c1_ - c0], ACT.Sqrt,
                                       bias=epst[:, 0:1]).then_inc(csd_done, 1)

                def sigmoids(c):
                    c0, c1_ = CHUNKS[c]
                    act.wait_ge(cn_done, c + 1)
                    if c == 0:
                        act.wait_ge(tail_out, 32)
                    if c:
                        act.wait_ge(cact_done, c)
                    for m in range(4):
                        ins = act.activation(csig[:, m, 0:c1_ - c0], craw[:, m, c0:c1_], ACT.Sigmoid,
                                             scale=prm[:, PRM_CNG + m:PRM_CNG + m + 1],
                                             bias=prm[:, PRM_CNB + m:PRM_CNB + m + 1])
                    ins.then_inc(csig_done, 1)

                def c_hi(c):
                    c0, c1_ = CHUNKS[c]
                    act.wait_ge(cact_done, c + 1)
                    act.activation(chi[:, :, c0:c1_], craw[:, :, c0:c1_], ACT.Copy).then_inc(chi_done, 1)

                slot_hi(act, 4, 5)
                for j in range(3 * (NG - 5)):
                    gate_evac(j)
                    if j in (2, 4):
                        x = (j - 2) // 2
                        act.wait_ge(tail_ready, x + 1)
                        act.wait_ge(gate_out2, 16 * 5)
                        act.activation(ctail[:, CC * x:CC * x + CC], bank[7][0:CW - 1, :], ACT.Copy
                                        ).then_inc(tail_done, 1)
                    if j in (7, 9, 11):
                        squares((j - 7) // 2)
                    if j == 15:
                        roots()
                    if j in (18, 22, 26):
                        sigmoids((j - 18) // 4)
                    if j in (21, 25, 29):
                        c_hi((j - 21) // 4)
                    if j % 3 == 2 and j // 3 < len(PREP3) - 4:
                        n = j // 3
                        act.wait_ge(g_ready, PREP3[n][1])
                        make_hi(act, raw3, n // 2 + 1, n, n % 2, whi[:, PREP3[n][0], :])
                    if j in (22, 25, 28, 31):
                        n = NG - 10 + (j - 22) // 3
                        act.wait_ge(g_ready, PREP3[n][1])
                        make_hi(act, raw3, n // 2 + 1, n, n % 2, whi[:, PREP3[n][0], :])

            @block.vector
            def _(dve):
                def sum_channels(c, src, out, half_done, done):
                    n = CHUNKS[c][1] - CHUNKS[c][0]
                    dve.tensor_tensor(csq[:, 0:2, 0:n], src[:, 0:2], src[:, 2:4], ALU.add).then_inc(half_done, 1)
                    dve.wait_ge(half_done, c + 1)
                    dve.tensor_tensor(out, csq[:, 0, 0:n], csq[:, 1, 0:n], ALU.add).then_inc(done, 1)

                dve.wait_ge(c_in, 64)
                for c, (c0, c1_) in enumerate(CHUNKS):
                    if c:
                        dve.wait_ge(csum_done, c)
                    sum_channels(c, craw[:, :, c0:c1_], crs[:, c0:c1_], chalf_done, csum_done)
                for c, (c0, c1_) in enumerate(CHUNKS):
                    dve.wait_ge(mean_ready, c + 1)
                    x = craw[:, :, c0:c1_]
                    dve.tensor_tensor(x, x, bank[4 + c][:, 0:c1_ - c0].unsqueeze(1).to_broadcast([P, 4, c1_ - c0]),
                                      ALU.subtract).then_inc(xc_done, 1)
                for c, (c0, c1_) in enumerate(CHUNKS):
                    dve.wait_ge(csq_done, c + 1)
                    sum_channels(c, csq[:, :, 0:c1_ - c0], csq[:, 0, 0:c1_ - c0], sqhalf_done, sqsum_done)
                for c, (c0, c1_) in enumerate(CHUNKS):
                    dve.wait_ge(csd_done, c + 1)
                    dve.reciprocal(crs[:, c0:c1_], crs[:, c0:c1_]).then_inc(crs_done, 1)
                    dve.wait_ge(crs_done, c + 1)
                    x = craw[:, :, c0:c1_]
                    dve.tensor_tensor(x, x, crs[:, c0:c1_].unsqueeze(1).to_broadcast([P, 4, c1_ - c0]),
                                      ALU.mult).then_inc(cn_done, 1)
                for c, (c0, c1_) in enumerate(CHUNKS):
                    dve.wait_ge(csig_done, c + 1)
                    dve.wait_ge(cn_done, c + 1)
                    for m in range(4):
                        ins = dve.tensor_scalar(craw[:, m, c0:c1_], craw[:, m, c0:c1_],
                                                prm[:, PRM_CNG + m:PRM_CNG + m + 1], prm[:, PRM_CNB + m:PRM_CNB + m + 1],
                                                ALU.mult, ALU.add)
                    ins.then_inc(caff_done, 1)
                    dve.wait_ge(caff_done, c + 1)
                    dve.tensor_tensor(craw[:, :, c0:c1_], craw[:, :, c0:c1_], csig[:, :, 0:c1_ - c0],
                                      ALU.mult).then_inc(cact_done, 1)

            @block.tensor
            def _(pe):
                def gate_job(j):
                    g, c = j // 3, j % 3
                    c0, c1_ = CHUNKS[c]
                    if c == 0 and g == 4:
                        pe.wait_ge(lo_done, 30)
                    if c == 0 and g >= 5:
                        pe.wait_ge(raw3[2], g - 4)
                    if j >= 4:
                        pe.wait_ge(g_ev, j - 3)
                    for k in range(KT):
                        ws = slice(P * k, P * k + P)
                        for i, (w, x) in enumerate(split_passes(whi, wlo, hhi, hlo)):
                            mm = pe.matmul(bank[j % 4][:, 0:c1_ - c0], w[:, g % 5, ws], x[:, k, c0:c1_],
                                           start=(k == 0 and i == 0), stop=(k == KT - 1 and i == 2))
                    mm.then_inc(g_ready, 1)

                def channel_mean(c, src, done):
                    pe.wait_ge(done, c + 1)
                    return pe.matmul(bank[4 + c][:, 0:CHUNKS[c][1] - CHUNKS[c][0]], ones[:, :], src, start=True, stop=True)

                for j in range(3 * (NG - 5)):
                    gate_job(j)
                    if j == 4:
                        pe.wait_ge(ones_done, 1)
                        for c, (c0, c1_) in enumerate(CHUNKS):
                            channel_mean(c, crs[:, c0:c1_], csum_done).then_inc(mean_ready, 1)
                    if j in (1, 3):
                        x = (j - 1) // 2
                        if x:
                            pe.wait_ge(tail_done, 1)
                        for m in range(4):
                            mm = pe.transpose(bank[7][0:CW - 1, P * m:P * m + P],
                                              utail[:, m, (CW - 1) * x:(CW - 1) * (x + 1)], ident[:, :])
                        mm.then_inc(tail_ready, 1)
                    if j in (8, 10, 12):
                        c = (j - 8) // 2
                        channel_mean(c, csq[:, 0, 0:CHUNKS[c][1] - CHUNKS[c][0]], sqsum_done).then_inc(var_ready, 1)

        hctx.close()

        x1 = sb("x1", [P, NT, D])
        CH_OF_TOK = [next(c for c in range(3) if CHUNKS[c][1] >= t0 + P) for t0 in TOK]

        def down_job(pe, d, acts, w_slots, i, down_ev, down_ready, lo_sem, lo_need, w_sem, w_need, banks=(4, 5, 6, 7)):
            t, half = d // 2, d % 2
            if d == 0 and later(w_need):
                pe.wait_ge(w_sem, w_need)
            if half == 0:
                pe.wait_ge(lo_sem, lo_need(CH_OF_TOK[t]))
            if d >= len(banks):
                pe.wait_ge(down_ev, 18 * i + d + 1 - len(banks))
            elif later(i):
                pe.wait_ge(down_ev, 18 * i)
            x_hi, x_lo = acts
            for k in range(2):
                w_hi, w_lo = w_slots[k]
                for n, (x, w) in enumerate(split_passes(x_hi, x_lo, w_hi, w_lo)):
                    mm = pe.matmul(bank[banks[d % len(banks)]][:, :], x[:, k, TOK[t]:TOK[t] + P],
                                   w[:, 512 * half:512 * half + 512],
                                   start=(k == 0 and n == 0), stop=(k == 1 and n == 2))
            mm.then_inc(down_ready, 1)

        def down_add(dve, d, i, down_ready, down_ev, banks=(4, 5, 6, 7)):
            t, half = d // 2, d % 2
            dve.wait_ge(down_ready, 18 * i + d + 1)
            if later(i):
                dve.wait_ge(down_ev, 18 * i + d - 17)
            y = x1[:, t, 512 * half:512 * half + 512]
            dve.tensor_tensor(y, bank[banks[d % len(banks)]][:, :], y, ALU.add).then_inc(down_ev, 1)

        w_out_slots = [(whi[:, 3 + k, :], wlo[:, 3 + k, :]) for k in range(2)]
        mhi = sb("mhi", [P, 2, T], F32R)
        mlo = sb("mlo", [P, 2, T], F32R)
        dn4_ready, dn4_ev, m_lo_done = sem("dn4_ready"), sem("dn4_ev"), sem("m_lo_done")
        raw4 = ([sem("raw4_in0"), sem("raw4_in1")], sem("hi4_done"), sem("lo4_done"))
        NI = KT // 2

        with ExitStack() as c4:
            ohi = sb("ohi", [P, 4, T], F32R, c4)
            olo = sb("olo", [P, 4, T], F32R, c4)
            gch = sb("gch", [P, 3, 2, 364], c=c4)
            mixa = sb("mixa", [P, 2, 364], c=c4)
            mixc = sb("mixc", [P, 2, 364], c=c4)
            x1_in, o_hi_done, o_lo_done = sem("x1_in"), sem("o_hi_done"), sem("o_lo_done")
            gch_in = [sem(f"gch_in{c}") for c in range(3)]
            ac_ready, ac_ev, mix_done, m_hi_done = sem("ac_ready"), sem("ac_ev"), sem("mix_done"), sem("m_hi_done")
            block = c4.enter_context(nc.Block())

            @block.sync
            def _(sp):
                def send_gates(i, j, c):
                    c0, c1_ = CHUNKS[c]
                    if j == 1:
                        sp.wait_ge(ac_ev, 12 * i + 2 * c + 2)
                    elif later(i):
                        sp.wait_ge(ac_ev, 12 * i + 2 * c - 4)
                    sp.dma_start(gch[:, c, :, 0:c1_ - c0],
                                 scr["gate"][ds(4 * i + 2 * j, 2)].rearrange("g p t -> p g t")[:, :, c0:c1_]
                                 ).then_inc(gch_in[c], 16)

                def load_x1(part):
                    t0, t1 = 3 * part, min(3 * part + 3, NT - 1)
                    sp.dma_start(x1[:, t0:t1, :], a["x_prompt"][0].rearrange("(t p) n -> p t n", p=P)[:, t0:t1, :]
                                 ).then_inc(x1_in, 16)
                    if part == 2:
                        sp.dma_start(x1[0:64, NT - 1, :], a["x_prompt"][0, SEQ - 64:SEQ, :]).then_inc(x1_in, 16)
                        sp.dma_start(x1[64:P, NT - 1, :], a["x_sample"][0]).then_inc(x1_in, 16)

                def round_(i, last):
                    for j in range(2):
                        for c in range(3):
                            if isinstance(i, int) and i == 0 and j == 1:
                                load_x1(c)
                            send_gates(i, j, c)
                    for k in range(4):
                        n = 4 * i + k
                        if last and k < 2:
                            send_ffn_weights(sp, raw4, n, k % 2, FIRST_FFN[k][1], 0)
                        elif not last:
                            send_out_weights(sp, raw4, n, k % 2, k, i + 1)

                sp.wait_ge(g_ev, 33)
                sp.dma_start(scr["gate"][NG - 1], gst[:, 0, :]).then_inc(gate_out[0], 16)
                sp.wait_ge(gate_out[0], 16 * 6)
                sp.wait_ge(gate_out[1], 16 * 5)
                round_(0, False)
                with sp.Fori(1, NI - 1) as i:
                    round_(i, False)
                round_(NI - 1, True)

            @block.gpsimd
            def _(pool):
                def round_(i, slots):
                    for j in range(2):
                        for c, (c0, c1_) in enumerate(CHUNKS):
                            pool.wait_ge(m_hi_done, 6 * i + 3 * j + c + 1)
                            pool.tensor_tensor(mlo[:, j, c0:c1_], mixa[:, (3 * j + c) % 2, 0:c1_ - c0],
                                               mhi[:, j, c0:c1_].bitcast(F32), ALU.subtract).then_inc(m_lo_done, 1)
                    for k, slot in enumerate(slots):
                        make_lo(pool, raw4, 4 * i + k, k % 2, wlo[:, slot, :], whi[:, slot, :])

                with pool.Fori(0, NI - 1) as i:
                    round_(i, (1, 2, 3, 4))
                round_(NI - 1, ())

            @block.scalar
            def _(act):
                for m in range(4):
                    act.wait_ge(o_in[m], 16)
                for c0, c1_ in CHUNKS:
                    for m in (0, 2):
                        act.activation(ohi[:, m:m + 2, c0:c1_], oraw[:, O_AT[m]:O_AT[m] + 2, c0:c1_],
                                       ACT.Copy).then_inc(o_hi_done, 1)

                def prepare(i, k, slot):
                    if slot in (1, 2):
                        act.wait_ge(ac_ready, 12 * i + 6 * slot)
                    elif slot > 2:
                        act.wait_ge(dn4_ready, 18 * i + 18)
                    make_hi(act, raw4, 2 * i + k // 2 + 1, 4 * i + k, k % 2, whi[:, slot, :])

                def round_(i, slots):
                    for j in range(2):
                        for c, (c0, c1_) in enumerate(CHUNKS):
                            act.wait_ge(mix_done, 6 * i + 3 * j + c + 1)
                            if j == 0 and c == 0 and (later(i)):
                                act.wait_ge(dn4_ready, 18 * i)
                            act.activation(mhi[:, j, c0:c1_], mixa[:, (3 * j + c) % 2, 0:c1_ - c0],
                                           ACT.Copy).then_inc(m_hi_done, 1)
                    for k, slot in enumerate(slots):
                        prepare(i, k, slot)

                round_(0, (1, 2, 3, 4))
                with act.Fori(1, NI - 1) as i:
                    round_(i, (1, 2, 3, 4))
                round_(NI - 1, ())

            @block.vector
            def _(dve):
                def mix(i, j, c):
                    c0, c1_ = CHUNKS[c]
                    n, b, x = c1_ - c0, (3 * j + c) * 2, (3 * j + c) % 2
                    dve.wait_ge(gch_in[c], 16 * (2 * i + j + 1))
                    dve.wait_ge(ac_ready, 12 * i + b + 1)
                    need = 6 * i + 3 * j + c - 1
                    if later(need):
                        dve.wait_ge(m_lo_done, need)
                        dve.wait_ge(mix_done, need + 1)
                    dve.scalar_tensor_tensor(out=mixc[:, x, 0:n], in0=bank[b % 4][:, 0:n],
                                             scalar=prm[:, ds(PRM_BCO + 2 * i + j, 1)], in1=gch[:, c, 1, 0:n],
                                             op0=ALU.add, op1=ALU.mult).then_inc(ac_ev, 1)
                    dve.wait_ge(ac_ready, 12 * i + b + 2)
                    dve.tensor_tensor(mixa[:, x, 0:n], bank[(b + 1) % 4][:, 0:n], gch[:, c, 0, 0:n],
                                      ALU.mult).then_inc(ac_ev, 1)
                    dve.wait_ge(ac_ev, 12 * i + b + 2)
                    dve.tensor_tensor(mixa[:, x, 0:n], mixa[:, x, 0:n], mixc[:, x, 0:n], ALU.add).then_inc(mix_done, 1)

                def round_(i):
                    for j in range(2):
                        for c in range(3):
                            mix(i, j, c)

                def down_adds(i):
                    for d in range(18):
                        down_add(dve, d, i, dn4_ready, dn4_ev)

                for c, (c0, c1_) in enumerate(CHUNKS):
                    for m in (0, 2):
                        dve.wait_ge(o_hi_done, 2 * c + m // 2 + 1)
                        dve.tensor_tensor(olo[:, m:m + 2, c0:c1_], oraw[:, O_AT[m]:O_AT[m] + 2, c0:c1_],
                                          ohi[:, m:m + 2, c0:c1_].bitcast(F32), ALU.subtract).then_inc(o_lo_done, 1)
                round_(0)
                dve.wait_ge(x1_in, 80)
                down_adds(0)
                with dve.Fori(1, NI - 1) as i:
                    round_(i)
                    down_adds(i)
                round_(NI - 1)
                for d in range(4):
                    down_add(dve, d, NI - 1, dn4_ready, dn4_ev)

            @block.tensor
            def _(pe):
                def branch_job(i, b):
                    j, c, attn = b // 6, b // 2 % 3, b % 2
                    c0, c1_ = CHUNKS[c]
                    if c == 0 and attn == 0 and (later(i)):
                        pe.wait_ge(raw4[2], 4 * i - 3 + j)
                    if b >= 4:
                        pe.wait_ge(ac_ev, 12 * i + b - 3)
                    elif later(i):
                        pe.wait_ge(ac_ev, 12 * i)
                    x_hi, x_lo = (ohi, olo) if attn else (chi, clo)
                    for k in range(4):
                        if attn and isinstance(i, int) and i == 0 and j == 0 and k in (0, 2):
                            pe.wait_ge(o_lo_done, 2 * c + k // 2 + 1)
                        ws = slice(P * k + (0 if attn else 512), P * k + (0 if attn else 512) + P)
                        for n, (w, x) in enumerate(split_passes(whi, wlo, x_hi, x_lo)):
                            mm = pe.matmul(bank[b % 4][:, 0:c1_ - c0], w[:, 1 + j, ws], x[:, k, c0:c1_],
                                           start=(k == 0 and n == 0), stop=(k == 3 and n == 2))
                    mm.then_inc(ac_ready, 1)

                def round_(i):
                    for b in range(12):
                        branch_job(i, b)
                    for d in range(18):
                        down_job(pe, d, (mhi, mlo), w_out_slots, i, dn4_ev, dn4_ready, m_lo_done,
                                 lambda c: 6 * i + 4 + c, raw4[2], 4 * i)

                round_(0)
                with pe.Fori(1, NI - 1) as i:
                    round_(i)
                for b in range(12):
                    branch_job(NI - 1, b)
                for d in range(4):
                    down_job(pe, d, (mhi, mlo), w_out_slots, NI - 1, dn4_ev, dn4_ready, m_lo_done,
                             lambda c: 6 * (NI - 1) + 4 + c, raw4[2], 4 * (NI - 1))

        FT = FF // P
        NF = FT // 2
        with ExitStack() as c5:
            h2hi = sb("h2hi", [P, KT, T], F32R, c5)
            h2lo = sb("h2lo", [P, KT, T], F32R, c5)
            w5hi = sb("w5hi", [P, D], F32R, c5)
            w5lo = sb("w5lo", [P, D], F32R, c5)
            gain = sb("gain", [P, D], c=c5)
            ftail = sb("ftail", [P, 4, 2 * FT], c=c5)
            ss5, sd5, rs5 = sb("ss5", [P, 2 * NT], c=c5), sb("sd5", [P, 2 * NT], c=c5), sb("rs5", [P, 2 * NT], c=c5)
            gain_in, ss5_done, sd5_done, rs5_done = sem("gain_in"), sem("ss5_done"), sem("sd5_done"), sem("rs5_done")
            xn5_done, xt5_ready, h2_hi_done, h2_lo_done = sem("xn5_done"), sem("xt5_ready"), sem("h2_hi_done"), sem("h2_lo_done")

            def up_product(pe, tau, c):
                c0, c1_ = CHUNKS[c]
                w_hi, w_lo = whi[:, tau, :], wlo[:, tau, :]
                for k in range(KT):
                    ws = slice(P * k, P * k + P)
                    for n, (w, x) in enumerate(split_passes(w_hi, w_lo, h2hi, h2lo)):
                        mm = pe.matmul(bank[(3 * tau + c) % 4][:, 0:c1_ - c0], w[:, ws], x[:, k, c0:c1_],
                                       start=(k == 0 and n == 0), stop=(k == KT - 1 and n == 2))
                mm.then_inc(up_ready, 1)

            up_ready = sem("up_ready")
            with ExitStack() as c5a:
                xn = sb("xn", [P, 2, D], c=c5a)
                sq5 = sb("sq5", [P, 2, D], c=c5a)
                block = c5a.enter_context(nc.Block())

                LAST = NI - 1
                DB = (6, 7)

                @block.gpsimd
                def _(pool):
                    for k, (slot, _what) in enumerate(FIRST_FFN):
                        make_lo(pool, raw4, 4 * LAST + k, k % 2, wlo[:, slot, :], whi[:, slot, :])

                @block.sync
                def _(sp):
                    sp.dma_start(gain[:, :], a["norm2_g"][0:1, :].to_broadcast([P, D])).then_inc(gain_in, 16)
                    for k in (2, 3):
                        send_ffn_weights(sp, raw4, 4 * LAST + k, k % 2, FIRST_FFN[k][1], 0)
                    sp.wait_ge(gain_in, 16)

                def hi_parts5(act, t):
                    new = 64 if t == NT - 1 else 0
                    for j in range(2):
                        act.wait_ge(xt5_ready, t + 1)
                        act.activation(h2hi[:, 4 * j:4 * j + 4, TOK[t] + new:TOK[t] + P],
                                       XB[2 * (t % 2) + j][:, :].rearrange("p (k t) -> p k t", k=4)[:, :, new:],
                                       ACT.Copy).then_inc(h2_hi_done, 1)

                @block.scalar
                def _(act):
                    def prepare(k):
                        make_hi(act, raw4, 2 * LAST + k // 2 + 1, 4 * LAST + k, k % 2, whi[:, FIRST_FFN[k][0], :])

                    for t in range(NT):
                        if t == NT - 2:
                            act.wait_ge(dn4_ready, 18 * NI)
                            prepare(3)
                        act.wait_ge(dn4_ev, 18 * LAST + 2 * t + 2)
                        if t >= 2:
                            act.wait_ge(ss5_done, t - 1)
                        act.activation(sq5[:, t % 2, :], x1[:, t, :], ACT.Square,
                                       accum_out=ss5[:, t:t + 1]).then_inc(ss5_done, 1)
                        act.wait_ge(ss5_done, t + 1)
                        act.activation(sd5[:, t:t + 1], ss5[:, t:t + 1], ACT.Sqrt, bias=epst[:, 0:1],
                                       scale=1.0 / D).then_inc(sd5_done, 1)
                        if t:
                            hi_parts5(act, t - 1)
                        if t in (1, 3, 5):
                            prepare(t // 2)
                    hi_parts5(act, NT - 1)

                @block.vector
                def _(dve):
                    def lo_parts5(t):
                        new = 64 if t == NT - 1 else 0
                        for j in range(2):
                            dve.wait_ge(h2_hi_done, 2 * t + j + 1)
                            at = slice(TOK[t] + new, TOK[t] + P)
                            dve.tensor_tensor(h2lo[:, 4 * j:4 * j + 4, at],
                                              XB[2 * (t % 2) + j][:, :].rearrange("p (k t) -> p k t", k=4)[:, :, new:],
                                              h2hi[:, 4 * j:4 * j + 4, at].bitcast(F32), ALU.subtract
                                              ).then_inc(h2_lo_done, 1)

                    dve.wait_ge(gain_in, 16)
                    for d in (4, 5):
                        down_add(dve, d, LAST, dn4_ready, dn4_ev, DB)
                    for t in range(NT):
                        dve.wait_ge(sd5_done, t + 1)
                        dve.reciprocal(rs5[:, t:t + 1], sd5[:, t:t + 1]).then_inc(rs5_done, 1)
                        dve.wait_ge(rs5_done, t + 1)
                        if t >= 2:
                            dve.wait_ge(xt5_ready, t - 1)
                        dve.scalar_tensor_tensor(out=xn[:, t % 2, :], in0=x1[:, t, :], scalar=rs5[:, t:t + 1],
                                                 in1=gain[:, :], op0=ALU.mult, op1=ALU.mult).then_inc(xn5_done, 1)
                        for d in range(2 * t + 6, min(2 * t + 8, 18)):
                            down_add(dve, d, LAST, dn4_ready, dn4_ev, DB)
                        if t:
                            lo_parts5(t - 1)
                    lo_parts5(NT - 1)

                @block.tensor
                def _(pe):
                    def down(d):
                        down_job(pe, d, (mhi, mlo), w_out_slots, LAST, dn4_ev, dn4_ready, m_lo_done,
                                 lambda c: 6 * LAST + 4 + c, raw4[2], 4 * LAST, DB)

                    down(4)
                    down(5)
                    for t in range(NT):
                        for d in range(2 * t + 6, min(2 * t + 8, 18)):
                            down(d)
                        if t in (NT - 3, NT - 2):
                            c = t - NT + 3
                            if c == 0:
                                pe.wait_ge(raw4[2], 4 * LAST + 1)
                            pe.wait_ge(h2_lo_done, 2 * (3 * c + 3))
                            up_product(pe, 0, c)
                        pe.wait_ge(xn5_done, t + 1)
                        if t >= 2:
                            pe.wait_ge(h2_lo_done, 2 * (t - 1))
                        for k in range(KT):
                            mm = pe.transpose(XB[2 * (t % 2) + k // 4][:, (k % 4) * P:(k % 4 + 1) * P],
                                              xn[:, t % 2, k * P:(k + 1) * P], ident[:, :])
                        mm.then_inc(xt5_ready, 1)

            with ExitStack() as c5b:
                UPC = 2 + SEQ + 2 + DEC
                NCH = [(0, 364), (364, 728), (728, UPC - 2)]
                ghi, glo = mhi, mlo
                up = sb("up", [P, 2, UPC], c=c5b)
                cvg = sb("cvg", [P, 3, 364], c=c5b)
                cvv = sb("cvv", [P, 2, 364], c=c5b)
                gsig = sb("gsig", [P, 2, 364], c=c5b)
                raw5 = ([sem("raw5_in0"), sem("raw5_in1")], sem("hi5_done"), sem("lo5_done"))
                up_init, up_ev, up_state, up_tail = sem("up_init"), sem("up_ev"), sem("up_state"), sem("up_tail")
                c2_done, c1_done, cv_done = sem("c2_done"), sem("c1_done"), sem("cv_done")
                gsig_done, silu_done, g_done, g_hi_done, g_lo_done = (sem("gsig_done"), sem("silu_done"), sem("g_done"),
                                                                     sem("g_hi_done"), sem("g_lo_done"))
                dn_ready, dn_ev = sem("dn_ready"), sem("dn_ev")
                y_ready, y_out, fgain_in = sem("y_ready"), [sem("y_out0"), sem("y_out1")], sem("fgain_in")
                ft_ready, ft_done, ft_out = sem("ft_ready"), sem("ft_done"), sem("ft_out")
                fss_done, fsd_done, frs_done = sem("fss_done"), sem("fsd_done"), sem("frs_done")
                w_of = [(whi[:, s, :], wlo[:, s, :]) for s in range(5)] + [(w5hi[:, :], w5lo[:, :])]
                PREP5, LAST5 = (0, 4, 5, 1, 2, 3), (4, 5)
                yst = up[:, :, 0:D]
                ysq = cvg[:, :, :].rearrange("p a n -> p (a n)")[:, 0:D]
                frow = cvv[:, :, :].rearrange("p a n -> p (a n)")[0:2 * FT, 0:4 * P].rearrange("p (w c) -> p w c", w=4)

                def pieces(c):
                    c0, c1_ = CHUNKS[c]
                    return [(c0, c1_, 0)] if c1_ <= SEQ else [(c0, SEQ, 0), (SEQ, c1_, 2)]

                def tile_at(tau, i):
                    return FT * (tau % 2) + 2 * i + tau // 2

                def steps(i, last):
                    for tau in (1, 2, 3):
                        for c in range(3):
                            yield i, tau, c
                    if not last:
                        for c in range(3):
                            yield i + 1, 0, c

                block = c5b.enter_context(nc.Block())

                @block.sync
                def _(sp):
                    def round_(i, slots):
                        for k, what in enumerate(slots):
                            send_ffn_weights(sp, raw5, 6 * i + k, k % 2, what, i if what >= 4 else i + 1)

                    sp.dma_start(gain[:, :], a["final_g"].rearrange("(a n) -> a n", a=1).to_broadcast([P, D])
                                 ).then_inc(fgain_in, 16)
                    round_(0, PREP5)
                    with sp.Fori(1, NF - 1) as i:
                        round_(i, PREP5)
                    round_(NF - 1, LAST5)
                    for t in range(NT):
                        sp.wait_ge(y_ready, t + 1)
                        if t < NT - 1:
                            sp.dma_start(o["y_prompt"][0, P * t:P * t + P, :], yst[:, t % 2, :]
                                            ).then_inc(y_out[t % 2], 16)
                        else:
                            sp.dma_start(o["y_sample"][0], yst[64:P, t % 2, :]).then_inc(y_out[t % 2], 16)
                        if t == 3:
                            sp.wait_ge(ft_done, 1)
                            for x, name in enumerate(("ffn_conv_prompt", "ffn_conv_sample")):
                                for r in range(2):
                                    sp.dma_start(o[name][0, 0, r].rearrange("(n c) -> n c", c=P),
                                                 frow[:, 2 * x + r, :]).then_inc(ft_out, 16)
                    sp.wait_ge(ft_out, 64)
                    sp.wait_ge(y_out[0], 16 * ((NT + 1) // 2))
                    sp.wait_ge(y_out[1], 16 * (NT // 2))

                @block.gpsimd
                def _(pool):
                    pool.memset(up[:, :, 0:2], 0.0).then_inc(up_init, 1)

                    def g_lo(i, j, c):
                        pool.wait_ge(g_hi_done, 6 * i + 3 * j + c + 1)
                        for x0, x1_, sh in pieces(c):
                            n0 = sh - NCH[c][0]
                            ins = pool.tensor_tensor(glo[:, j, x0:x1_], cvv[:, (3 * j + c) % 2, x0 + n0:x1_ + n0],
                                                     ghi[:, j, x0:x1_].bitcast(F32), ALU.subtract)
                        ins.then_inc(g_lo_done, 1)

                    def window(i, slots):
                        def prep(k):
                            if k < len(slots):
                                w_hi, w_lo = w_of[slots[k]]
                                make_lo(pool, raw5, 6 * i + k, k % 2, w_lo, w_hi)

                        prep(0)
                        prep(1)
                        g_lo(i, 0, 0)
                        prep(2)
                        g_lo(i, 0, 1)
                        g_lo(i, 0, 2)
                        prep(3)
                        prep(4)
                        for c in range(3):
                            g_lo(i, 1, c)
                        prep(5)

                    with pool.Fori(0, NF - 1) as i:
                        window(i, PREP5)
                    window(NF - 1, LAST5)

                @block.scalar
                def _(act):
                    def copy_up(i, tau, c):
                        c0, c1_ = CHUNKS[c]
                        x = tau % 2
                        act.wait_ge(up_ready, 12 * i + 3 * tau + c + 1)
                        need = 12 * i + 3 * (tau - 2) + min(c + 2, 3)
                        if later(i) or tau >= 2:
                            act.wait_ge(cv_done, need)
                        if c == 2 and (later(i) or tau >= 2):
                            act.wait_ge(up_tail, 8 * i + 2 * tau - 2)
                        for x0, x1_, sh in pieces(c):
                            ins = act.activation(up[:, x, x0 + sh + 2:x1_ + sh + 2],
                                                 bank[(3 * tau + c) % 4][:, x0 - c0:x1_ - c0], ACT.Copy)
                        ins.then_inc(up_ev, 1)
                        if c == 1:
                            act.activation(up[:, x, SEQ + 2:SEQ + 4], ffn_state[:, :, ds(tile_at(tau, i), 1)]
                                           .rearrange("p w a -> p (w a)"), ACT.Copy).then_inc(up_state, 1)
                        if c == 2:
                            act.wait_ge(up_ev, 12 * i + 3 * tau + 3)
                            for y, first in enumerate((SEQ, UPC - 2)):
                                act.activation(ftail[:, 2 * y:2 * y + 2, ds(tile_at(tau, i), 1)].rearrange("p w a -> p (w a)"),
                                               up[:, x, first:first + 2], ACT.Copy).then_inc(up_tail, 1)

                    def gate_sig(i, j, c):
                        n, r = NCH[c][1] - NCH[c][0], 6 * i + 3 * j + c
                        act.wait_ge(cv_done, 12 * i + 6 * j + c + 1)
                        if later(r - 1):
                            act.wait_ge(silu_done, r - 1)
                        act.activation(gsig[:, (3 * j + c) % 2, 0:n], cvg[:, c, 0:n], ACT.Sigmoid
                                        ).then_inc(gsig_done, 1)

                    def g_hi(i, j, c):
                        act.wait_ge(g_done, 6 * i + 3 * j + c + 1)
                        if j == 0 and c == 0 and later(i):
                            act.wait_ge(dn_ready, 18 * i)
                        for x0, x1_, sh in pieces(c):
                            n0 = sh - NCH[c][0]
                            ins = act.activation(ghi[:, j, x0:x1_], cvv[:, (3 * j + c) % 2, x0 + n0:x1_ + n0], ACT.Copy)
                        ins.then_inc(g_hi_done, 1)

                    def gating(i, tau, c):
                        if tau % 2:
                            g_hi(i, tau // 2, c)
                        else:
                            gate_sig(i, tau // 2, c)

                    def prep(i, k, s):
                        if s < 4:
                            act.wait_ge(up_ready, 12 * i + 3 * s + 3)
                        elif later(i):
                            act.wait_ge(dn_ready, 18 * i)
                        make_hi(act, raw5, 3 * i + k // 2 + 1, 6 * i + k, k % 2, w_of[s][0])

                    PREP_AT = {(1, 0): 0, (1, 1): 1, (1, 2): 2, (2, 0): 3, (3, 0): 4, (0, 0): 5}

                    def window(i, slots, last=False):
                        before = (i, 0, 2)
                        for step in steps(i, last):
                            gating(*before)
                            copy_up(*step)
                            before = step
                            k = PREP_AT.get(step[1:], 9)
                            if k < len(slots):
                                prep(i, k, slots[k])
                        if last:
                            gating(*before)

                    act.wait_ge(up_init, 1)
                    for c in range(3):
                        if c:
                            gating(0, 0, c - 1)
                        copy_up(0, 0, c)
                    window(0, PREP5)
                    with act.Fori(1, NF - 1) as i:
                        window(i, PREP5)
                    window(NF - 1, LAST5, True)
                    act.wait_ge(g_done, 6 * NF)
                    for t in range(NT):
                        act.wait_ge(dn_ev, 18 * (NF - 1) + 2 * t + 2)
                        if t:
                            act.wait_ge(fss_done, t)
                        act.activation(ysq, x1[:, t, :], ACT.Square, accum_out=ss5[:, NT + t:NT + t + 1]
                                        ).then_inc(fss_done, 1)
                        act.wait_ge(fss_done, t + 1)
                        act.activation(sd5[:, NT + t:NT + t + 1], ss5[:, NT + t:NT + t + 1], ACT.Sqrt, bias=epst[:, 0:1],
                                       scale=1.0 / D).then_inc(fsd_done, 1)
                        if t == 2:
                            act.wait_ge(ft_ready, 1)
                            act.wait_ge(g_lo_done, 6 * NF)
                            act.activation(frow, bank[0][0:2 * FT, :].rearrange("p (w c) -> p w c", w=4),
                                           ACT.Copy).then_inc(ft_done, 1)

                @block.vector
                def _(dve):
                    def conv(i, tau, c):
                        n0, n1 = NCH[c]
                        n, at, r = n1 - n0, 12 * i + 3 * tau + c, 6 * i + 3 * (tau // 2) + c
                        tile = tile_at(tau, i)
                        dve.wait_ge(up_ev, at + 1)
                        if c == 2:
                            dve.wait_ge(up_state, 4 * i + tau + 1)
                        if tau % 2 == 0:
                            dst = cvg[:, c, 0:n]
                            if later(i) or tau >= 2:
                                dve.wait_ge(g_done, r - 2)
                        else:
                            dst = cvv[:, (3 * (tau // 2) + c) % 2, 0:n]
                            if later(r - 1):
                                dve.wait_ge(g_lo_done, r - 1)

                        def w(k):
                            return ffw[:, k, ds(tile, 1)]

                        src = up[:, tau % 2, :]
                        dve.tensor_scalar(dst, src[:, n0 + 2:n1 + 2], w(2), prm[:, ds(PRM_FDB + tile, 1)],
                                          ALU.mult, ALU.add).then_inc(c2_done, 1)
                        dve.wait_ge(c2_done, at + 1)
                        dve.scalar_tensor_tensor(out=dst, in0=src[:, n0 + 1:n1 + 1], scalar=w(1), in1=dst, op0=ALU.mult,
                                                 op1=ALU.add).then_inc(c1_done, 1)
                        dve.wait_ge(c1_done, at + 1)
                        dve.scalar_tensor_tensor(out=dst, in0=src[:, n0:n1], scalar=w(0), in1=dst, op0=ALU.mult,
                                                 op1=ALU.add).then_inc(cv_done, 1)

                    def silu(i, j, c):
                        n, r = NCH[c][1] - NCH[c][0], 6 * i + 3 * j + c
                        dve.wait_ge(gsig_done, r + 1)
                        dve.wait_ge(cv_done, 12 * i + 6 * j + c + 1)
                        dve.tensor_tensor(cvg[:, c, 0:n], cvg[:, c, 0:n], gsig[:, (3 * j + c) % 2, 0:n],
                                          ALU.mult).then_inc(silu_done, 1)

                    def product(i, j, c):
                        n, r, x = NCH[c][1] - NCH[c][0], 6 * i + 3 * j + c, (3 * j + c) % 2
                        dve.wait_ge(silu_done, r + 1)
                        dve.wait_ge(cv_done, 12 * i + 6 * j + 3 + c + 1)
                        dve.tensor_tensor(cvv[:, x, 0:n], cvv[:, x, 0:n], cvg[:, c, 0:n], ALU.mult).then_inc(g_done, 1)

                    def window(i, last=False):
                        before = (i, 0, 2)
                        for step in steps(i, last):
                            if before[1] % 2 == 0:
                                silu(before[0], before[1] // 2, before[2])
                            conv(*step)
                            if step[1] % 2:
                                product(step[0], step[1] // 2, step[2])
                            before = step

                    def final_norm(t):
                        dve.wait_ge(fsd_done, t + 1)
                        dve.reciprocal(rs5[:, NT + t:NT + t + 1], sd5[:, NT + t:NT + t + 1]).then_inc(frs_done, 1)
                        dve.wait_ge(frs_done, t + 1)
                        dve.wait_ge(dn_ev, 18 * (NF - 1) + 2 * t + 2)
                        if t >= 2:
                            dve.wait_ge(y_out[t % 2], 16 * (t // 2))
                        dve.scalar_tensor_tensor(out=yst[:, t % 2, :], in0=x1[:, t, :], scalar=rs5[:, NT + t:NT + t + 1],
                                                 in1=gain[:, :], op0=ALU.mult, op1=ALU.mult).then_inc(y_ready, 1)

                    for c in range(3):
                        if c:
                            silu(0, 0, c - 1)
                        conv(0, 0, c)
                    window(0)
                    for d in range(18):
                        down_add(dve, d, 0, dn_ready, dn_ev)
                    with dve.Fori(1, NF - 1) as i:
                        window(i)
                        for d in range(18):
                            down_add(dve, d, i, dn_ready, dn_ev)
                    window(NF - 1, True)
                    dve.wait_ge(cv_done, 12 * NF)
                    dve.wait_ge(up_tail, 8 * NF)
                    dve.wait_ge(fgain_in, 16)
                    for d in range(18):
                        down_add(dve, d, NF - 1, dn_ready, dn_ev)
                        if d % 2 and d >= 3:
                            final_norm(d // 2 - 1)
                    final_norm(NT - 1)

                @block.tensor
                def _(pe):
                    def up_job(i, tau, c):
                        c0, c1_ = CHUNKS[c]
                        job = 12 * i + 3 * tau + c
                        if c == 0 and later(i):
                            pe.wait_ge(raw5[2], 6 * (i - 1) + PREP5.index(tau) + 1)
                        if later(job, 4):
                            pe.wait_ge(up_ev, job - 3)
                        up_product(pe, tau, c)

                    def tails():
                        pe.wait_ge(up_ev, 12 * NF)
                        pe.wait_ge(up_tail, 8 * NF)
                        for w in range(4):
                            mm = pe.transpose(bank[0][0:2 * FT, P * w:P * w + P], ftail[:, w, :], ident[:, :])
                        mm.then_inc(ft_ready, 1)

                    def window(i, last=False):
                        for step in steps(i, last):
                            up_job(*step)
                        slots = LAST5 if last else PREP5
                        for d in range(18):
                            down_job(pe, d, (ghi, glo), w_of[4:6], i, dn_ev, dn_ready, g_lo_done, lambda c: 6 * i + 4 + c,
                                     raw5[2], 6 * i + slots.index(5) + 1)
                            if last and d == 3:
                                tails()

                    up_job(0, 0, 2)
                    window(0)
                    with pe.Fori(1, NF - 1) as i:
                        window(i)
                    window(NF - 1, True)


_INS = ["x_prompt", "x_sample", "cache_sb_k", "cache_sb_v", "state_conv", "state_ffn_conv", "norm1_g", "w_in", "b_in",
        "q_norm_g", "k_norm_g", "w_attn_out", "dw_w", "dw_b", "cn_g", "cn_b", "w_conv_out", "b_conv_out", "w_out",
        "norm2_g", "w_up", "ffn_dw_w", "ffn_dw_b", "w_down", "final_g"]
_OUTS = {
    "y_prompt": (1, SEQ, D), "y_sample": (1, DEC, D),
    "k_prompt": (1, 1, SEQ, H, DH), "v_prompt": (1, 1, SEQ, H, DH),
    "k_sample": (1, 1, DEC, H, DH), "v_sample": (1, 1, DEC, H, DH),
    "conv_prompt": (1, 1, CW - 1, CC), "conv_sample": (1, 1, CW - 1, CC),
    "ffn_conv_prompt": (1, 1, FW - 1, 2 * FF), "ffn_conv_sample": (1, 1, FW - 1, 2 * FF),
}
_SCRATCH = {"o": (PAIRS, P, T), "c": (PAIRS, P, T), "gate": (2 * KT, P, T)}


def kernel(**inputs):
    import numpy as _np
    import concourse.bacc as _bacc
    from concourse.bass_utils import run_bass_kernel_spmd as _run

    nc = _bacc.Bacc("TRN2", target_bir_lowering=False, num_devices=1)
    arrays, a = {}, {}
    for name in _INS:
        arrays[f"in_{name}"] = _np.ascontiguousarray(inputs[name])
        a[name] = nc.dram_tensor(f"in_{name}", arrays[f"in_{name}"].shape, F32, kind="ExternalInput").ap()
    o = {n: nc.dram_tensor(f"out_{n}", s, F32, kind="ExternalOutput").ap() for n, s in _OUTS.items()}
    scr = {n: nc.dram_tensor(f"scr_{n}", s, F32, kind="Internal").ap() for n, s in _SCRATCH.items()}
    build(nc, a, o, scr)
    r = _run(nc, [arrays], core_ids=[0])
    return tuple(r.results[0][f"out_{n}"] for n in _OUTS)
```
